# Optimizing a Trainium2 kernel written in Bass

```python
import jax, jax.numpy as jnp
from jax import lax
import numpy as np
import math

D_MODEL = 1024
BATCH = 1
SEQ = 512
DEPTH = 1

MIX_WIDTH = D_MODEL
MLSTM_WIDTH = D_MODEL // 2
MLSTM_HEADS = 4
MLSTM_HEAD_DIM = MLSTM_WIDTH // MLSTM_HEADS
CHUNK = 64
CONV_WIDTH = 4
POOL_WIDTH = MIX_WIDTH - MLSTM_WIDTH
POOL_WINDOWS = (2, 4, 8, 16)
POOL_GROUP = POOL_WIDTH // len(POOL_WINDOWS)
N_IN = 4 * MLSTM_WIDTH + 2 * MLSTM_HEADS + POOL_WIDTH
MEM_LEN = 256
XATTN_HEADS = 4
XATTN_HEAD_DIM = D_MODEL // XATTN_HEADS
N_EXPERTS = 16
N_GROUPS = 4
EXPERTS_PER_GROUP = N_EXPERTS // N_GROUPS
TOP_K = 2
D_EXPERT = D_MODEL // 4
MOE_BLOCK = 128
DEEPNORM_ALPHA = (2 * DEPTH) ** 0.25
DEEPNORM_BETA = (8 * DEPTH) ** -0.25
LN_EPS = 1e-5


def layer_norm(x, g, b):
    xf = x.astype(jnp.float32)
    mu = xf.mean(-1, keepdims=True)
    var = jnp.square(xf - mu).mean(-1, keepdims=True)
    return ((xf - mu) * lax.rsqrt(var + LN_EPS) * g + b).astype(x.dtype)

def causal_depthwise_conv(u, w):
    S = u.shape[1]
    K = w.shape[0]
    up = jnp.pad(u, ((0, 0), (K - 1, 0), (0, 0)))
    return sum(up[:, j:j + S] * w[j] for j in range(K))

def mlstm_chunkwise(q, k, v, i_pre, f_pre):
    B, S, H, dh = q.shape
    L = CHUNK
    NC = S // L

    def chunk(t):
        t = t.reshape((B, NC, L, H) + t.shape[3:])
        return jnp.moveaxis(t, 3, 1)

    q = chunk(q.astype(jnp.float32)) * dh ** -0.5
    k = chunk(k.astype(jnp.float32))
    v = chunk(v.astype(jnp.float32))
    ig = chunk(i_pre.astype(jnp.float32))
    b = jnp.cumsum(jax.nn.log_sigmoid(chunk(f_pre.astype(jnp.float32))), axis=-1)
    b_last = b[..., -1]

    w_state = b_last[..., None] - b + ig
    m_loc = w_state.max(-1)
    a = jnp.exp(w_state - m_loc[..., None])
    C_loc = jnp.einsum('bhcl,bhcld,bhcle->bhcde', a, k, v)
    n_loc = jnp.einsum('bhcl,bhcld->bhcd', a, k)

    def step(carry, inp):
        C, n, m = carry
        Cl, nl, ml, bl = inp
        m_new = jnp.maximum(bl + m, ml)
        s_old = jnp.exp(bl + m - m_new)
        s_new = jnp.exp(ml - m_new)
        C_new = s_old[..., None, None] * C + s_new[..., None, None] * Cl
        n_new = s_old[..., None] * n + s_new[..., None] * nl
        return (C_new, n_new, m_new), (C, n, m)

    init = (jnp.zeros((B, H, dh, dh), jnp.float32),
            jnp.zeros((B, H, dh), jnp.float32),
            jnp.zeros((B, H), jnp.float32))
    xs = tuple(jnp.moveaxis(t, 2, 0) for t in (C_loc, n_loc, m_loc, b_last))
    _, (C_prev, n_prev, m_prev) = lax.scan(step, init, xs)
    C_prev = jnp.moveaxis(C_prev, 0, 2)
    n_prev = jnp.moveaxis(n_prev, 0, 2)
    m_prev = jnp.moveaxis(m_prev, 0, 2)

    causal = jnp.tril(jnp.ones((L, L), dtype=bool))
    log_d = jnp.where(causal, b[..., :, None] - b[..., None, :] + ig[..., None, :], -jnp.inf)
    log_inter = b + m_prev[..., None]
    m_t = jnp.maximum(log_d.max(-1), log_inter)
    p = jnp.exp(log_d - m_t[..., None]) * jnp.einsum('bhcld,bhcsd->bhcls', q, k)
    inter = jnp.exp(log_inter - m_t)
    num = (jnp.einsum('bhcls,bhcse->bhcle', p, v)
           + inter[..., None] * jnp.einsum('bhcld,bhcde->bhcle', q, C_prev))
    den = p.sum(-1) + inter * jnp.einsum('bhcld,bhcd->bhcl', q, n_prev)
    h = num / jnp.maximum(jnp.abs(den), jnp.exp(-m_t))[..., None]
    return jnp.moveaxis(h, 1, 3).reshape(B, S, H, dh)

def multiscale_pool(u):
    S = u.shape[1]
    pos = jnp.arange(1, S + 1, dtype=jnp.float32)[:, None]
    outs = []
    for g, w in enumerate(POOL_WINDOWS):
        ug = u[..., g * POOL_GROUP:(g + 1) * POOL_GROUP].astype(jnp.float32)
        cs = jnp.cumsum(ug, axis=1)
        lagged = jnp.pad(cs, ((0, 0), (w, 0), (0, 0)))[:, :S]
        outs.append((cs - lagged) / jnp.minimum(pos, w) - ug)
    return jnp.stack(outs, axis=2)

def hybrid_mixer(x, w_in, b_i, b_f, conv_qk, head_norm_g, pool_w, pool_scale, w_out):
    B, S, _ = x.shape
    M, H, dh = MLSTM_WIDTH, MLSTM_HEADS, MLSTM_HEAD_DIM
    z = x @ w_in
    qk = jax.nn.silu(causal_depthwise_conv(z[..., :2 * M], conv_qk))
    q = qk[..., :M].reshape(B, S, H, dh)
    k = qk[..., M:].reshape(B, S, H, dh)
    v = z[..., 2 * M:3 * M].reshape(B, S, H, dh)
    o_pre = z[..., 3 * M:4 * M]
    i_pre = z[..., 4 * M:4 * M + H] + b_i
    f_pre = z[..., 4 * M + H:4 * M + 2 * H] + b_f
    u = z[..., 4 * M + 2 * H:]

    h = mlstm_chunkwise(q, k, v, i_pre, f_pre)
    mu = h.mean(-1, keepdims=True)
    var = jnp.square(h - mu).mean(-1, keepdims=True)
    h = (h - mu) * lax.rsqrt(var + LN_EPS) * head_norm_g.reshape(H, dh).astype(jnp.float32)
    h = h.reshape(B, S, M) * jax.nn.sigmoid(o_pre.astype(jnp.float32))

    pooled = multiscale_pool(u)
    pm = jnp.einsum('bsgc,gcd->bsgd', pooled, pool_w.astype(jnp.float32))
    pm = pm.reshape(B, S, POOL_WIDTH) * pool_scale.astype(jnp.float32)

    mixed = jnp.concatenate([h, pm], axis=-1).astype(x.dtype)
    return mixed @ w_out

def memory_cross_attention(x, mem, w_q, w_kv, w_o):
    B, S, D = x.shape
    Mlen = mem.shape[1]
    q = (x @ w_q).reshape(B, S, XATTN_HEADS, XATTN_HEAD_DIM)
    kv = (mem @ w_kv).reshape(B, Mlen, 2, XATTN_HEADS, XATTN_HEAD_DIM)
    s = jnp.einsum('bshd,bmhd->bhsm', q, kv[:, :, 0]).astype(jnp.float32) * XATTN_HEAD_DIM ** -0.5
    p = jax.nn.softmax(s, axis=-1).astype(x.dtype)
    o = jnp.einsum('bhsm,bmhd->bshd', p, kv[:, :, 1]).reshape(B, S, D)
    return o @ w_o

def grouped_moe(x, router_w, router_bias, w_gate, w_up, w_down):
    B, S, D = x.shape
    T = B * S
    A = T * TOP_K
    xt = x.reshape(T, D)
    scores = jax.nn.sigmoid((xt @ router_w).astype(jnp.float32))
    sel = scores + router_bias.astype(jnp.float32)
    grp_score = lax.top_k(sel.reshape(T, N_GROUPS, EXPERTS_PER_GROUP), 2)[0].sum(-1)
    best = jnp.argmax(grp_score, axis=-1)
    in_grp = (jnp.arange(N_EXPERTS) // EXPERTS_PER_GROUP)[None, :] == best[:, None]
    _, idx = lax.top_k(jnp.where(in_grp, sel, -jnp.inf), TOP_K)
    gate = jnp.take_along_axis(scores, idx, axis=-1)
    gate = gate / gate.sum(-1, keepdims=True)

    e = idx.reshape(A).astype(jnp.int32)
    e_sorted, order = lax.sort((e, jnp.arange(A, dtype=jnp.int32)), num_keys=1)
    counts = jnp.bincount(e, length=N_EXPERTS)
    padded = (counts + MOE_BLOCK - 1) // MOE_BLOCK * MOE_BLOCK
    pend = jnp.cumsum(padded)
    pstart = pend - padded
    start = jnp.cumsum(counts) - counts
    dest_sorted = pstart[e_sorted] + jnp.arange(A, dtype=jnp.int32) - start[e_sorted]
    R = A + N_EXPERTS * MOE_BLOCK
    NB = R // MOE_BLOCK
    buf = jnp.zeros((R, D), x.dtype).at[dest_sorted].set(xt[order // TOP_K])
    blk_e = jnp.minimum(jnp.searchsorted(pend, jnp.arange(NB, dtype=jnp.int32) * MOE_BLOCK,
                                         side='right'), N_EXPERTS - 1)

    def expert_block(args):
        xb, ei = args
        hb = jax.nn.silu(xb @ w_gate[ei]) * (xb @ w_up[ei])
        return hb @ w_down[ei]

    yb = lax.map(expert_block, (buf.reshape(NB, MOE_BLOCK, D), blk_e)).reshape(R, D)
    dest = jnp.zeros((A,), jnp.int32).at[order].set(dest_sorted)
    y = (yb[dest].reshape(T, TOP_K, D) * gate[..., None].astype(x.dtype)).sum(1)
    return y.reshape(B, S, D)

def first_inputs(seed: int = 0) -> dict:
    key = jax.random.key(seed)
    ks = jax.random.split(key, 24)
    f32 = jnp.float32
    D, L_ = D_MODEL, DEPTH
    beta = DEEPNORM_BETA
    nrm = lambda k, shape, s: jax.random.normal(k, shape, f32) * s
    col_scale = jnp.asarray(np.concatenate([
        np.ones(2 * MLSTM_WIDTH), np.full(MLSTM_WIDTH, beta), np.ones(MLSTM_WIDTH + 2 * MLSTM_HEADS),
        np.full(POOL_WIDTH, beta)]).astype(np.float32))
    kv_scale = jnp.asarray(np.concatenate([np.ones(D), np.full(D, beta)]).astype(np.float32))
    return {
        "x": nrm(ks[0], (BATCH, SEQ, D), 1.0),
        "mem": nrm(ks[1], (BATCH, MEM_LEN, D), 1.0),
        "w_in": nrm(ks[2], (L_, D, N_IN), D ** -0.5) * col_scale,
        "b_i": nrm(ks[3], (L_, MLSTM_HEADS), 0.1),
        "b_f": jnp.linspace(3.0, 6.0, MLSTM_HEADS, dtype=f32)[None, :] + nrm(ks[4], (L_, MLSTM_HEADS), 0.1),
        "conv_qk": nrm(ks[5], (L_, CONV_WIDTH, 2 * MLSTM_WIDTH), CONV_WIDTH ** -0.5),
        "head_norm_g": 1.0 + nrm(ks[6], (L_, MLSTM_WIDTH), 0.05),
        "pool_w": nrm(ks[7], (L_, len(POOL_WINDOWS), POOL_GROUP, POOL_GROUP), POOL_GROUP ** -0.5),
        "pool_scale": 1.0 + nrm(ks[8], (L_, POOL_WIDTH), 0.1),
        "w_mix_out": nrm(ks[9], (L_, MIX_WIDTH, D), MIX_WIDTH ** -0.5 * beta),
        "ln_mix_g": 1.0 + nrm(ks[10], (L_, D), 0.05),
        "ln_mix_b": nrm(ks[11], (L_, D), 0.02),
        "w_xq": nrm(ks[12], (L_, D, D), D ** -0.5),
        "w_xkv": nrm(ks[13], (L_, D, 2 * D), D ** -0.5) * kv_scale,
        "w_xo": nrm(ks[14], (L_, D, D), D ** -0.5 * beta),
        "ln_x_g": 1.0 + nrm(ks[15], (L_, D), 0.05),
        "ln_x_b": nrm(ks[16], (L_, D), 0.02),
        "router_w": nrm(ks[17], (D, N_EXPERTS), D ** -0.5),
        "router_bias": nrm(ks[18], (N_EXPERTS,), 0.01),
        "w_gate": nrm(ks[19], (L_, N_EXPERTS, D, D_EXPERT), D ** -0.5 * beta),
        "w_up": nrm(ks[20], (L_, N_EXPERTS, D, D_EXPERT), D ** -0.5 * beta),
        "w_down": nrm(ks[21], (L_, N_EXPERTS, D_EXPERT, D), D_EXPERT ** -0.5 * beta),
        "ln_moe_g": 1.0 + nrm(ks[22], (L_, D), 0.05),
        "ln_moe_b": nrm(ks[23], (L_, D), 0.02),
    }

def first_block(x, mem, w_in, b_i, b_f, conv_qk, head_norm_g, pool_w, pool_scale, w_mix_out,
              ln_mix_g, ln_mix_b, w_xq, w_xkv, w_xo, ln_x_g, ln_x_b, router_w, router_bias,
              w_gate, w_up, w_down, ln_moe_g, ln_moe_b):
    for l in range(DEPTH):
        mix = hybrid_mixer(x, w_in[l], b_i[l], b_f[l], conv_qk[l], head_norm_g[l],
                           pool_w[l], pool_scale[l], w_mix_out[l])
        x = layer_norm(DEEPNORM_ALPHA * x + mix, ln_mix_g[l], ln_mix_b[l])
        xa = memory_cross_attention(x, mem, w_xq[l], w_xkv[l], w_xo[l])
        x = layer_norm(DEEPNORM_ALPHA * x + xa, ln_x_g[l], ln_x_b[l])
        ff = grouped_moe(x, router_w, router_bias, w_gate[l], w_up[l], w_down[l])
        x = layer_norm(DEEPNORM_ALPHA * x + ff, ln_moe_g[l], ln_moe_b[l])
    return x


GRID_W = 64
CTX_LEN = 256
N_MIXERS = 3
HY_ORDER = 2
HY_FILTER_WIDTH = 64
HY_EMB_DIM = 33
HY_INNER_MLPS = 2
HY_DECAY_TARGET = 1e-2
HY_SHORT_DECAY_PCT = 0.3
HY_LONG_DECAY_PCT = 1.5
RW_HEAD_DIM = 64
RW_HEADS = D_MODEL // RW_HEAD_DIM
RW_DECAY_LORA = max(32, int(round(1.8 * D_MODEL ** 0.5 / 32)) * 32)
RW_A_LORA = max(32, int(round(1.8 * D_MODEL ** 0.5 / 32)) * 32)
RW_GATE_LORA = max(32, int(round(0.6 * D_MODEL ** 0.8 / 32)) * 32)
RW_GN_EPS = 64e-5
FN_GROUPS = 8
FN_GROUP_DIM = D_MODEL // FN_GROUPS
EC_CAPACITY = 2
D_FF_EXPERT = 2 * D_MODEL
ADALN_EPS = 1e-6
DEEPNORM_ALPHA_2 = (2 * DEPTH) ** 0.25
DEEPNORM_BETA_2 = (8 * DEPTH) ** -0.25


F32 = jnp.float32

def _layer_norm(x, eps):
    xf = x.astype(F32)
    mu = jnp.mean(xf, -1, keepdims=True)
    var = jnp.mean(jnp.square(xf - mu), -1, keepdims=True)
    return (xf - mu) * lax.rsqrt(var + eps)

def _ln_affine(x, g, b):
    return (_layer_norm(x, LN_EPS) * g.astype(F32) + b.astype(F32)).astype(x.dtype)

def _modulate(x, shift, scale):
    return (_layer_norm(x, ADALN_EPS) * (1.0 + scale.astype(F32)) + shift.astype(F32)).astype(x.dtype)

def _grid_pos_embed(rows, dim):
    r_idx = jnp.repeat(jnp.arange(rows, dtype=F32), GRID_W)
    c_idx = jnp.tile(jnp.arange(GRID_W, dtype=F32), rows)
    quarter = dim // 4
    omega = 1.0 / (10000.0 ** (jnp.arange(quarter, dtype=F32) / quarter))
    def emb(p):
        a = p[:, None] * omega[None, :]
        return jnp.concatenate([jnp.sin(a), jnp.cos(a)], -1)
    return jnp.concatenate([emb(r_idx), emb(c_idx)], -1)

def _centred_conv3(u, w, b):
    up = jnp.pad(u, ((0, 0), (1, 1), (0, 0)))
    return up[:, :-2] * w[0] + up[:, 1:-1] * w[1] + up[:, 2:] * w[2] + b

def _hyena_filters(L, f_w1, f_b1, f_freq, f_w2, f_b2, f_w3):
    pos = jnp.arange(L, dtype=F32)
    t01 = pos / max(L - 1, 1)
    bands = (HY_EMB_DIM - 1) // 2
    f = jnp.linspace(1e-4, bands - 1, bands, dtype=F32)
    ang = f[None, :] * (2.0 * math.pi * pos / L)[:, None]
    z = jnp.concatenate([t01[:, None], jnp.cos(ang), -jnp.sin(ang)], -1)
    freq = f_freq.astype(F32)
    a = jnp.sin(freq * (z @ f_w1.astype(F32) + f_b1.astype(F32)))
    for n in range(HY_INNER_MLPS):
        a = jnp.sin(freq * (a @ f_w2[n].astype(F32) + f_b2[n].astype(F32)))
    h = (a @ f_w3.astype(F32)).reshape(L, 2, HY_ORDER, D_MODEL)
    max_decay = math.log(HY_DECAY_TARGET) / HY_SHORT_DECAY_PCT
    min_decay = math.log(HY_DECAY_TARGET) / HY_LONG_DECAY_PCT
    deltas = jnp.linspace(min_decay, max_decay, D_MODEL, dtype=F32)
    window = jnp.exp(-t01[:, None] * jnp.abs(deltas)[None, :])
    h = h * window[:, None, None, :]
    two_sided = jnp.concatenate([h[:, 0], jnp.zeros((1, HY_ORDER, D_MODEL), F32), h[:0:-1, 1]], 0)
    two_sided = two_sided / jnp.sum(jnp.abs(two_sided), 0, keepdims=True)
    return jnp.fft.rfft(two_sided, axis=0)

def _hyena(h, w_in, b_in, conv_w, conv_b, f_w1, f_b1, f_freq, f_w2, f_b2, f_w3, f_bias, w_out, b_out):
    _, L, _ = h.shape
    u = _centred_conv3(h @ w_in + b_in, conv_w, conv_b)
    v, x1, x2 = jnp.split(u, 3, -1)
    kf = _hyena_filters(L, f_w1, f_b1, f_freq, f_w2, f_b2, f_w3)
    def long_conv(zin, o):
        zf = zin.astype(F32)
        y = jnp.fft.irfft(jnp.fft.rfft(zf, n=2 * L, axis=1) * kf[None, :, o], n=2 * L, axis=1)[:, :L]
        return (y + zf * f_bias[o].astype(F32)).astype(h.dtype)
    z = x1 * long_conv(v, 0)
    z = x2 * long_conv(z, 1)
    return z @ w_out + b_out

def _heads(t):
    return t.astype(F32).reshape(t.shape[:-1] + (RW_HEADS, RW_HEAD_DIM))

def _token_shift_bidir(h):
    hp = jnp.pad(h, ((0, 0), (1, 1), (0, 0)))
    return 0.5 * (hp[:, :-2] + hp[:, 2:]) - h

def _rwkv_prep(h, mu, wr, wk, wv, w0, w1, w2, a0, a1, a2, k_k, k_a):
    B_, T, _ = h.shape
    xx = _token_shift_bidir(h)
    xr, xw, xk, xv, xa, xg = [h + xx * mu[n] for n in range(6)]
    k = xk @ wk
    lw = jnp.einsum('nbtr,nrc->nbtc', jnp.tanh(jnp.einsum('btc,ncr->nbtr', xw, w1)), w2).astype(F32) + w0[:, None, None, :].astype(F32)
    decay = jnp.exp(-jnp.exp(-jax.nn.softplus(-lw) - 0.5))
    a = jax.nn.sigmoid(jnp.einsum('nbtr,nrc->nbtc', jnp.einsum('btc,ncr->nbtr', xa, a1), a2).astype(F32) + a0[:, None, None, :].astype(F32))
    kk = (k * k_k).astype(F32).reshape(B_, T, RW_HEADS, RW_HEAD_DIM)
    kk = kk * lax.rsqrt(jnp.maximum(jnp.sum(kk * kk, -1, keepdims=True), 1e-24))
    kk = kk.reshape(B_, T, D_MODEL)
    k_dir = k.astype(F32)[None] * (1.0 + (a - 1.0) * k_a.astype(F32))
    return {"r": (xr @ wr).astype(F32), "v": (xv @ wv).astype(F32), "kk": kk, "decay": decay,
            "k": k_dir, "kka": kk[None] * a, "xg": xg}

def _bidir_seq(tc, tl, directional):
    if directional:
        fc, bc, fl, bl = tc[0], tc[1], tl[0], tl[1]
    else:
        fc, bc, fl, bl = tc, tc, tl, tl
    fwd = jnp.concatenate([fc, fl], 1)
    bwd = jnp.concatenate([jnp.flip(bc, 1), jnp.flip(bl, 1)], 1)
    return jnp.stack([fwd, bwd], 0)

def _wkv_scan(r, decay, k, v, kk, kka):
    def step(S, inp):
        r_t, w_t, k_t, v_t, kk_t, kka_t = inp
        sa = jnp.einsum('dbhvk,dbhk->dbhv', S, kk_t)
        S = S * w_t[..., None, :] - sa[..., :, None] * kka_t[..., None, :] + v_t[..., :, None] * k_t[..., None, :]
        return S, jnp.einsum('dbhvk,dbhk->dbhv', S, r_t)
    S0 = jnp.zeros(r.shape[:2] + (RW_HEADS, RW_HEAD_DIM, RW_HEAD_DIM), F32)
    xs = tuple(jnp.moveaxis(t, 2, 0) for t in (r, decay, k, v, kk, kka))
    _, y = lax.scan(step, S0, xs)
    return jnp.moveaxis(y, 0, 2)

def _rwkv_mixer(hc, hl, prep_params, g1, g2, r_k, gn_g, gn_b, w_o, ctx_out):
    pc = _rwkv_prep(hc, *prep_params)
    pl = _rwkv_prep(hl, *prep_params)
    n_ctx = hc.shape[1]
    def seq(name, directional):
        return _heads(_bidir_seq(pc[name], pl[name], directional))
    y = _wkv_scan(seq("r", False), seq("decay", True), seq("k", True), seq("v", False), seq("kk", False), seq("kka", True))
    def finish(y_dir, p, h):
        wkv = y_dir[0] + jnp.flip(y_dir[1], 1)
        m = jnp.mean(wkv, -1, keepdims=True)
        var = jnp.mean(jnp.square(wkv - m), -1, keepdims=True)
        gn = (wkv - m) * lax.rsqrt(var + RW_GN_EPS) * _heads(gn_g) + _heads(gn_b)
        bonus = jnp.sum(_heads(p["r"])[None] * _heads(p["k"]) * _heads(r_k), axis=(0, -1))[..., None] * _heads(p["v"])
        g = jax.nn.sigmoid(p["xg"] @ g1) @ g2
        o = (gn + bonus).reshape(h.shape).astype(h.dtype) * g
        return o @ w_o
    yl = finish(y[:, :, n_ctx:], pl, hl)
    yc = finish(y[:, :, :n_ctx], pc, hc) if ctx_out else None
    return yc, yl

def _fourier(h, w_o, b_o):
    B_, T, _ = h.shape
    hg = h.astype(F32).reshape(B_, T, FN_GROUPS, FN_GROUP_DIM)
    mixed = jnp.real(jnp.fft.fft2(hg, axes=(1, 3), norm="ortho")).reshape(B_, T, D_MODEL)
    return mixed.astype(h.dtype) @ w_o + b_o

def _expert_choice_moe(h, w_router, w1, w3, w2):
    B_, T, _ = h.shape
    cap = EC_CAPACITY * T // N_EXPERTS
    aff = jax.nn.softmax((h @ w_router).astype(F32), -1)
    gate, idx = lax.top_k(jnp.swapaxes(aff, 1, 2), cap)
    bidx = jnp.arange(B_)[:, None, None]
    xe = h[bidx, idx]
    he = jax.nn.silu(jnp.einsum('becd,edf->becf', xe, w1)) * jnp.einsum('becd,edf->becf', xe, w3)
    ye = jnp.einsum('becf,efd->becd', he, w2) * gate[..., None].astype(h.dtype)
    return jnp.zeros_like(h).at[bidx, idx].add(ye)

def second_inputs(seed: int = 0) -> dict:
    key = jax.random.key(seed)
    keys = iter(jax.random.split(key, 64))
    def nrm(shape, scale):
        return scale * jax.random.normal(next(keys), shape, F32)
    def unif(shape, lo, hi):
        return jax.random.uniform(next(keys), shape, F32, lo, hi)
    D, E, F = D_MODEL, N_EXPERTS, D_FF_EXPERT
    n_a = len(range(0, DEPTH, N_MIXERS))
    n_b = len(range(1, DEPTH, N_MIXERS))
    n_c = len(range(2, DEPTH, N_MIXERS))
    FW = HY_FILTER_WIDTH
    return {
        "x": nrm((BATCH, SEQ, D), 1.0),
        "c": nrm((BATCH, D), 1.0),
        "ctx": nrm((BATCH, CTX_LEN, D), 1.0),
        "c_ctx": nrm((D,), 1.0),
        "mod_w": nrm((DEPTH, D, 6 * D), 0.25 * D ** -0.5),
        "mod_b": nrm((DEPTH, 6 * D), 0.02),
        "ln_g": 1.0 + nrm((DEPTH, 2, D), 0.02),
        "ln_b": nrm((DEPTH, 2, D), 0.02),
        "moe_router": nrm((DEPTH, D, E), D ** -0.5),
        "moe_w1": nrm((DEPTH, E, D, F), D ** -0.5),
        "moe_w3": nrm((DEPTH, E, D, F), D ** -0.5),
        "moe_w2": nrm((DEPTH, E, F, D), DEEPNORM_BETA_2 * F ** -0.5),
        "hy_w_in": nrm((n_a, D, 3 * D), D ** -0.5),
        "hy_b_in": nrm((n_a, 3 * D), 0.02),
        "hy_conv_w": nrm((n_a, 3, 3 * D), 3 ** -0.5),
        "hy_conv_b": nrm((n_a, 3 * D), 0.02),
        "hy_f_w1": nrm((n_a, HY_EMB_DIM, FW), HY_EMB_DIM ** -0.5),
        "hy_f_b1": nrm((n_a, FW), 0.1),
        "hy_f_freq": 1.0 + nrm((n_a, FW), 0.02),
        "hy_f_w2": nrm((n_a, HY_INNER_MLPS, FW, FW), FW ** -0.5),
        "hy_f_b2": nrm((n_a, HY_INNER_MLPS, FW), 0.1),
        "hy_f_w3": nrm((n_a, FW, 2 * HY_ORDER * D), FW ** -0.5),
        "hy_f_bias": nrm((n_a, HY_ORDER, D), 1.0),
        "hy_w_out": nrm((n_a, D, D), DEEPNORM_BETA_2 * D ** -0.5),
        "hy_b_out": nrm((n_a, D), 0.02),
        "rw_mu": unif((n_b, 6, D), 0.0, 1.0),
        "rw_wr": nrm((n_b, D, D), D ** -0.5),
        "rw_wk": nrm((n_b, D, D), D ** -0.5),
        "rw_wv": nrm((n_b, D, D), D ** -0.5),
        "rw_w0": unif((n_b, 2, D), -6.0, 1.0),
        "rw_w1": nrm((n_b, 2, D, RW_DECAY_LORA), D ** -0.5),
        "rw_w2": nrm((n_b, 2, RW_DECAY_LORA, D), 0.1 * RW_DECAY_LORA ** -0.5),
        "rw_a0": nrm((n_b, 2, D), 0.1),
        "rw_a1": nrm((n_b, 2, D, RW_A_LORA), D ** -0.5),
        "rw_a2": nrm((n_b, 2, RW_A_LORA, D), 0.1 * RW_A_LORA ** -0.5),
        "rw_kk": 0.85 + nrm((n_b, D), 0.02),
        "rw_ka": 1.0 + nrm((n_b, D), 0.02),
        "rw_g1": nrm((n_b, D, RW_GATE_LORA), D ** -0.5),
        "rw_g2": nrm((n_b, RW_GATE_LORA, D), RW_GATE_LORA ** -0.5),
        "rw_rk": nrm((n_b, D), 0.1),
        "rw_gn_g": 1.0 + nrm((n_b, D), 0.02),
        "rw_gn_b": nrm((n_b, D), 0.02),
        "rw_wo": nrm((n_b, D, D), DEEPNORM_BETA_2 * D ** -0.5),
        "fn_wo": nrm((n_c, D, D), DEEPNORM_BETA_2 * D ** -0.5),
        "fn_bo": nrm((n_c, D), 0.02),
    }

def second_block(x, c, ctx, c_ctx, mod_w, mod_b, ln_g, ln_b, moe_router, moe_w1, moe_w3, moe_w2,
              hy_w_in, hy_b_in, hy_conv_w, hy_conv_b, hy_f_w1, hy_f_b1, hy_f_freq, hy_f_w2, hy_f_b2, hy_f_w3,
              hy_f_bias, hy_w_out, hy_b_out,
              rw_mu, rw_wr, rw_wk, rw_wv, rw_w0, rw_w1, rw_w2, rw_a0, rw_a1, rw_a2, rw_kk, rw_ka,
              rw_g1, rw_g2, rw_rk, rw_gn_g, rw_gn_b, rw_wo,
              fn_wo, fn_bo):
    n_lat = x.shape[1]
    rows = n_lat // GRID_W
    x = x + _grid_pos_embed(rows, D_MODEL).astype(x.dtype)[None]
    xc = ctx
    readers = [i for i in range(DEPTH) if i % N_MIXERS == 1]
    last_reader = readers[-1] if readers else -1
    for i in range(DEPTH):
        kind, j = i % N_MIXERS, i // N_MIXERS
        ctx_in = i <= last_reader
        ctx_full = i < last_reader
        m_l = jnp.split((jax.nn.silu(c) @ mod_w[i] + mod_b[i])[:, None, :], 6, -1)
        hl = _modulate(x, m_l[0], m_l[1])
        if ctx_in:
            m_c = jnp.split((jax.nn.silu(c_ctx) @ mod_w[i] + mod_b[i])[None, None, :], 6, -1)
            hc = _modulate(xc, m_c[0], m_c[1])
        if kind == 0:
            hy = (hy_w_in[j], hy_b_in[j], hy_conv_w[j], hy_conv_b[j], hy_f_w1[j], hy_f_b1[j], hy_f_freq[j],
                  hy_f_w2[j], hy_f_b2[j], hy_f_w3[j], hy_f_bias[j], hy_w_out[j], hy_b_out[j])
            yl = _hyena(hl, *hy)
            yc = _hyena(hc, *hy) if ctx_full else None
        elif kind == 1:
            prep = (rw_mu[j], rw_wr[j], rw_wk[j], rw_wv[j], rw_w0[j], rw_w1[j], rw_w2[j],
                    rw_a0[j], rw_a1[j], rw_a2[j], rw_kk[j], rw_ka[j])
            yc, yl = _rwkv_mixer(hc, hl, prep, rw_g1[j], rw_g2[j], rw_rk[j], rw_gn_g[j], rw_gn_b[j], rw_wo[j], ctx_full)
        else:
            yl = _fourier(hl, fn_wo[j], fn_bo[j])
            yc = _fourier(hc, fn_wo[j], fn_bo[j]) if ctx_full else None
        x = _ln_affine(DEEPNORM_ALPHA_2 * x + (1.0 + m_l[2]) * yl, ln_g[i, 0], ln_b[i, 0])
        hl = _modulate(x, m_l[3], m_l[4])
        x = _ln_affine(DEEPNORM_ALPHA_2 * x + (1.0 + m_l[5]) * _expert_choice_moe(hl, moe_router[i], moe_w1[i], moe_w3[i], moe_w2[i]),
                       ln_g[i, 1], ln_b[i, 1])
        if ctx_full:
            xc = _ln_affine(DEEPNORM_ALPHA_2 * xc + (1.0 + m_c[2]) * yc, ln_g[i, 0], ln_b[i, 0])
            hc = _modulate(xc, m_c[3], m_c[4])
            xc = _ln_affine(DEEPNORM_ALPHA_2 * xc + (1.0 + m_c[5]) * _expert_choice_moe(hc, moe_router[i], moe_w1[i], moe_w3[i], moe_w2[i]),
                            ln_g[i, 1], ln_b[i, 1])
    return x


def setup_inputs(seed=0):
    out = dict(first_inputs(seed))
    for name, value in second_inputs(seed + 1).items():
        if name != "x":
            out[name + "_2"] = value
    return out


def reference(
    x, mem, w_in, b_i, b_f, conv_qk, head_norm_g, pool_w, pool_scale, w_mix_out, ln_mix_g,
    ln_mix_b, w_xq, w_xkv, w_xo, ln_x_g, ln_x_b, router_w, router_bias, w_gate, w_up, w_down,
    ln_moe_g, ln_moe_b, c_2, ctx_2, c_ctx_2, mod_w_2, mod_b_2, ln_g_2, ln_b_2, moe_router_2,
    moe_w1_2, moe_w3_2, moe_w2_2, hy_w_in_2, hy_b_in_2, hy_conv_w_2, hy_conv_b_2, hy_f_w1_2,
    hy_f_b1_2, hy_f_freq_2, hy_f_w2_2, hy_f_b2_2, hy_f_w3_2, hy_f_bias_2, hy_w_out_2,
    hy_b_out_2, rw_mu_2, rw_wr_2, rw_wk_2, rw_wv_2, rw_w0_2, rw_w1_2, rw_w2_2, rw_a0_2, rw_a1_2,
    rw_a2_2, rw_kk_2, rw_ka_2, rw_g1_2, rw_g2_2, rw_rk_2, rw_gn_g_2, rw_gn_b_2, rw_wo_2,
    fn_wo_2, fn_bo_2,
):
    x = first_block(
        x, mem, w_in, b_i, b_f, conv_qk, head_norm_g, pool_w, pool_scale, w_mix_out, ln_mix_g,
        ln_mix_b, w_xq, w_xkv, w_xo, ln_x_g, ln_x_b, router_w, router_bias, w_gate, w_up,
        w_down, ln_moe_g, ln_moe_b,
    )
    return second_block(
        x, c_2, ctx_2, c_ctx_2, mod_w_2, mod_b_2, ln_g_2, ln_b_2, moe_router_2, moe_w1_2,
        moe_w3_2, moe_w2_2, hy_w_in_2, hy_b_in_2, hy_conv_w_2, hy_conv_b_2, hy_f_w1_2,
        hy_f_b1_2, hy_f_freq_2, hy_f_w2_2, hy_f_b2_2, hy_f_w3_2, hy_f_bias_2, hy_w_out_2,
        hy_b_out_2, rw_mu_2, rw_wr_2, rw_wk_2, rw_wv_2, rw_w0_2, rw_w1_2, rw_w2_2, rw_a0_2,
        rw_a1_2, rw_a2_2, rw_kk_2, rw_ka_2, rw_g1_2, rw_g2_2, rw_rk_2, rw_gn_g_2, rw_gn_b_2,
        rw_wo_2, fn_wo_2, fn_bo_2,
    )


_drawn_inputs = setup_inputs


def setup_inputs(seed=0):
    import zlib

    import numpy as np

    out = dict(_drawn_inputs(seed))
    spreads = {}
    factors = {'b_i': 64.0,
     'head_norm_g': 4.231,
     'router_bias': 2.877,
     'ln_moe_b': 2.857,
     'hy_b_in_2': 3.639,
     'hy_conv_b_2': 3.456,
     'hy_f_b1_2': 2.795,
     'hy_f_freq_2': 8.0,
     'hy_b_out_2': 3.732,
     'pool_scale': 3.311}
    for name, (base, spread) in spreads.items():
        noise = np.random.default_rng([zlib.crc32(name.encode()), seed]).standard_normal(out[name].shape)
        drawn = base * np.exp(spread * noise) if base else spread * noise
        out[name] = __import__('jax').numpy.asarray(drawn.astype(out[name].dtype))
    for name, factor in factors.items():
        out[name] = (out[name] * factor).astype(out[name].dtype)
    return out
```

```python
from contextlib import ExitStack

import concourse.bass as bass
from concourse import mybir

P = 128
D = 1024
KD = D // P
S = 512
ST = S // P
MEM = 256
HEADS = 4
DH = 128
XDH = 256
NE = 16
NGRP = 4
FE = 256
FF = 2048
CAP = 64
POOLW = (2, 4, 8, 16)
HW = 64
EMB = 33
UNIT = 2048
COLS = UNIT // KD
RING = 12
ALPHA = 2.0 ** 0.25
LN_EPS = 1e-5
MOD_EPS = 1e-6
NEG = -1.0e30

F32 = mybir.dt.float32
ALU = mybir.AluOpType
ACT = mybir.ActivationFunctionType
AX = mybir.AxisListType.X

STREAM = [("mod", 24), ("in", 10), ("mix", 4), ("xkv", 8), ("xq", 4), ("xo", 4), ("moe1", 3 * NE),
          ("hyin", 12), ("hyout", 4)]
BASE = {}
_n = 0
for _name, _units in STREAM:
    BASE[_name] = _n
    _n += _units
UNITS = _n

VECS = [("conv", 32), ("head_g", 4), ("pool_scale", 4), ("ln_mix_g", 8), ("ln_mix_b", 8), ("ln_x_g", 8),
        ("ln_x_b", 8), ("ln_moe_g", 8), ("ln_moe_b", 8), ("mod_b", 48), ("ln_g2", 16), ("ln_b2", 16),
        ("hy_b_in", 24), ("hy_conv_w", 72), ("hy_conv_b", 24), ("hy_f_bias", 16), ("hy_b_out", 8), ("c", 8)]
VAT = {}
_n = 0
for _name, _units in VECS:
    VAT[_name] = _n
    _n += _units
NVEC = _n

TWO_PI = 6.283185307179586
PI_HI = 6.28125
PI_LO = TWO_PI - PI_HI
ROUND = 12582912.0
PI_IN = 3.1415925


class Count:

    def __init__(self, sem):
        self.sem, self.n, self.i, self.per, self.first = sem, 0, None, 0, 0

    def at(self, more=0):
        v = self.n + more
        return v if self.i is None else v + self.i * self.per

    def inc(self, ins, by=1):
        ins.then_inc(self.sem, by)
        self.n += by

    def enter(self, i, per):
        self.i, self.per, self.first = i, per, self.n

    def leave(self, rounds):
        assert self.n - self.first == self.per, (self.n - self.first, self.per)
        self.n, self.i = self.first + self.per * rounds, None


class Banks:

    def __init__(self, psum, banks, filled, emptied):
        self.psum, self.banks = psum, banks
        self.filled, self.emptied = Count(filled), Count(emptied)

    def bank(self, more=0):
        return self.psum[:, self.banks[(self.filled.n + more) % len(self.banks)], :]


def build(nc, ins, out):
    with ExitStack() as ctx:
        def sb(name, shape):
            return ctx.enter_context(nc.sbuf_tensor(name, shape, F32))

        def sem(name):
            return ctx.enter_context(nc.semaphore(name))

        ring = sb("ring", [P, RING, UNIT])
        arena = sb("arena", [P, 6, KD * S])
        psum = ctx.enter_context(nc.psum_tensor("psum", [P, 8, 512], F32))

        ones = sb("ones", [P, P])
        mean_w = sb("mean_w", [P, P])
        ident = sb("ident", [P, P])
        iota = sb("iota", [P, CAP])
        vec = sb("vec", [P, NVEC])
        fvec = sb("fvec", [HW, 4])
        fw1 = sb("fw1", [EMB, HW])
        fw2 = sb("fw2", [HW, 2, HW])
        gbias = sb("gbias", [HEADS, 2])
        wgate = sb("wgate", [P, KD, 8])
        pool16 = sb("pool16", [P, 4, 16])
        router = sb("router", [P, 2, KD, NE])
        rbias = sb("rbias", [P, NE])
        lower = sb("lower", [P, NE, NE])
        csil = sb("csil", [P, KD, 32])
        modc = sb("modc", [P, 48])
        modp = sb("modp", [P, 48])
        modg = sb("modg", [P, 8])
        filt_rn = sb("filt_rn", [P, 16])
        acol = sb("acol", [P, ST, HEADS])
        tiny = sb("tiny", [P, 4, 8])
        route = sb("route", [P, 6, ST * NE])
        gates = sb("gates", [P, ST, NE])
        slot = sb("slot", [P, ST, NE + 2])
        aff = sb("aff", [P, ST, NE + 2])
        epsv = sb("epsv", [P, 1])

        def vcol(name, j):
            return vec[:, VAT[name] + j:VAT[name] + j + 1]

        def region(r, at=0, tiles=KD, width=S):
            return arena[:, r, at:at + tiles * width].rearrange("p (k n) -> p k n", k=tiles)

        dft_f = region(0).rearrange("p (a k) n -> p a k n", a=2)
        h_fwd, h_bwd = region(1, 0, ST), region(1, 2048, ST)
        h_even, h_odd = region(2, 0, ST), region(2, 2048, ST)
        k_out = region(3)
        abs_sum = region(4, 0, ST)
        mlp = region(4, 2048, 4)
        abs_tmp = region(4, 3072, 1)[:, 0, :]
        fw3 = arena[0:HW, 5, :]
        mod_row = region(1, 0, 2, 256)
        x = region(0)
        qk = region(1)
        conv = region(2)
        v_tok, o_gate = region(3, 0, ST), region(3, 2048, ST)
        u_pad = arena[:, 4, 0:528]
        pool_a = arena[:, 4, 528:1056]
        pool_b = arena[:, 4, 1056:1584]
        rows = [arena[0:HEADS, 4, 1584 + 512 * n:2096 + 512 * n] for n in range(4)]
        mixed = region(5)
        decay = region(2, 0, ST)
        hn = region(2, 2048, 4)
        mem_t, k_x = region(3, 0, KD, MEM), region(3, 2048, KD, MEM)
        v_x = region(4, 0, 2, D)
        p_exp = region(4, 2048, 4, MEM)
        p_t = region(4, 3072, 2)
        q_x, o_x = region(5), region(1)
        gate_bc = arena[:, 1:3, :].rearrange("p a (e n) -> p (a e) n", n=S)
        y1 = region(3)
        hid = region(4)
        silu1 = region(5, 0, 2)
        gate_t = arena[0:NE, 5, 1024:1536]
        pos = region(5)
        h2 = region(4)
        u_hy = [region(1), region(2), region(3)]
        z_tok = region(4, 0, ST, D)
        spec = region(5)
        h_tok = region(5, 0, ST, D)
        y2 = region(1)
        x_sel = region(2, 0, 1, D)
        x_sel_t = region(2, 1024, KD, P)
        y_sel = region(2, 2048, 1, D)
        onehot = region(2, 3072, ST, P)
        onehot_g = region(2, 3584, ST, P)
        hid2, silu2 = region(3, 0, 1, FF), region(3, 2048, 1, FF)
        hid2_t = region(4, 0, FF // P, P)
        scat = arena[:, 4, 2048:2560]
        aff_t = arena[0:NE, 4, 2560:3072]
        work_t = arena[0:NE, 4, 3072:3584]
        mask_t = arena[0:NE, 4, 3584:4096]
        hpad = arena[:, 5, 0:2 * (S + 2)].rearrange("p (b n) -> p b n", b=2)
        scratch = sb("scratch", [P, 2, S])
        last_row = scratch[:, 0, :].rearrange("p (k n) -> p k n", k=ST)
        poolw = scratch[:, 1, :].rearrange("p (k n) -> p k n", k=4)
        ln_r = ptmp = scratch
        top8 = sb("top8", [NE, 8])

        s_arrived = [sem(f"arrived{r}") for r in range(RING)]
        s_used = sem("units_used")
        s_ma, s_ea = sem("act_filled"), sem("act_emptied")
        s_md, s_ed = sem("dve_filled"), sem("dve_emptied")
        s_const = sem("pool_consts")
        s_vec = sem("vectors_in")
        s_cf = sem("dft_in")
        s_step = sem("dve_step")
        s_astep = sem("act_step")
        s_mlp = sem("mlp_arg")
        s_sin = sem("mlp_sine")
        s_hw = sem("taps_windowed")
        s_eo = sem("taps_even_odd")
        s_kst = sem("filter_stored")
        s_kout = sem("filter_copied")
        s_abs = sem("taps_abs_sum")
        s_csil = sem("c_silu")
        s_mrow = sem("mod_row_read")
        s_x = sem("x_in")
        s_free = sem("stage_end")
        s_gb = sem("gate_rows")
        s_gl = sem("gate_ln")
        s_conv = sem("conv_done")
        s_qk = sem("qk_ready")
        s_upad = sem("pool_input")
        s_pool = sem("pool_done")
        s_row = sem("rows_ready")
        s_exp = sem("decay_exp")
        s_tri = sem("decay_masked")
        s_rv = sem("inverse_var")
        s_rstd = sem("rstd")
        s_hn = sem("head_square")
        s_ho = sem("head_out")
        s_den = sem("den_abs")
        s_res = sem("residual_sum")
        s_lnc = sem("ln_centred")
        s_lnq = sem("ln_square")
        s_lnm = sem("ln_scaled")
        s_lno = sem("ln_out")
        s_mem = sem("mem_in")
        s_xs = sem("scores_shifted")
        s_xe = sem("scores_exp")
        s_xp = sem("probs_ready")
        s_pread = sem("probs_read")
        s_em = sem("den_floor")
        s_ohg = sem("gated_onehots")
        s_aff = sem("affinities")
        s_r0 = sem("logits_shifted")
        s_r1 = sem("logits_exp")
        s_gt = sem("gates_ready")
        s_gbc = sem("gates_spread")
        s_si1 = sem("silu1")
        s_hid = sem("hidden1")
        s_pos = sem("pos_in")
        s_px = sem("pos_added")
        s_hz = sem("hy_pad_zero")
        s_uc = sem("hy_conv")
        s_zt = sem("z_tok_ready")
        s_k = sem("spectrum_product")
        s_z1 = sem("z_next")
        s_ys = sem("hy_out_scaled")
        s_top = sem("top_ready")
        s_oh = sem("onehots")
        s_si2 = sem("silu2")
        s_hid2 = sem("hidden2")
        s_y0 = sem("y2_zero")
        s_g2 = sem("moe2_groups_a")
        s_out = sem("out_stored")

        note = {}

        block = ctx.enter_context(nc.Block())

        @block.sync
        def _(sp):
            used = Count(s_used)
            turn = [0]

            def load(src, dst_shape=None):
                slot_ = turn[0] % RING
                if used.i is not None or turn[0] >= RING:
                    sp.wait_ge(s_used, used.at(1 - RING))
                dst = ring[:, slot_, :]
                if dst_shape is not None:
                    dst = dst_shape(dst)
                sp.dma_start(dst, src).then_inc(s_arrived[slot_], 16)
                used.n += 1
                turn[0] += 1

            small = [(vec[:], ins["vecs"]), (fvec[:], ins["fvecs"]), (fw1[:], ins["fw1"]), (fw2[:], ins["fw2"]),
                     (mlp[0:EMB, 3, :], ins["zfeat"]), (gbias[:], ins["gbias"]), (wgate[:], ins["wgate"]),
                     (poolw, ins["poolw"]), (pool16[:], ins["pool16"]), (last_row, ins["last_row"]),
                     (router[:], ins["router"]), (rbias[:], ins["rbias"].broadcast_to([P, NE])),
                     (lower[:], ins["lower"].broadcast_to([P, NE, NE])), (fw3, ins["fw3"])]
            for dst, src in small:
                sp.dma_start(dst, src).then_inc(s_vec, 16)
            sp.dma_start(dft_f, ins["dft"][0:2].rearrange("a p (k n) -> p a k n", k=ST)).then_inc(s_cf, 16)
            for half in range(2):
                load(ins["window"][half])
            for u in range(24):
                load(ins["stream"][BASE["mod"] + u])
            sp.wait_ge(s_free, 1)
            sp.dma_start(x, ins["x"]).then_inc(s_x, 16)
            for u in range(14):
                load(ins["stream"][BASE["in"] + u])
            sp.wait_ge(s_ho, HEADS)
            sp.dma_start(mem_t, ins["mem"]).then_inc(s_mem, 16)
            for u in range(16):
                load(ins["stream"][BASE["xkv"] + u])
            with sp.Fori(0, 3 * NE // RING) as i:
                used.enter(i, RING)
                for j in range(RING):
                    load(ins["stream"][BASE["moe1"] + RING * i + j])
                used.leave(3 * NE // RING)
            turn[0] += 3 * NE - RING
            for u in range(12):
                load(ins["stream"][BASE["hyin"] + u])
            sp.wait_ge(s_lnc, 2 * KD + 1)
            sp.dma_start(pos, ins["pos"]).then_inc(s_pos, 16)
            for order in range(2):
                for half in range(2):
                    load(ins["dft"][0])
                    load(ins["dft"][1])
                    if order == 0 and half == 0:
                        sp.wait_ge(s_kst, 16 * 4)
                    c = 2 * half + order
                    load(ins["spectra"][c, :, 0:4, :], lambda d: d.rearrange("p (k n) -> p k n", k=4))
                    load(ins["spectra"][c, :, 4:8, :], lambda d: d.rearrange("p (k n) -> p k n", k=4))
                    load(ins["dft"][2])
                    load(ins["dft"][3])
            for u in range(4):
                load(ins["stream"][BASE["hyout"] + u])
            with sp.Fori(0, NE // 2) as i:
                used.enter(i, 48)
                for name in ("w1", "w3"):
                    for k in range(KD):
                        for e in range(2):
                            load(ins[name][2 * i + e, k])
                for k in range(KD):
                    for e in range(2):
                        load(ins["w2"][2 * i + e, k].rearrange("(a p) n -> p a n", a=2),
                             lambda d: d.rearrange("p (a n) -> p a n", a=2))
                used.leave(NE // 2)
            sp.wait_ge(s_lno, 8 * 7)
            sp.dma_start(out, x).then_inc(s_out, 16)
            sp.wait_ge(s_out, 16)

        @block.gpsimd
        def _(pool):
            pool.memset(ones[:], 1.0).then_inc(s_const, 1)
            pool.memset(mean_w[:], 1.0 / D).then_inc(s_const, 1)
            pool.memset(ident[:], 0.0).then_inc(s_const, 1)
            pool.memset(csil[:], 0.0).then_inc(s_const, 1)
            pool.memset(slot[:], -1.0).then_inc(s_const, 1)
            pool.memset(aff[:], 0.0).then_inc(s_const, 1)
            pool.memset(epsv[:], 0.0).then_inc(s_const, 1)
            pool.wait_ge(s_const, 7)
            pool.affine_select(out=ident[:], in_=ident[:], compare_op=ALU.not_equal, fill=1.0, base=0,
                               pattern=[[-1, P]], channel_multiplier=1).then_inc(s_const, 1)
            pool.iota(iota[:], pattern=[[1, CAP]], base=0, channel_multiplier=0,
                      allow_small_or_imprecise_dtypes=True).then_inc(s_const, 1)
            for h in range(HEADS):
                for j in range(ST):
                    pool.wait_ge(s_exp, ST * h + j + 1)
                    blk = decay[:, j, P * j:P * j + P]
                    pool.affine_select(out=blk, in_=blk, compare_op=ALU.is_ge, fill=0.0, base=0,
                                       pattern=[[1, P]], channel_multiplier=-1).then_inc(s_tri, 1)

        @block.tensor
        def _(pe):
            bk_a = Banks(psum, [0, 1, 2, 3], s_ma, s_ea)
            bk_d = Banks(psum, [4, 5, 6, 7], s_md, s_ed)
            unit_no = Count(s_used)
            turn = [0]
            owed = []
            keep = [0]

            def begin(b):
                if b.filled.i is not None or b.filled.n >= len(b.banks):
                    pe.wait_ge(b.emptied.sem, b.filled.at(1 - len(b.banks)))
                return b.bank()

            def mm(o, lhs, rhs, start, stop, ends=None, tr=False):
                if tr:
                    ins_ = pe.transpose(o, lhs, rhs)
                else:
                    ins_ = pe.matmul(o, lhs, rhs, start=start, stop=stop)
                if ends is not None:
                    ends.filled.inc(ins_)
                elif len(owed) > keep[0]:
                    ins_.then_inc(owed.pop(0), 1)
                return ins_

            def read(b, ago=0):
                pe.wait_ge(b.emptied.sem, b.filled.at(-ago))

            def unit():
                slot_ = turn[0] % RING
                turns = turn[0] // RING + 1
                v = 16 * turns if unit_no.i is None else unit_no.i * (16 * unit_no.per // RING) + 16 * turns
                pe.wait_ge(s_arrived[slot_], v)
                turn[0] += 1
                unit_no.n += 1
                return ring[:, slot_, :]

            def used():
                owed.append(s_used)

            def enter(i, rounds, per_units, per_a, per_d):
                unit_no.enter(i, per_units)
                bk_a.filled.enter(i, per_a)
                bk_d.filled.enter(i, per_d)
                return turn[0], rounds

            def leave(entry):
                t0, rounds = entry
                for c_ in (unit_no, bk_a.filled, bk_d.filled):
                    c_.leave(rounds)
                turn[0] = t0 + unit_no.per * rounds

            def project(units, rhs, b, n=S):
                for _u in range(units):
                    w = unit()
                    for j in range(COLS // P):
                        o = begin(b)
                        for k in range(KD):
                            mm(o[:, 0:n], w[:, COLS * k + P * j:COLS * k + P * j + P], rhs[:, k, :],
                               k == 0, k == KD - 1, b if k == KD - 1 else None)
                    used()

            def project_tok(units, lhs, tiles, b):
                for _u in range(units):
                    w = unit()
                    for t in range(tiles):
                        o = begin(b)
                        for k in range(KD):
                            mm(o[:, 0:COLS], lhs[:, k, P * t:P * t + P], w[:, COLS * k:COLS * k + COLS],
                               k == 0, k == KD - 1, b if k == KD - 1 else None)
                    used()

            ln_no = [0]

            def summed(k):
                pe.wait_ge(s_ed, bk_d.filled.n - KD + k + 1)

            def layer_norm(src, sq, ready, tail=lambda: None):
                o = begin(bk_d)
                for k in range(KD):
                    ready(k)
                    mm(o, mean_w[:], src[:, k, :], k == 0, k == KD - 1, bk_d if k == KD - 1 else None)
                tail()
                o = begin(bk_d)
                for k in range(KD):
                    pe.wait_ge(s_lnq, KD * ln_no[0] + k + 1)
                    mm(o, mean_w[:], sq[:, k, :], k == 0, k == KD - 1, bk_d if k == KD - 1 else None)
                ln_no[0] += 1

            pe.wait_ge(s_const, 9)
            pe.wait_ge(s_vec, 16 * 14)
            for n in range(3):
                o = begin(bk_d)
                if n == 0:
                    mm(o[0:HW, :], fw1[:], mlp[0:EMB, 3, :], True, True, bk_d)
                else:
                    pe.wait_ge(s_sin, n)
                    mm(o[0:HW, :], fw2[:, n - 1, :], mlp[0:HW, 0, :], True, True, bk_d)
            pe.wait_ge(s_sin, 3)
            pe.wait_ge(s_cf, 16)
            for c in range(4):
                half, order = c // 2, c % 2
                if order == 0:
                    unit()
                for dirn in range(2):
                    for t in range(ST):
                        o = begin(bk_d)
                        at = 2 * D * dirn + D * order + 512 * half
                        mm(o, mlp[0:HW, 0, P * t:P * t + P], fw3[:, at:at + 512], True, True, bk_d)
                pe.wait_ge(s_eo, 2 * c + 2)
                if order == 1:
                    used()
                for r in range(8):
                    o = begin(bk_a)
                    part = h_even if r < 4 else h_odd
                    for k in range(ST):
                        last = r != 4 and k == ST - 1
                        mm(o, dft_f[:, r // 4, k, P * (r % 4):P * (r % 4) + P], part[:, k, :],
                           k == 0, last, bk_a if last else None)
                    if r == 4:
                        for k in range(ST):
                            mm(o, last_row[:, k, :], h_bwd[:, k, :], False, k == ST - 1,
                               bk_a if k == ST - 1 else None)
            o = begin(bk_d)
            pe.wait_ge(s_abs, 4)
            for c in range(4):
                half, order = c // 2, c % 2
                for n in range(4):
                    col = 8 * order + 4 * half + n
                    mm(o[:, col:col + 1], abs_sum[:, c, P * n:P * n + P], ones[:, 0:1], True, True,
                       bk_d if c == 3 and n == 3 else None)
            owed.append(s_free)
            col_bank = begin(bk_d)
            pe.wait_ge(s_csil, 1)
            for u in range(25):
                if u < 24:
                    w = unit()
                    o = begin(bk_a)
                    for r in range(2):
                        for g in range(4):
                            k = 4 * r + g
                            mm(o[32 * g:32 * g + 32, 0:COLS], csil[:, k, :], w[:, COLS * k:COLS * k + COLS],
                               r == 0, r == 1, bk_a if k == 7 else None)
                    used()
                if u > 0:
                    read(bk_a, 1 if u < 24 else 0)
                    for j in range(2):
                        col = 2 * (u - 1) + j
                        mm(col_bank[:, col:col + 1], mod_row[:, (u - 1) % 2, P * j:P * j + P], ones[:, 0:1],
                           True, True, bk_d if col == 47 else None)
                    if u < 24:
                        owed.append(s_mrow)
            pe.wait_ge(s_x, 16)
            for g in range(2):
                o = begin(bk_d)
                for k in range(KD):
                    mm(o[0:HEADS, :], wgate[:, k, 4 * g:4 * g + 4], x[:, k, :], k == 0, k == KD - 1,
                       bk_d if k == KD - 1 else None)
            note["qk"] = bk_d.filled.n
            project(4, x, bk_d)
            project_tok(2, x, ST, bk_a)
            project(2, x, bk_a)
            note["u"] = bk_a.filled.n
            project(2, x, bk_a)
            for g in range(4):
                o = begin(bk_a)
                pe.wait_ge(s_pool, g + 1)
                mm(o, poolw[:, g, :], mixed[:, g, :], True, True, bk_a)
            o = begin(bk_a)
            pe.wait_ge(s_row, 1)
            for t in range(ST):
                mm(o[:, HEADS * t:HEADS * t + HEADS], rows[0][:, P * t:P * t + P], ident[0:HEADS, 0:HEADS],
                   True, True, bk_a if t == ST - 1 else None, tr=True)
            pe.wait_ge(s_row, 2)
            pe.wait_ge(s_em, 1)
            for h in range(HEADS):
                pick = ident[0:HEADS, h:h + 1].broadcast_to([HEADS, P])
                o = begin(bk_a)
                mm(o, pick, rows[2], True, True, bk_a)
                pe.wait_ge(s_qk, KD)
                for j in range(ST):
                    o = begin(bk_d)
                    mm(o[:, P * j:S], qk[:, 4 + h, P * j:P * j + P], qk[:, h, P * j:S], True, True, bk_d)
                den = begin(bk_a)
                note["den", h] = bk_a.filled.n
                e_bc = begin(bk_d)
                mm(e_bc, pick, rows[3], True, True, bk_d)
                read(bk_d, 1)
                for j in range(ST):
                    mm(den[:, P * j:S], ones[:], decay[:, j, P * j:S], j == 0, j == ST - 1,
                       bk_a if j == ST - 1 else None)
                num = begin(bk_d)
                for j in range(ST):
                    mm(num[:, P * j:S], v_tok[:, j, P * h:P * h + P], decay[:, j, P * j:S], j == 0,
                       j == ST - 1, bk_d if j == ST - 1 else None)
                read(bk_d)
                o = begin(bk_d)
                mm(o, ones[:], hn[:, 0, :], True, True, bk_d)
                o = begin(bk_d)
                pe.wait_ge(s_hn, h + 1)
                mm(o, ones[:], hn[:, 1, :], True, True, bk_d)
            pe.wait_ge(s_ho, HEADS)
            project(4, mixed, bk_d)

            def keys_values():
                pe.wait_ge(s_mem, 16)
                project(4, mem_t, bk_a, MEM)
                project_tok(4, mem_t, 2, bk_a)

            layer_norm(region(1), region(2), summed, keys_values)
            pe.wait_ge(s_lno, KD)
            project(4, x, bk_a)
            read(bk_a)
            note["scores"] = bk_d.filled.n
            for h in range(HEADS):
                for t in range(ST):
                    o = begin(bk_d)
                    for i in range(2):
                        mm(o[:, 0:MEM], q_x[:, 2 * h + i, P * t:P * t + P], k_x[:, 2 * h + i, :],
                           i == 0, i == 1, bk_d if i == 1 else None)
                pe.wait_ge(s_xp, ST * (h + 1))
                for m in range(2):
                    o = begin(bk_a)
                    for t in range(ST):
                        mm(o[:, P * t:P * t + P], p_exp[:, t, P * m:P * m + P], ident[:], True, True,
                           bk_a if t == ST - 1 else None, tr=True)
                owed.append(s_pread)
                read(bk_a)
                for i in range(2):
                    o = begin(bk_a)
                    for m in range(2):
                        mm(o, v_x[:, m, P * (2 * h + i):P * (2 * h + i) + P], p_t[:, m, :], m == 0, m == 1,
                           bk_a if m == 1 else None)
            read(bk_a)
            keep[0] = 2
            project(4, o_x, bk_d)
            layer_norm(region(2), region(3), summed)
            pe.wait_ge(s_lno, 2 * KD)
            note["router"] = bk_a.filled.n
            o = begin(bk_a)
            for t in range(ST):
                for k in range(KD):
                    mm(o[:, NE * t:NE * t + NE], x[:, k, P * t:P * t + P], router[:, 0, k, :], k == 0,
                       k == KD - 1, bk_a if t == ST - 1 and k == KD - 1 else None)
            pe.wait_ge(s_gt, 1)
            o = begin(bk_a)
            for t in range(ST):
                mm(o[0:NE, P * t:P * t + P], gates[:, t, :], ident[:], True, True,
                   bk_a if t == ST - 1 else None, tr=True)
            read(bk_a)
            for e in range(NE):
                o = begin(bk_a)
                mm(o, ident[0:NE, e:e + 1].broadcast_to([NE, P]), gate_t, True, True, bk_a)
            note["spread"] = bk_a.filled.n
            note["moe1_a"], note["moe1_d"] = bk_a.filled.n, bk_d.filled.n
            assert len(owed) == 2
            keep[0] = 0
            rounds = 3 * NE // RING
            with pe.Fori(0, rounds) as i:
                entry = enter(i, rounds, RING, 8, 24)
                for pair in range(2):
                    for e in range(2):
                        for b in (bk_a, bk_d):
                            w = unit()
                            for j in range(2):
                                o = begin(b)
                                for k in range(KD):
                                    mm(o, w[:, FE * k + P * j:FE * k + P * j + P], x[:, k, :], k == 0,
                                       k == KD - 1, b if k == KD - 1 else None)
                            used()
                    w_d = [unit(), unit()]
                    pe.wait_ge(s_hid, 8 * i + 4 * (pair + 1))
                    for n in range(KD):
                        o = begin(bk_d)
                        for m in range(4):
                            mm(o, w_d[m // 2][:, D * (m % 2) + P * n:D * (m % 2) + P * n + P],
                               hid[:, 4 * pair + m, :], m == 0, m == 3, bk_d if m == 3 else None)
                    used()
                    used()
                assert len(owed) == 2
                leave(entry)
            layer_norm(region(3), region(1), summed)
            layer_norm(x, region(2), lambda k: pe.wait_ge(s_px, k + 1))
            pe.wait_ge(s_lno, 4 * KD)
            note["u_hy"] = bk_a.filled.n
            project(12, h2, bk_a)

            def to_tokens(src):
                for t in range(ST):
                    for half in range(2):
                        o = begin(bk_a)
                        for n in range(4):
                            mm(o[:, P * n:P * n + P], src[:, 4 * half + n, P * t:P * t + P], ident[:], True, True,
                               bk_a if n == 3 else None, tr=True)

            for order in range(2):
                pe.wait_ge(s_uc, 3 * KD)
                if order:
                    pe.wait_ge(s_z1, KD)
                to_tokens(u_hy[0])
                read(bk_a)
                for half in range(2):
                    cos_f, sin_f = [unit().rearrange("p (k n) -> p k n", k=ST) for _ in range(2)]
                    note["k", order, half] = [(turn[0] % RING, 16 * (turn[0] // RING + 1)),
                                              ((turn[0] + 1) % RING, 16 * ((turn[0] + 1) // RING + 1))]
                    for r in range(4):
                        for f in (cos_f, sin_f):
                            o = begin(bk_d)
                            for k in range(ST):
                                mm(o, f[:, k, P * r:P * r + P], z_tok[:, k, 512 * half:512 * half + 512],
                                   k == 0, k == ST - 1, bk_d if k == ST - 1 else None)
                    used()
                    used()
                    unit()
                    unit()
                    pe.wait_ge(s_k, 4 * (2 * order + half + 1))
                    used()
                    used()
                    inv = [unit().rearrange("p (k n) -> p k n", k=4) for _ in range(2)]
                    for n in range(4):
                        o = begin(bk_d)
                        for r in range(8):
                            mm(o, spec[:, r, P * n:P * n + P], inv[r // 4][:, r % 4, :], r == 0, r == 7,
                               bk_d if r == 7 else None)
                    used()
                    used()
            pe.wait_ge(s_z1, 2 * KD)
            note["hyout"] = bk_a.filled.n
            keep[0] = 2
            project(4, u_hy[0], bk_a)
            layer_norm(region(2), region(3), lambda k: pe.wait_ge(s_res, k + 1))
            layer_norm(x, region(3), lambda k: pe.wait_ge(s_lno, 4 * KD + k + 1))
            pe.wait_ge(s_lno, 6 * KD)
            o = begin(bk_d)
            for t in range(ST):
                for k in range(KD):
                    mm(o[:, NE * t:NE * t + NE], h2[:, k, P * t:P * t + P], router[:, 1, k, :], k == 0,
                       k == KD - 1, bk_d if t == ST - 1 and k == KD - 1 else None)
            to_tokens(h2)
            o = begin(bk_a)
            pe.wait_ge(s_aff, 1)
            for t in range(ST):
                mm(o[0:NE, P * t:P * t + P], aff[:, t, 0:NE], ident[:], True, True,
                   bk_a if t == ST - 1 else None, tr=True)
            note["aff_t"] = bk_a.filled.n
            o = begin(bk_d)
            pe.wait_ge(s_top, 1)
            for t in range(ST):
                mm(o[:, NE * t:NE * t + NE], mask_t[:, P * t:P * t + P], ident[0:NE, 0:NE], True, True,
                   bk_d if t == ST - 1 else None, tr=True)

            def gather():
                for n in range(2):
                    o = begin(bk_a)
                    for t in range(ST):
                        mm(o, onehot[:, t, :], h_tok[:, t, 512 * n:512 * n + 512], t == 0, t == ST - 1,
                           bk_a if t == ST - 1 else None)
                for n in range(2):
                    read(bk_a, 1)
                    o = begin(bk_a)
                    for j in range(4):
                        mm(o[:, P * j:P * j + P], x_sel[:, 0, 512 * n + P * j:512 * n + P * j + P], ident[:],
                           True, True, bk_a if j == 3 else None, tr=True)

            pe.wait_ge(s_oh, 1)
            gather()
            assert len(owed) == 2
            keep[0] = 0
            note["moe2_a"], note["moe2_d"] = bk_a.filled.n, bk_d.filled.n
            with pe.Fori(0, NE // 2) as i:
                entry = enter(i, NE // 2, 48, 12, 16)
                read(bk_a)
                for b in (bk_a, bk_d):
                    if b is bk_d:
                        read(bk_d)
                    o = [b.bank(n) for n in range(4)]
                    for k in range(KD):
                        w = [unit(), unit()]
                        for n in range(4):
                            for e in range(2):
                                mm(o[n][CAP * e:CAP * e + CAP, :], x_sel_t[:, k, CAP * e:CAP * e + CAP],
                                   w[e][:, 512 * n:512 * n + 512], k == 0, k == KD - 1,
                                   b if k == KD - 1 and e == 1 else None)
                        used()
                        used()
                pe.wait_ge(s_oh, i + 2)
                gather()
                for n in range(4):
                    o = begin(bk_d)
                    for j in range(4):
                        f = 4 * n + j
                        mm(o[:, P * j:P * j + P], hid2[:, 0, P * f:P * f + P], ident[:], True, True,
                           bk_d if j == 3 else None, tr=True)
                pe.wait_ge(s_ohg, i + 1)
                for n in range(2):
                    o = begin(bk_a)
                    for j in range(2):
                        mm(o[:, P * j:P * j + P], onehot_g[:, 2 * n + j, :], ident[:], True, True,
                           bk_a if j == 1 else None, tr=True)
                read(bk_d)
                begin(bk_a)
                pe.wait_ge(s_ea, bk_a.filled.at(-2))
                o = [bk_a.bank(n) for n in range(2)]
                for k in range(KD):
                    w = [unit(), unit()]
                    for a in range(2):
                        for n in range(2):
                            for e in range(2):
                                mm(o[n][CAP * e:CAP * e + CAP, :], hid2_t[:, 2 * k + a, CAP * e:CAP * e + CAP],
                                   w[e][:, D * a + 512 * n:D * a + 512 * n + 512], k == 0 and a == 0,
                                   k == KD - 1 and a == 1, bk_a if k == KD - 1 and a == 1 and e == 1 else None)
                    used()
                    used()
                read(bk_a)
                for n in range(KD):
                    o = begin(bk_d)
                    mm(o, y_sel[:, 0, P * n:P * n + P], scat, True, True, bk_d)
                assert len(owed) == 2
                leave(entry)
            layer_norm(region(2), region(3), lambda k: pe.wait_ge(s_res, KD + k + 1))

        @block.scalar
        def _(act):
            bk = Banks(psum, [0, 1, 2, 3], s_ma, s_ea)
            step = Count(s_astep)
            inv_var = [0]
            ln_no = [0]

            def take():
                act.wait_ge(s_ma, bk.filled.at(1))
                o = bk.bank()
                bk.filled.n += 1
                return o

            def empty(o, dst, func=ACT.Identity, **more):
                bk.emptied.inc(act.activation(dst, o, func, **more))

            def let_go(o):
                bk.emptied.inc(act.activation(tiny[0:1, 0, 7:8], o[0:1, 0:1], ACT.Copy))

            def layer_norm(cen, sq, gain, shift, dst):
                for k in range(KD):
                    act.wait_ge(s_lnc, KD * ln_no[0] + k + 1)
                    act.activation(sq[:, k, :], cen[:, k, :], ACT.Square).then_inc(s_lnq, 1)
                yield
                rstd(ln_r[:, 1, :], ln_r[:, 0, :])
                for k in range(KD):
                    act.wait_ge(s_lnm, KD * ln_no[0] + k + 1)
                    act.activation(dst[:, k, :], cen[:, k, :], ACT.Identity, bias=shift(k), scale=gain(k))\
                       .then_inc(s_lno, 1)
                ln_no[0] += 1

            def rstd(dst, src):
                inv_var[0] += 1
                act.wait_ge(s_rv, inv_var[0])
                act.activation(dst, src, ACT.Sqrt).then_inc(s_rstd, 1)

            def whole(steps):
                for _ in steps:
                    pass

            act.wait_ge(s_vec, 16 * 14)
            act.wait_ge(s_const, 9)
            c_at = VAT["c"]
            act.activation(csil[:, :, 0], vec[:, c_at:c_at + KD], ACT.Silu).then_inc(s_csil, 1)
            for n in range(3):
                act.wait_ge(s_mlp, n + 1)
                act.activation(mlp[0:HW, 0, :], mlp[0:HW, 1, :], ACT.Sin).then_inc(s_sin, 1)
            for c in range(4):
                if c:
                    act.wait_ge(s_kst, 16 * c)
                for r in range(8):
                    empty(take(), k_out[:, r, :])
                act.wait_ge(s_ea, bk.emptied.at())
                act.dma_start(ins["spectra"][c], k_out).then_inc(s_kst, 16)
            act.wait_ge(s_abs, 4)
            for u in range(24):
                if u >= 2:
                    act.wait_ge(s_mrow, u - 1)
                o = take()
                empty(o[:, 0:COLS], mod_row[:, u % 2, :])
            act.wait_ge(s_gb, 1)
            step.inc(act.activation(rows[2], rows[2], ACT.Exp, scale=-1.0))
            act.wait_ge(s_astep, step.at())
            act.activation(rows[2], rows[2], ACT.Ln, bias=1.0).then_inc(s_gl, 1)
            act.wait_ge(s_row, 3)
            act.activation(rows[3], rows[3], ACT.Exp, scale=-1.0).then_inc(s_em, 1)
            for n in range(KD):
                act.wait_ge(s_ed, note["qk"] + n + 1)
                act.activation(qk[:, n, :], conv[:, n, :], ACT.Silu).then_inc(s_qk, 1)
            act.wait_ge(s_kst, 64)
            for u in range(2):
                for t in range(ST):
                    o = take()
                    empty(o[:, 0:COLS], v_tok[:, t, COLS * u:COLS * u + COLS])
            for h in range(HEADS):
                empty(take(), o_gate[:, h, :], ACT.Sigmoid)
            for g in range(4):
                if g:
                    act.wait_ge(s_pool, g)
                empty(take(), u_pad[:, 16:528])
            for g in range(4):
                empty(take(), mixed[:, 4 + g, :], scale=vcol("pool_scale", g))
            o = take()
            empty(o[:, 0:ST * HEADS], acol[:])
            act.wait_ge(s_ea, bk.emptied.at())
            for h in range(HEADS):
                o = take()
                if h:
                    act.wait_ge(s_hn, h)
                for j in range(ST):
                    act.activation(decay[:, j, P * j:S], o[:, P * j:S], ACT.Exp, bias=acol[:, j, h:h + 1])\
                       .then_inc(s_exp, 1)
                let_go(o)
                if h:
                    act.wait_ge(s_ho, h)
                empty(take(), hn[:, 2, :], ACT.Abs)
                rstd(hn[:, 3, :], hn[:, 3, :])
            ln = layer_norm(region(1), region(2), lambda k: vcol("ln_mix_g", k), lambda k: vcol("ln_mix_b", k), x)
            next(ln)
            act.wait_ge(s_ho, HEADS)
            for n in range(KD):
                o = take()
                empty(o[:, 0:MEM], k_x[:, n, :])
            for u in range(4):
                for m in range(2):
                    o = take()
                    empty(o[:, 0:COLS], v_x[:, m, COLS * u:COLS * u + COLS])
            whole(ln)
            for n in range(KD):
                empty(take(), q_x[:, n, :])
            for h in range(HEADS):
                for t in range(ST):
                    act.wait_ge(s_ed, note["scores"] + ST * h + t + 1)
                    act.activation(p_exp[:, t, :], p_exp[:, t, :], ACT.Exp, scale=XDH ** -0.5,
                                   accum_out=tiny[:, t, 1:2]).then_inc(s_xe, 1)
                for m in range(2):
                    empty(take(), p_t[:, m, :])
                for n in range(2):
                    empty(take(), o_x[:, 2 * h + n, :])
            whole(layer_norm(region(2), region(3), lambda k: vcol("ln_x_g", k), lambda k: vcol("ln_x_b", k), x))
            o = take()
            empty(o[:, 0:ST * NE], route[:, 0, :], ACT.Sigmoid)
            o = take()
            empty(o[0:NE, :], gate_t)
            for e in range(NE):
                empty(take(), gate_bc[:, e, :])
            rounds = 3 * NE // RING
            with act.Fori(0, rounds) as i:
                bk.filled.enter(i, 8)
                bk.emptied.enter(i, 8)
                for q in range(8):
                    o = take()
                    if q >= 2:
                        act.wait_ge(s_hid, 8 * i + q - 1)
                    empty(o, silu1[:, q % 2, :], ACT.Silu)
                bk.filled.leave(rounds)
                bk.emptied.leave(rounds)
            whole(layer_norm(region(3), region(1), lambda k: vcol("ln_moe_g", k), lambda k: vcol("ln_moe_b", k), x))
            whole(layer_norm(region(1), region(2), lambda k: modp[:, 8 + k:9 + k], lambda k: modc[:, k:k + 1], h2))
            act.wait_ge(s_hz, 1)
            for n in range(3 * KD):
                o = take()
                if n >= 2:
                    act.wait_ge(s_uc, n - 1)
                empty(o, hpad[:, n % 2, 1:S + 1], bias=vcol("hy_b_in", n))

            def rows_of_tokens(dst):
                for t in range(ST):
                    for half in range(2):
                        empty(take(), dst[:, t, 512 * half:512 * half + 512])

            for order in range(2):
                rows_of_tokens(z_tok)
            for n in range(KD):
                empty(take(), region(2)[:, n, :], bias=modg[:, n:n + 1], scale=modp[:, 16 + n:17 + n])
            whole(layer_norm(region(2), region(3), lambda k: vcol("ln_g2", k), lambda k: vcol("ln_b2", k), x))
            whole(layer_norm(region(1), region(3), lambda k: modp[:, 32 + k:33 + k],
                             lambda k: modc[:, 24 + k:25 + k], h2))
            act.wait_ge(s_r0, 1)
            act.activation(route[:, 0, :], route[:, 0, :], ACT.Exp).then_inc(s_r1, 1)
            rows_of_tokens(h_tok)
            o = take()
            empty(o[0:NE, :], aff_t)

            def gathered():
                for n in range(2):
                    empty(take(), x_sel[:, 0, 512 * n:512 * n + 512])
                for n in range(2):
                    o = take()
                    empty(o.rearrange("p (k n) -> p k n", k=4), x_sel_t[:, 4 * n:4 * n + 4, :])

            gathered()
            with act.Fori(0, NE // 2) as i:
                bk.filled.enter(i, 12)
                bk.emptied.enter(i, 12)
                for n in range(4):
                    empty(take(), silu2[:, 0, 512 * n:512 * n + 512], ACT.Silu)
                gathered()
                for n in range(2):
                    o = take()
                    empty(o[:, 0:256], scat[:, 256 * n:256 * n + 256])
                for n in range(2):
                    empty(take(), y_sel[:, 0, 512 * n:512 * n + 512])
                bk.filled.leave(NE // 2)
                bk.emptied.leave(NE // 2)
            whole(layer_norm(region(2), region(3), lambda k: vcol("ln_g2", 8 + k), lambda k: vcol("ln_b2", 8 + k), x))

        @block.vector
        def _(dve):
            bk = Banks(psum, [4, 5, 6, 7], s_md, s_ed)
            step = Count(s_step)
            inv_var = [0]
            ln_no = [0]

            def take():
                dve.wait_ge(s_md, bk.filled.at(1))
                o = bk.bank()
                bk.filled.n += 1
                return o

            def done(ins_):
                bk.emptied.inc(ins_)

            def let_go(o):
                done(dve.tensor_copy(tiny[0:1, 1, 7:8], o[0:1, 0:1]))

            def after_bank():
                dve.wait_ge(s_ed, bk.emptied.at())

            def do(ins_):
                step.inc(ins_)

            def after():
                dve.wait_ge(s_step, step.at())

            def tt(dst, a, b, op):
                return dve.tensor_tensor(dst, a, b, op)

            def ts(dst, a, s1, op0, s2=None, op1=None):
                if op1 is None:
                    return dve.tensor_scalar(dst, a, s1, None, op0)
                return dve.tensor_scalar(dst, a, s1, s2, op0, op1)

            def stt(dst, a, scal, b, op0, op1):
                return dve.scalar_tensor_tensor(out=dst, in0=a, scalar=scal, in1=b, op0=op0, op1=op1)

            def inverse_var(o, dst, scale, eps):
                done(ts(dst, o, scale, ALU.mult, eps, ALU.add))
                after_bank()
                dve.reciprocal(dst, dst).then_inc(s_rv, 1)
                inv_var[0] += 1
                dve.wait_ge(s_rstd, inv_var[0])

            def layer_norm(src, cen, eps=LN_EPS):
                o = take()
                for k in range(KD):
                    tt(cen[:, k, :], src[:, k, :], o, ALU.subtract).then_inc(s_lnc, 1)
                let_go(o)
                inverse_var(take(), ln_r[:, 0, :], 1.0, eps)
                for k in range(KD):
                    tt(cen[:, k, :], cen[:, k, :], ln_r[:, 1, :], ALU.mult).then_inc(s_lnm, 1)
                ln_no[0] += 1

            dve.wait_ge(s_vec, 16 * 14)
            dve.wait_ge(s_const, 9)
            a, r = mlp[0:HW, 1, :], mlp[0:HW, 2, :]
            for n in range(3):
                o = take()
                b_col = fvec[:, 0:1] if n == 0 else fvec[:, n + 1:n + 2]
                done(ts(a, o[0:HW, :], b_col, ALU.add, fvec[:, 1:2], ALU.mult))
                after_bank()
                do(ts(r, a, 1.0 / TWO_PI, ALU.mult, ROUND, ALU.add))
                after()
                do(ts(r, r, ROUND, ALU.subtract))
                after()
                do(stt(a, r, -PI_HI, a, ALU.mult, ALU.add))
                after()
                do(stt(a, r, -PI_LO, a, ALU.mult, ALU.add))
                after()
                ts(a, a, -PI_IN, ALU.max, PI_IN, ALU.min).then_inc(s_mlp, 1)
            for c in range(4):
                half = c // 2
                dve.wait_ge(s_arrived[half], 16)
                win = ring[:, half, :].rearrange("p (k n) -> p k n", k=ST)
                if c:
                    dve.wait_ge(s_ma, 8 * c)
                for taps in (h_fwd, h_bwd):
                    for t in range(ST):
                        done(tt(taps[:, t, :], take(), win[:, t, :], ALU.mult))
                after_bank()
                do(dve.memset(h_bwd[0:1, 0, :], 0.0))
                after()
                tt(h_even, h_fwd, h_bwd, ALU.add).then_inc(s_eo, 1)
                tt(h_odd, h_fwd, h_bwd, ALU.subtract).then_inc(s_eo, 1)
                do(dve.tensor_reduce(abs_sum[:, c, :], h_fwd.rearrange("p k n -> p n k"), AX, ALU.add,
                                     apply_absolute_value=True))
                do(dve.tensor_reduce(abs_tmp, h_bwd.rearrange("p k n -> p n k"), AX, ALU.add,
                                     apply_absolute_value=True))
                after()
                tt(abs_sum[:, c, :], abs_sum[:, c, :], abs_tmp, ALU.add).then_inc(s_abs, 1)
            done(dve.reciprocal(filt_rn[:], take()[:, 0:16]))
            m_at = VAT["mod_b"]
            done(tt(modc[:], take()[:, 0:48], vec[:, m_at:m_at + 48], ALU.add))
            after_bank()
            do(ts(modp[:], modc[:], 1.0, ALU.add))
            after()
            b_at = VAT["hy_b_out"]
            do(tt(modg[:], modp[:, 16:24], vec[:, b_at:b_at + KD], ALU.mult))
            done(ts(rows[0], take()[0:HEADS, :], gbias[:, 0:1], ALU.add))
            done(ts(rows[1], take()[0:HEADS, :], gbias[:, 1:2], ALU.add))
            after_bank()
            stt(rows[2], rows[1], -1.0, rows[1], ALU.mult, ALU.max).then_inc(s_gb, 1)
            dve.wait_ge(s_gl, 1)
            do(stt(rows[1], rows[1], 0.0, rows[2], ALU.min, ALU.subtract))
            after()
            do(dve.tensor_tensor_scan(rows[3], rows[1], rows[1], 0.0, ALU.add, ALU.bypass))
            after()
            tt(rows[0], rows[0], rows[3], ALU.subtract).then_inc(s_row, 1)
            dve.wait_ge(s_row, 1)
            do(dve.tensor_tensor_scan(rows[1], rows[0], rows[0], 0.0, ALU.max, ALU.max))
            after()
            ts(rows[2], rows[1], -1.0, ALU.mult).then_inc(s_row, 1)
            tt(rows[3], rows[3], rows[1], ALU.add).then_inc(s_row, 1)
            for n in range(KD):
                z = take()
                do(ts(conv[:, n, :], z, vcol("conv", 24 + n), ALU.mult))
                for back in range(1, 4):
                    after()
                    ins_ = stt(conv[:, n, back:S], z[:, 0:S - back], vcol("conv", 8 * (3 - back) + n),
                               conv[:, n, back:S], ALU.mult, ALU.add)
                    if back == 3:
                        done(ins_)
                    else:
                        do(ins_)
            do(dve.memset(u_pad[:, 0:16], 0.0))
            for g in range(4):
                dve.wait_ge(s_ea, note["u"] + g + 1)
                after()
                cur, lo = u_pad, 0
                for d in range(g + 1):
                    nxt = (pool_a, pool_b)[d % 2]
                    lo += 1 << d
                    do(tt(nxt[:, lo:528], cur[:, lo:528], cur[:, lo - (1 << d):528 - (1 << d)], ALU.add))
                    after()
                    cur = nxt
                do(stt(mixed[:, g, :], cur[:, 16:528], 1.0 / POOLW[g], u_pad[:, 16:528], ALU.mult, ALU.subtract))
                do(tt(route[:, 0, 0:16], cur[:, 16:32], pool16[:, g, :], ALU.mult))
                after()
                tt(mixed[:, g, 0:16], route[:, 0, 0:16], u_pad[:, 16:32], ALU.subtract).then_inc(s_pool, 1)
            for h in range(HEADS):
                for j in range(ST):
                    o = take()
                    dve.wait_ge(s_tri, ST * h + j + 1)
                    done(stt(decay[:, j, P * j:S], o[:, P * j:S], DH ** -0.5, decay[:, j, P * j:S],
                             ALU.mult, ALU.mult))
                dve.wait_ge(s_ea, note["den", h] + 1)
                done(tt(hn[:, 2, :], take(), hn[:, 2, :], ALU.max))
                after_bank()
                do(dve.reciprocal(hn[:, 2, :], hn[:, 2, :]))
                after()
                done(tt(hn[:, 0, :], take(), hn[:, 2, :], ALU.mult))
                after_bank()
                done(stt(hn[:, 0, :], take(), -1.0 / DH, hn[:, 0, :], ALU.mult, ALU.add))
                after_bank()
                tt(hn[:, 1, :], hn[:, 0, :], hn[:, 0, :], ALU.mult).then_inc(s_hn, 1)
                inverse_var(take(), hn[:, 3, :], 1.0 / DH, LN_EPS)
                do(tt(hn[:, 0, :], hn[:, 0, :], hn[:, 3, :], ALU.mult))
                after()
                stt(mixed[:, h, :], hn[:, 0, :], vcol("head_g", h), o_gate[:, h, :], ALU.mult, ALU.mult)\
                    .then_inc(s_ho, 1)
            for n in range(KD):
                done(stt(region(1)[:, n, :], x[:, n, :], ALPHA, take(), ALU.mult, ALU.add))
            after_bank()
            layer_norm(region(1), region(1))
            for h in range(HEADS):
                if h:
                    dve.wait_ge(s_pread, h)
                for t in range(ST):
                    o = take()
                    do(dve.tensor_reduce(tiny[:, t, 0:1], o[:, 0:MEM], AX, ALU.max))
                    after()
                    done(ts(p_exp[:, t, :], o[:, 0:MEM], tiny[:, t, 0:1], ALU.subtract))
                for t in range(ST):
                    dve.wait_ge(s_xe, ST * h + t + 1)
                    do(dve.reciprocal(tiny[:, t, 2:3], tiny[:, t, 1:2]))
                    after()
                    ts(p_exp[:, t, :], p_exp[:, t, :], tiny[:, t, 2:3], ALU.mult).then_inc(s_xp, 1)
            dve.wait_ge(s_lno, KD)
            for n in range(KD):
                done(stt(region(2)[:, n, :], x[:, n, :], ALPHA, take(), ALU.mult, ALU.add))
            after_bank()
            layer_norm(region(2), region(2))
            dve.wait_ge(s_ea, note["router"] + 1)
            score = route[:, 0, :]
            sel = route[:, 1, :]
            g2 = route[:, 2, :]
            pairs = ptmp[:, 0, 0:96].rearrange("p (g q) -> p g q", q=6)
            cmp_ = ptmp[:, 1, 0:256].rearrange("p (e f) -> p e f", e=NE)
            cmp2 = ptmp[:, 0, 256:512].rearrange("p (e f) -> p e f", e=NE)
            for t in range(ST):
                do(tt(sel[:, NE * t:NE * t + NE], score[:, NE * t:NE * t + NE], rbias[:], ALU.add))
            after()
            sel4 = sel.rearrange("p (g m) -> p g m", m=4)
            q = 0
            for i_ in range(4):
                for j_ in range(i_ + 1, 4):
                    do(tt(pairs[:, :, q], sel4[:, :, i_], sel4[:, :, j_], ALU.add))
                    q += 1
            after()
            do(dve.tensor_reduce(g2[:, 0:16], pairs, AX, ALU.max))
            after()

            def ranks(dst, val, n):
                c1, c2 = cmp_[:, 0:n, 0:n], cmp2[:, 0:n, 0:n]
                of = val.rearrange("p (o f) -> p o f", o=1).broadcast_to([P, n, n])
                to = val.rearrange("p (e o) -> p e o", o=1).broadcast_to([P, n, n])
                do(tt(c1, of, to, ALU.is_equal))
                do(tt(c2, of, to, ALU.is_gt))
                after()
                do(tt(c1, c1, lower[:, 0:n, 0:n], ALU.mult))
                after()
                do(tt(c1, c1, c2, ALU.add))
                after()
                do(dve.tensor_reduce(dst, c1, AX, ALU.add))
                after()

            for t in range(ST):
                ranks(g2[:, 16 + 4 * t:20 + 4 * t], g2[:, 4 * t:4 * t + 4], 4)
            do(ts(g2[:, 16:32], g2[:, 16:32], 0.0, ALU.is_equal))
            after()
            do(ts(g2[:, 32:48], g2[:, 16:32], 1.0, ALU.subtract, -NEG, ALU.mult))
            in_group = g2[:, 16:32].rearrange("p (g o) -> p g o", o=1).broadcast_to([P, 16, 4])
            out_group = g2[:, 32:48].rearrange("p (g o) -> p g o", o=1).broadcast_to([P, 16, 4])
            do(tt(sel4, sel4, in_group, ALU.mult))
            after()
            do(tt(sel4, sel4, out_group, ALU.add))
            after()
            rank = route[:, 3, :]
            for t in range(ST):
                ranks(rank[:, NE * t:NE * t + NE], sel[:, NE * t:NE * t + NE], NE)
            do(stt(rank, rank, 2.0, score, ALU.is_lt, ALU.mult))
            after()
            rank3 = rank.rearrange("p (t e) -> p t e", e=NE)
            do(dve.tensor_reduce(route[:, 4, 0:ST], rank3, AX, ALU.add))
            after()
            do(dve.reciprocal(route[:, 4, 8:8 + ST], route[:, 4, 0:ST]))
            after()
            for t in range(ST):
                ins_ = ts(gates[:, t, :], rank3[:, t, :], route[:, 4, 8 + t:9 + t], ALU.mult)
                if t == ST - 1:
                    ins_.then_inc(s_gt, 1)
                else:
                    do(ins_)
            dve.wait_ge(s_lno, 2 * KD)
            do(ts(y1, x, ALPHA, ALU.mult))
            after()
            dve.wait_ge(s_ea, note["spread"])
            rounds = 3 * NE // RING
            with dve.Fori(0, rounds) as i:
                bk.filled.enter(i, 24)
                bk.emptied.enter(i, 24)
                step.enter(i, 8)
                for pair in range(2):
                    for m in range(4):
                        o = take()
                        q = 4 * pair + m
                        dve.wait_ge(s_ea, 8 * i + note["moe1_a"] + q + 1)
                        done(tt(hid[:, q, :], o, silu1[:, q % 2, :], ALU.mult))
                        after_bank()
                        tt(hid[:, q, :], hid[:, q, :], gate_bc[:, 4 * i + 2 * pair + m // 2, :], ALU.mult)\
                            .then_inc(s_hid, 1)
                    for n in range(KD):
                        done(tt(y1[:, n, :], take(), y1[:, n, :], ALU.add))
                for _ in range(8):
                    step.n += 1
                step.n -= 8
                step.per = 0
                bk.filled.leave(rounds)
                bk.emptied.leave(rounds)
                step.leave(rounds)
            after_bank()
            layer_norm(region(3), region(3))
            dve.wait_ge(s_pos, 16)
            for k in range(KD):
                dve.wait_ge(s_lno, 2 * KD + k + 1)
                tt(x[:, k, :], x[:, k, :], pos[:, k, :], ALU.add).then_inc(s_px, 1)
            dve.wait_ge(s_px, KD)
            dve.memset(hpad, 0.0).then_inc(s_hz, 1)
            layer_norm(x, region(1), MOD_EPS)
            for n in range(3 * KD):
                dst = u_hy[n // KD][:, n % KD, :]
                dve.wait_ge(s_ea, note["u_hy"] + n + 1)
                do(ts(dst, hpad[:, n % 2, 1:S + 1], vcol("hy_conv_w", 24 + n), ALU.mult,
                      vcol("hy_conv_b", n), ALU.add))
                after()
                do(stt(dst, hpad[:, n % 2, 0:S], vcol("hy_conv_w", n), dst, ALU.mult, ALU.add))
                after()
                stt(dst, hpad[:, n % 2, 2:S + 2], vcol("hy_conv_w", 48 + n), dst, ALU.mult, ALU.add)\
                    .then_inc(s_uc, 1)
            dve.wait_ge(s_uc, 3 * KD)
            for order in range(2):
                for half in range(2):
                    ks = []
                    for slot_, value in note["k", order, half]:
                        dve.wait_ge(s_arrived[slot_], value)
                        ks.append(ring[:, slot_, :].rearrange("p (k n) -> p k n", k=4))
                    kc, ksn = ks
                    for r_ in range(4):
                        zc, zs = take(), take()
                        t1, t2 = ptmp[:, 0, :], ptmp[:, 1, :]
                        do(tt(spec[:, r_, :], zc, kc[:, r_, :], ALU.mult))
                        done(tt(spec[:, 4 + r_, :], zc, ksn[:, r_, :], ALU.mult))
                        do(tt(t1, zs, ksn[:, r_, :], ALU.mult))
                        done(tt(t2, zs, kc[:, r_, :], ALU.mult))
                        after()
                        after_bank()
                        if r_ == 0:
                            do(dve.tensor_copy(spec[0:1, 4, :], t1[0:1, :]))
                            after()
                            do(dve.memset(t1[0:1, :], 0.0))
                            do(dve.memset(t2[0:1, :], 0.0))
                            after()
                        do(tt(spec[:, r_, :], spec[:, r_, :], t1, ALU.subtract))
                        tt(spec[:, 4 + r_, :], spec[:, 4 + r_, :], t2, ALU.add).then_inc(s_k, 1)
                        dve.wait_ge(s_k, 4 * (2 * order + half) + r_ + 1)
                    after()
                    for n in range(4):
                        m = 4 * half + n
                        z = u_hy[0][:, m, :]
                        t1, t2 = ptmp[:, 0, :], ptmp[:, 1, :]
                        do(ts(t1, z, vcol("hy_f_bias", 8 * order + m), ALU.mult))
                        after()
                        done(stt(t2, take(), filt_rn[:, 8 * order + m:8 * order + m + 1], t1, ALU.mult, ALU.add))
                        after_bank()
                        tt(z, t2, u_hy[1 + order][:, m, :], ALU.mult).then_inc(s_z1, 1)
                        dve.wait_ge(s_z1, KD * order + 4 * half + n + 1)
            for n in range(KD):
                dve.wait_ge(s_ea, note["hyout"] + n + 1)
                stt(region(2)[:, n, :], x[:, n, :], ALPHA, region(2)[:, n, :], ALU.mult, ALU.add)\
                    .then_inc(s_res, 1)
            dve.wait_ge(s_res, KD)
            layer_norm(region(2), region(2))
            dve.wait_ge(s_lno, 5 * KD)
            layer_norm(x, region(1), MOD_EPS)
            logit = route[:, 0, :]
            l3 = logit.rearrange("p (t e) -> p t e", e=NE)
            o = take()[:, 0:ST * NE]
            do(dve.tensor_reduce(route[:, 1, 0:ST], o.rearrange("p (t e) -> p t e", e=NE), AX, ALU.max))
            after()
            for t in range(ST):
                ins_ = ts(l3[:, t, :], o[:, NE * t:NE * t + NE], route[:, 1, t:t + 1], ALU.subtract)
                if t == ST - 1:
                    done(ins_)
                else:
                    do(ins_)
            after_bank()
            after()
            do(dve.memset(tiny[:, 3, 3:4], 0.0))
            after()
            dve.memset(tiny[:, 3, 4:5], 0.0).then_inc(s_r0, 1)
            dve.wait_ge(s_r1, 1)
            do(dve.tensor_reduce(route[:, 2, 0:ST], l3, AX, ALU.add))
            after()
            do(dve.reciprocal(route[:, 2, 8:8 + ST], route[:, 2, 0:ST]))
            after()
            for t in range(ST):
                ins_ = ts(aff[:, t, 0:NE], l3[:, t, :], route[:, 2, 8 + t:9 + t], ALU.mult)
                if t == ST - 1:
                    ins_.then_inc(s_aff, 1)
                else:
                    do(ins_)
            dve.wait_ge(s_lno, 6 * KD)
            do(dve.memset(y2, 0.0))
            dve.wait_ge(s_ea, note["aff_t"])
            do(dve.tensor_copy(work_t, aff_t))
            after()
            for _ in range(CAP // 8):
                do(dve.max(top8[:], work_t))
                after()
                do(dve.match_replace(work_t, top8[:], work_t, -1.0))
                after()
            do(ts(mask_t, work_t, 0.0, ALU.is_lt))
            after()
            do(dve.tensor_tensor_scan(work_t, mask_t, mask_t, 0.0, ALU.add, ALU.bypass))
            after()
            do(tt(work_t, work_t, mask_t, ALU.mult))
            after()
            ts(mask_t, work_t, 1.0, ALU.subtract).then_inc(s_top, 1)
            o = take()
            done(dve.tensor_copy(slot[:, :, 0:NE], o[:, 0:ST * NE].rearrange("p (t e) -> p t e", e=NE)))
            after_bank()

            def one_hot(first, gated):
                for t in range(ST):
                    for e in range(2):
                        place = slot[:, t, bass.ds(first + e, 1)]
                        at = slice(CAP * e, CAP * e + CAP)
                        if gated:
                            ins_ = ts(onehot_g[:, t, at], iota[:], place, ALU.is_equal,
                                      aff[:, t, bass.ds(first + e, 1)], ALU.mult)
                        else:
                            ins_ = ts(onehot[:, t, at], iota[:], place, ALU.is_equal)
                        if t == ST - 1 and e == 1:
                            ins_.then_inc(s_ohg if gated else s_oh, 1)

            one_hot(0, False)
            with dve.Fori(0, NE // 2) as i:
                bk.filled.enter(i, 16)
                bk.emptied.enter(i, 16)
                dve.wait_ge(s_ma, 12 * i + note["moe2_a"] + 1)
                one_hot(2 * i + 2, False)
                one_hot(2 * i, True)
                for n in range(4):
                    o = take()
                    dve.wait_ge(s_ea, 12 * i + note["moe2_a"] + n + 1)
                    done(tt(hid2[:, 0, 512 * n:512 * n + 512], o, silu2[:, 0, 512 * n:512 * n + 512], ALU.mult))
                for n in range(4):
                    o = take()
                    done(dve.tensor_copy(hid2_t[:, 4 * n:4 * n + 4, :], o.rearrange("p (k n) -> p k n", k=4)))
                for n in range(KD):
                    done(tt(y2[:, n, :], take(), y2[:, n, :], ALU.add))
                bk.filled.leave(NE // 2)
                bk.emptied.leave(NE // 2)
            after_bank()
            for n in range(KD):
                do(ts(y2[:, n, :], y2[:, n, :], modp[:, 40 + n:41 + n], ALU.mult))
                after()
                stt(region(2)[:, n, :], x[:, n, :], ALPHA, y2[:, n, :], ALU.mult, ALU.add).then_inc(s_res, 1)
            dve.wait_ge(s_res, 2 * KD)
            layer_norm(region(2), region(2))


def _constants():
    import numpy as np

    t = np.arange(S)
    f = np.arange(S)
    n = 2 * S
    ang = 2.0 * np.pi * ((t[:, None] * f[None, :]) % n) / n
    sign = 1.0 - 2.0 * (t % 2)
    fwd = np.concatenate([np.cos(ang), np.sin(ang)], 1)
    fwd[:, S] = sign
    weight = np.where(f == 0, 1.0, 2.0) / n
    inv = np.concatenate([(np.cos(ang) * weight).T, (np.sin(ang) * 2.0 / n).T], 0)
    inv[S] = sign / n
    dft = [fwd[:, 512 * a:512 * a + 512].reshape(ST, P, 512).transpose(1, 0, 2).reshape(P, UNIT) for a in range(2)]
    dft += [inv[512 * a:512 * a + 512].reshape(4, P, S).transpose(1, 0, 2).reshape(P, UNIT) for a in range(2)]
    last = np.zeros((S, P))
    last[:, 0] = 2.0 * sign
    f32 = np.float32
    t01 = t.astype(f32) / f32(S - 1)
    bands = (EMB - 1) // 2
    freq = np.linspace(1e-4, bands - 1, bands, dtype=f32)
    angle = freq[None, :] * (f32(2.0 * np.pi) * t.astype(f32) / f32(S))[:, None]
    z = np.concatenate([t01[:, None], np.cos(angle), -np.sin(angle)], -1)
    hi, lo = np.log(1e-2) / 0.3, np.log(1e-2) / 1.5
    delta = np.linspace(lo, hi, D, dtype=f32)
    window = np.exp(-t01[:, None] * np.abs(delta)[None, :])
    window = window.reshape(ST, P, 2, 512).transpose(2, 1, 0, 3).reshape(2, P, UNIT)
    quarter = D // 4
    omega = f32(1.0) / (f32(10000.0) ** (np.arange(quarter, dtype=f32) / f32(quarter)))

    def emb(p):
        a = p.astype(f32)[:, None] * omega[None, :]
        return np.concatenate([np.sin(a), np.cos(a)], -1)

    pos = np.concatenate([emb(t // 64), emb(t % 64)], -1)
    pool16 = np.stack([1.0 / np.minimum(np.arange(1, 17), w) for w in POOLW])
    lower = (np.arange(NE)[None, :] < np.arange(NE)[:, None])
    return {
        "dft": np.stack(dft), "last_row": last.reshape(ST, P, P).transpose(1, 0, 2), "zfeat": z.T,
        "window": window, "pos": pos.T.reshape(KD, P, S).transpose(1, 0, 2),
        "pool16": np.broadcast_to(pool16, (P, 4, 16)), "lower": lower[None],
    }


def _layout(a):
    import numpy as np

    def slabs(w):
        n = w.shape[1] // COLS
        return w.reshape(KD, P, n, COLS).transpose(2, 1, 0, 3).reshape(n, P, UNIT)

    def cols(v):
        v = v.reshape(-1, P)
        return v.T

    w_in = a["w_in"][0]
    m = 4 * 512
    moe1 = np.empty((NE, 3, P, UNIT), np.float32)
    for j, name in enumerate(("w_gate", "w_up")):
        moe1[:, j] = a[name][0].reshape(NE, KD, P, FE).transpose(0, 2, 1, 3).reshape(NE, P, UNIT)
    moe1[:, 2] = a["w_down"][0].reshape(NE, 2, P, D).transpose(0, 2, 1, 3).reshape(NE, P, UNIT)
    moe1 = moe1.reshape(NE // 2, 2, 3, P, UNIT)
    moe1 = np.concatenate([moe1[:, :, 0:2].reshape(NE // 2, 4, P, UNIT), moe1[:, :, 2]], 1)
    parts = {
        "mod": slabs(a["mod_w_2"][0]), "in": slabs(np.concatenate([w_in[:, :m], w_in[:, m + 8:]], 1)),
        "mix": slabs(a["w_mix_out"][0]), "xkv": slabs(a["w_xkv"][0]), "xq": slabs(a["w_xq"][0]),
        "xo": slabs(a["w_xo"][0]), "moe1": moe1.reshape(3 * NE, P, UNIT), "hyin": slabs(a["hy_w_in_2"][0]),
        "hyout": slabs(a["hy_w_out_2"][0]),
    }
    vecs = {
        "conv": a["conv_qk"][0], "head_g": a["head_norm_g"][0], "pool_scale": a["pool_scale"][0],
        "ln_mix_g": a["ln_mix_g"][0], "ln_mix_b": a["ln_mix_b"][0], "ln_x_g": a["ln_x_g"][0],
        "ln_x_b": a["ln_x_b"][0], "ln_moe_g": a["ln_moe_g"][0], "ln_moe_b": a["ln_moe_b"][0],
        "mod_b": a["mod_b_2"][0], "ln_g2": a["ln_g_2"][0], "ln_b2": a["ln_b_2"][0], "hy_b_in": a["hy_b_in_2"][0],
        "hy_conv_w": a["hy_conv_w_2"][0], "hy_conv_b": a["hy_conv_b_2"][0], "hy_f_bias": a["hy_f_bias_2"][0],
        "hy_b_out": a["hy_b_out_2"][0], "c": a["c_2"][0],
    }
    router = np.stack([a["router_w"], a["moe_router_2"][0]])
    return {
        "stream": np.concatenate([parts[name] for name, _ in STREAM]),
        "vecs": np.concatenate([cols(vecs[name]) for name, _ in VECS], 1),
        "fvecs": np.stack([a["hy_f_b1_2"][0], a["hy_f_freq_2"][0], a["hy_f_b2_2"][0, 0], a["hy_f_b2_2"][0, 1]], 1),
        "fw1": a["hy_f_w1_2"][0], "fw2": a["hy_f_w2_2"][0].transpose(1, 0, 2), "fw3": a["hy_f_w3_2"][0],
        "gbias": np.stack([a["b_i"][0], a["b_f"][0]], 1),
        "wgate": w_in[:, m:m + 8].reshape(KD, P, 8).transpose(1, 0, 2),
        "poolw": a["pool_w"][0].transpose(1, 0, 2),
        "router": router.reshape(2, KD, P, NE).transpose(2, 0, 1, 3), "rbias": a["router_bias"][None],
        "x": a["x"][0].T.reshape(KD, P, S).transpose(1, 0, 2),
        "mem": a["mem"][0].T.reshape(KD, P, MEM).transpose(1, 0, 2),
        "w1": a["moe_w1_2"][0].reshape(NE, KD, P, FF), "w3": a["moe_w3_2"][0].reshape(NE, KD, P, FF),
        "w2": a["moe_w2_2"][0].reshape(NE, KD, 2 * P, D),
    }


def kernel(**inputs):
    import numpy as np
    import concourse.bacc as bacc
    from concourse.bass_utils import run_bass_kernel_spmd

    a = {name: np.asarray(v) for name, v in inputs.items()}
    arrays = {**_layout(a), **_constants()}
    arrays = {f"in_{name}": np.ascontiguousarray(v, np.float32) for name, v in arrays.items()}
    nc = bacc.Bacc("TRN2", target_bir_lowering=False, num_devices=1)
    ins = {name[3:]: nc.dram_tensor(name, v.shape, F32, kind="ExternalInput").ap() for name, v in arrays.items()}
    ins["spectra"] = nc.dram_tensor("in_spectra", (4, P, 8, 512), F32, kind="Internal").ap()
    out = nc.dram_tensor("out", (P, KD, S), F32, kind="ExternalOutput").ap()
    build(nc, ins, out)
    r = run_bass_kernel_spmd(nc, [arrays], core_ids=[0])
    got = r.results[0]["out"]
    return got.transpose(2, 1, 0).reshape(1, S, D)
```

```python
from contextlib import ExitStack

import concourse.bass as bass
from concourse import mybir

P = 128
D = 1024
KD = D // P
S = 512
ST = S // P
MEM = 256
HEADS = 4
DH = 128
XDH = 256
NE = 16
NGRP = 4
FE = 256
FF = 2048
EPG = NE // NGRP
BLOCKS = 7
ORDER1 = [0, 1, 3, 4, 2, 6, 7, 5, 9, 10, 8, 11]
CAP = 64
POOLW = (2, 4, 8, 16)
HW = 64
EMB = 33
UNIT = 2048
COLS = UNIT // KD
RING = 12
ALPHA = 2.0 ** 0.25
LN_EPS = 1e-5
MOD_EPS = 1e-6
NEG = -1.0e30

F32 = mybir.dt.float32
ALU = mybir.AluOpType
ACT = mybir.ActivationFunctionType
AX = mybir.AxisListType.X

STREAM = [("in", 10), ("mix", 4), ("xkv", 8), ("xq", 4), ("xo", 4), ("mod", 24), ("hyin", 12), ("hyout", 4)]
BASE = {}
_n = 0
for _name, _units in STREAM:
    BASE[_name] = _n
    _n += _units
UNITS = _n

VECS = [("conv", 32), ("head_g", 4), ("pool_scale", 4), ("ln_mix_g", 8), ("ln_mix_b", 8), ("ln_x_g", 8),
        ("ln_x_b", 8), ("ln_moe_g", 8), ("ln_moe_b", 8), ("mod_b", 48), ("ln_g2", 16), ("ln_b2", 16),
        ("hy_b_in", 24), ("hy_conv_w", 72), ("hy_conv_b", 24), ("hy_f_bias", 16), ("hy_b_out", 8), ("c", 8)]
VAT = {}
_n = 0
for _name, _units in VECS:
    VAT[_name] = _n
    _n += _units
NVEC = _n

TWO_PI = 6.283185307179586
PI_HI = 6.28125
PI_LO = TWO_PI - PI_HI
ROUND = 12582912.0
PI_IN = 3.1415925


class Count:

    def __init__(self, sem):
        self.sem, self.n, self.i, self.per, self.first = sem, 0, None, 0, 0

    def at(self, more=0):
        v = self.n + more
        return v if self.i is None else v + self.i * self.per

    def inc(self, ins, by=1):
        ins.then_inc(self.sem, by)
        self.n += by

    def enter(self, i, per):
        self.i, self.per, self.first = i, per, self.n

    def leave(self, rounds):
        assert self.n - self.first == self.per, (self.n - self.first, self.per)
        self.n, self.i = self.first + self.per * rounds, None


class Banks:

    def __init__(self, psum, banks, filled, emptied):
        self.psum, self.banks = psum, banks
        self.filled, self.emptied = Count(filled), Count(emptied)

    def bank(self, more=0):
        return self.psum[:, self.banks[(self.filled.n + more) % len(self.banks)], :]


def build(nc, ins, out):
    with ExitStack() as ctx:
        def sb(name, shape):
            return ctx.enter_context(nc.sbuf_tensor(name, shape, F32))

        def sem(name):
            return ctx.enter_context(nc.semaphore(name))

        ring = sb("ring", [P, RING, UNIT])
        arena = sb("arena", [P, 6, KD * S])
        psum = ctx.enter_context(nc.psum_tensor("psum", [P, 8, 512], F32))

        ones = sb("ones", [P, P])
        mean_w = sb("mean_w", [P, P])
        ident = sb("ident", [P, P])
        iota = sb("iota", [P, CAP])
        vec = sb("vec", [P, NVEC])
        fvec = sb("fvec", [HW, 4])
        fw1 = sb("fw1", [EMB, HW])
        fw2 = sb("fw2", [HW, 2, HW])
        gbias = sb("gbias", [HEADS, 2])
        wgate = sb("wgate", [P, KD, 8])
        pool16 = sb("pool16", [P, 4, 16])
        router = sb("router", [P, 2, KD, NE])
        rbias = sb("rbias", [P, NE])
        lower = sb("lower", [P, NE, NE])
        csil = sb("csil", [P, KD, 32])
        tri4 = sb("tri4", [NGRP, NGRP])
        gcol = sb("gcol", [NGRP, 8 + BLOCKS + 1])
        block_group = ctx.enter_context(nc.sbuf_tensor("block_group", [1, 8], mybir.dt.int32))
        slot1 = sb("slot1", [P, ST])
        gate_loc = sb("gate_loc", [P, ST, EPG])
        gate_blk = sb("gate_blk", [P, 8, EPG])
        modc = sb("modc", [P, 48])
        modp = sb("modp", [P, 48])
        modg = sb("modg", [P, 8])
        filt_rn = sb("filt_rn", [P, 16])
        acol = sb("acol", [P, ST, HEADS])
        tiny = sb("tiny", [P, 4, 8])
        route = sb("route", [P, 6, ST * NE])
        gates = sb("gates", [P, ST, NE])
        slot = sb("slot", [P, ST, NE + 2])
        aff = sb("aff", [P, ST, NE + 2])
        epsv = sb("epsv", [P, 1])

        def vcol(name, j):
            return vec[:, VAT[name] + j:VAT[name] + j + 1]

        def region(r, at=0, tiles=KD, width=S):
            return arena[:, r, at:at + tiles * width].rearrange("p (k n) -> p k n", k=tiles)

        dft_f = region(0).rearrange("p (a k) n -> p a k n", a=2)
        h_fwd, h_bwd = region(1, 0, ST), region(1, 2048, ST)
        h_even, h_odd = region(2, 0, ST), region(2, 2048, ST)
        k_out = region(3)
        abs_sum = region(4, 0, ST)
        mlp = region(4, 2048, 4)
        abs_tmp = region(4, 3072, 1)[:, 0, :]
        fw3 = arena[0:HW, 5, :]
        x = region(0)
        qk = region(1)
        conv = region(2)
        v_tok, o_gate = region(3, 0, ST), region(3, 2048, ST)
        u_pad = arena[:, 4, 0:528]
        pool_a = arena[:, 4, 528:1056]
        pool_b = arena[:, 4, 1056:1584]
        rows = [arena[0:HEADS, 4, 1584 + 512 * n:2096 + 512 * n] for n in range(4)]
        mixed = region(5)
        decay = region(2, 0, ST)
        hn = region(2, 2048, 4)
        mem_t, k_x = region(3, 0, KD, MEM), region(3, 2048, KD, MEM)
        v_x = region(4, 0, 2, D)
        p_exp = region(4, 2048, 4, MEM)
        p_t = region(4, 3072, 2)
        q_x, o_x = region(5), region(1)
        x_tok = region(1, 0, ST, D)
        place = region(2, 0, ST, D)
        place_t = region(5, 0, BLOCKS + 1, S)
        g_rows = [arena[0:NGRP, 5, 512 * n:512 * n + 512] for n in range(3)]
        y1 = region(3)
        iota_d = arena[:, 4, 0:D]
        silu1 = region(4, 0, 2, FE)
        hid = region(4, 512, 2, FE)
        x_blk = region(4, 1024, KD, P)
        y_blk = arena[:, 4, 2048:3072]
        mod_row = region(4, 3072, 2, COLS)
        hid_t = region(4, 3584, 4, P)
        pos = region(5)
        h2 = region(4)
        u_hy = [region(1), region(2), region(3)]
        z_tok = region(4, 0, ST, D)
        spec = region(5)
        h_tok = region(5, 0, ST, D)
        y2 = region(1)
        x_sel = region(2, 0, 1, D)
        x_sel_t = region(2, 1024, KD, P)
        y_sel = region(2, 2048, 1, D)
        onehot = region(2, 3072, ST, P)
        onehot_g = region(2, 3584, ST, P)
        hid2, silu2 = region(3, 0, 1, FF), region(3, 2048, 1, FF)
        hid2_t = region(4, 0, FF // P, P)
        scat = arena[:, 4, 2048:2560]
        aff_t = arena[0:NE, 4, 2560:3072]
        work_t = arena[0:NE, 4, 3072:3584]
        mask_t = arena[0:NE, 4, 3584:4096]
        hpad = arena[:, 5, 0:2 * (S + 2)].rearrange("p (b n) -> p b n", b=2)
        scratch = sb("scratch", [P, 2, S])
        last_row = scratch[:, 0, :].rearrange("p (k n) -> p k n", k=ST)
        poolw = scratch[:, 1, :].rearrange("p (k n) -> p k n", k=4)
        ln_r = ptmp = scratch
        top8 = sb("top8", [NE, 8])
        in_group4 = route[:, 2, 16:32]

        s_arrived = [sem(f"arrived{r}") for r in range(RING)]
        s_used = sem("units_used")
        s_ma, s_ea = sem("act_filled"), sem("act_emptied")
        s_md, s_ed = sem("dve_filled"), sem("dve_emptied")
        s_const = sem("pool_consts")
        s_vec = sem("vectors_in")
        s_cf = sem("dft_in")
        s_step = sem("dve_step")
        s_astep = sem("act_step")
        s_mlp = sem("mlp_arg")
        s_sin = sem("mlp_sine")
        s_hw = sem("taps_windowed")
        s_eo = sem("taps_even_odd")
        s_kst = sem("filter_stored")
        s_kout = sem("filter_copied")
        s_abs = sem("taps_abs_sum")
        s_csil = sem("c_silu")
        s_mrow = sem("mod_row_read")
        s_mm = sem("mod_columns")
        s_mread = sem("mod_columns_read")
        s_x = sem("x_in")
        s_gb = sem("gate_rows")
        s_gl = sem("gate_ln")
        s_conv = sem("conv_done")
        s_qk = sem("qk_ready")
        s_upad = sem("pool_input")
        s_pool = sem("pool_done")
        s_row = sem("rows_ready")
        s_exp = sem("decay_exp")
        s_tri = sem("decay_masked")
        s_rv = sem("inverse_var")
        s_rstd = sem("rstd")
        s_hn = sem("head_square")
        s_ho = sem("head_out")
        s_den = sem("den_abs")
        s_res = sem("residual_sum")
        s_lnc = sem("ln_centred")
        s_lnq = sem("ln_square")
        s_lnm = sem("ln_scaled")
        s_lno = sem("ln_out")
        s_mem = sem("mem_in")
        s_xs = sem("scores_shifted")
        s_xe = sem("scores_exp")
        s_xp = sem("probs_ready")
        s_pread = sem("probs_read")
        s_em = sem("den_floor")
        s_ohg = sem("gated_onehots")
        s_aff = sem("affinities")
        s_r0 = sem("logits_shifted")
        s_r1 = sem("logits_exp")
        s_gt = sem("group_masks")
        s_blk = sem("block_groups")
        s_start = sem("group_blocks")
        s_sm = sem("place_rows")
        s_pl = sem("places")
        s_iota = sem("iota_ready")
        s_slot = sem("place_columns")
        s_si1 = sem("silu1")
        s_hid = sem("hidden1")
        s_mt, s_et = sem("blk_filled"), sem("blk_emptied")
        s_my, s_ey = sem("out_filled"), sem("out_emptied")
        s_pos = sem("pos_in")
        s_px = sem("pos_added")
        s_hz = sem("hy_pad_zero")
        s_uc = sem("hy_conv")
        s_zt = sem("z_tok_ready")
        s_k = sem("spectrum_product")
        s_z1 = sem("z_next")
        s_ys = sem("hy_out_scaled")
        s_top = sem("top_ready")
        s_oh = sem("onehots")
        s_si2 = sem("silu2")
        s_hid2 = sem("hidden2")
        s_y0 = sem("y2_zero")
        s_g2 = sem("moe2_groups_a")
        s_out = sem("out_stored")

        note = {}

        block = ctx.enter_context(nc.Block())

        @block.sync
        def _(sp):
            used = Count(s_used)
            turn = [0]

            def load(src, dst_shape=None):
                slot_ = turn[0] % RING
                if used.i is not None or turn[0] >= RING:
                    sp.wait_ge(s_used, used.at(1 - RING))
                dst = ring[:, slot_, :]
                if dst_shape is not None:
                    dst = dst_shape(dst)
                sp.dma_start(dst, src).then_inc(s_arrived[slot_], 16)
                used.n += 1
                turn[0] += 1

            small = [(vec[:], ins["vecs"]), (fvec[:], ins["fvecs"]), (fw1[:], ins["fw1"]), (fw2[:], ins["fw2"]),
                     (mlp[0:EMB, 3, :], ins["zfeat"]), (gbias[:], ins["gbias"]), (wgate[:], ins["wgate"]),
                     (poolw, ins["poolw"]), (pool16[:], ins["pool16"]), (last_row, ins["last_row"]),
                     (router[:], ins["router"]), (rbias[:], ins["rbias"].broadcast_to([P, NE])),
                     (tri4[:], ins["tri4"]), (lower[:], ins["lower"].broadcast_to([P, NE, NE])), (fw3, ins["fw3"])]
            for dst, src in small:
                sp.dma_start(dst, src).then_inc(s_vec, 16)
            sp.dma_start(dft_f, ins["dft"][0:2].rearrange("a p (k n) -> p a k n", k=ST)).then_inc(s_cf, 16)
            for half in range(2):
                load(ins["window"][half])
            sp.wait_ge(s_ma, 8 * 4)
            sp.dma_start(x, ins["x"]).then_inc(s_x, 16)
            for u in range(14):
                load(ins["stream"][BASE["in"] + u])
            sp.wait_ge(s_ho, HEADS)
            sp.dma_start(mem_t, ins["mem"]).then_inc(s_mem, 16)
            for u in range(16 + 24):
                load(ins["stream"][BASE["xkv"] + u])
            sp.wait_ge(s_blk, 1)
            with sp.Fori(0, BLOCKS) as i:
                used.enter(i, RING)
                group = sp.value_load(block_group[0:1, bass.ds(i, 1)], min_val=0, max_val=NGRP - 1)
                for j in ORDER1:
                    load(ins["moe1"][group, j])
                used.leave(BLOCKS)
            turn[0] += RING * (BLOCKS - 1)
            for u in range(12):
                load(ins["stream"][BASE["hyin"] + u])
            sp.wait_ge(s_lnc, 2 * KD + 1)
            sp.dma_start(pos, ins["pos"]).then_inc(s_pos, 16)
            for order in range(2):
                for half in range(2):
                    load(ins["dft"][0])
                    load(ins["dft"][1])
                    if order == 0 and half == 0:
                        sp.wait_ge(s_kst, 16 * 4)
                    c = 2 * half + order
                    load(ins["spectra"][c, :, 0:4, :], lambda d: d.rearrange("p (k n) -> p k n", k=4))
                    load(ins["spectra"][c, :, 4:8, :], lambda d: d.rearrange("p (k n) -> p k n", k=4))
                    load(ins["dft"][2])
                    load(ins["dft"][3])
            for u in range(4):
                load(ins["stream"][BASE["hyout"] + u])
            with sp.Fori(0, NE // 2) as i:
                used.enter(i, 48)
                for name in ("w1", "w3"):
                    for k in range(KD):
                        for e in range(2):
                            load(ins[name][2 * i + e, k])
                for k in range(KD):
                    for e in range(2):
                        load(ins["w2"][2 * i + e, k].rearrange("(a p) n -> p a n", a=2),
                             lambda d: d.rearrange("p (a n) -> p a n", a=2))
                used.leave(NE // 2)
            sp.wait_ge(s_lno, 8 * 7)
            sp.dma_start(out, x).then_inc(s_out, 16)
            sp.wait_ge(s_out, 16)

        @block.gpsimd
        def _(pool):
            pool.memset(ones[:], 1.0).then_inc(s_const, 1)
            pool.memset(mean_w[:], 1.0 / D).then_inc(s_const, 1)
            pool.memset(ident[:], 0.0).then_inc(s_const, 1)
            pool.memset(csil[:], 0.0).then_inc(s_const, 1)
            pool.memset(slot[:], -1.0).then_inc(s_const, 1)
            pool.memset(aff[:], 0.0).then_inc(s_const, 1)
            pool.memset(epsv[:], 0.0).then_inc(s_const, 1)
            pool.wait_ge(s_const, 7)
            pool.affine_select(out=ident[:], in_=ident[:], compare_op=ALU.not_equal, fill=1.0, base=0,
                               pattern=[[-1, P]], channel_multiplier=1).then_inc(s_const, 1)
            pool.iota(iota[:], pattern=[[1, CAP]], base=0, channel_multiplier=0,
                      allow_small_or_imprecise_dtypes=True).then_inc(s_const, 1)
            for h in range(HEADS):
                for j in range(ST):
                    pool.wait_ge(s_exp, ST * h + j + 1)
                    blk = decay[:, j, P * j:P * j + P]
                    pool.affine_select(out=blk, in_=blk, compare_op=ALU.is_ge, fill=0.0, base=0,
                                       pattern=[[1, P]], channel_multiplier=-1).then_inc(s_tri, 1)
            pool.wait_ge(s_lnc, KD + 1)
            pool.iota(iota_d, pattern=[[1, D]], base=0, channel_multiplier=0,
                      allow_small_or_imprecise_dtypes=True).then_inc(s_iota, 1)

        @block.tensor
        def _(pe):
            bk_a = Banks(psum, [0, 1, 2, 3], s_ma, s_ea)
            bk_d = Banks(psum, [4, 5, 6, 7], s_md, s_ed)
            unit_no = Count(s_used)
            turn = [0]
            owed = []
            keep = [0]

            def begin(b):
                if b.filled.i is not None or b.filled.n >= len(b.banks):
                    pe.wait_ge(b.emptied.sem, b.filled.at(1 - len(b.banks)))
                return b.bank()

            def mm(o, lhs, rhs, start, stop, ends=None, tr=False):
                if tr:
                    ins_ = pe.transpose(o, lhs, rhs)
                else:
                    ins_ = pe.matmul(o, lhs, rhs, start=start, stop=stop)
                if ends is not None:
                    ends.filled.inc(ins_)
                elif len(owed) > keep[0]:
                    ins_.then_inc(owed.pop(0), 1)
                return ins_

            def read(b, ago=0):
                pe.wait_ge(b.emptied.sem, b.filled.at(-ago))

            def unit():
                slot_ = turn[0] % RING
                turns = turn[0] // RING + 1
                v = 16 * turns if unit_no.i is None else unit_no.i * (16 * unit_no.per // RING) + 16 * turns
                pe.wait_ge(s_arrived[slot_], v)
                turn[0] += 1
                unit_no.n += 1
                return ring[:, slot_, :]

            def used():
                owed.append(s_used)

            def enter(i, rounds, per_units, per_a, per_d):
                unit_no.enter(i, per_units)
                bk_a.filled.enter(i, per_a)
                bk_d.filled.enter(i, per_d)
                return turn[0], rounds

            def leave(entry):
                t0, rounds = entry
                for c_ in (unit_no, bk_a.filled, bk_d.filled):
                    c_.leave(rounds)
                turn[0] = t0 + unit_no.per * rounds

            def project(units, rhs, b, n=S):
                for _u in range(units):
                    w = unit()
                    for j in range(COLS // P):
                        o = begin(b)
                        for k in range(KD):
                            mm(o[:, 0:n], w[:, COLS * k + P * j:COLS * k + P * j + P], rhs[:, k, :],
                               k == 0, k == KD - 1, b if k == KD - 1 else None)
                    used()

            def project_tok(units, lhs, tiles, b):
                for _u in range(units):
                    w = unit()
                    for t in range(tiles):
                        o = begin(b)
                        for k in range(KD):
                            mm(o[:, 0:COLS], lhs[:, k, P * t:P * t + P], w[:, COLS * k:COLS * k + COLS],
                               k == 0, k == KD - 1, b if k == KD - 1 else None)
                    used()

            def to_tokens(src):
                for t in range(ST):
                    for half in range(2):
                        o = begin(bk_a)
                        for n in range(4):
                            mm(o[:, P * n:P * n + P], src[:, 4 * half + n, P * t:P * t + P], ident[:], True, True,
                               bk_a if n == 3 else None, tr=True)

            ln_no = [0]

            def summed(k):
                pe.wait_ge(s_ed, bk_d.filled.n - KD + k + 1)

            def layer_norm(src, sq, ready, tail=lambda: None):
                o = begin(bk_d)
                for k in range(KD):
                    ready(k)
                    mm(o, mean_w[:], src[:, k, :], k == 0, k == KD - 1, bk_d if k == KD - 1 else None)
                tail()
                o = begin(bk_d)
                for k in range(KD):
                    pe.wait_ge(s_lnq, KD * ln_no[0] + k + 1)
                    mm(o, mean_w[:], sq[:, k, :], k == 0, k == KD - 1, bk_d if k == KD - 1 else None)
                ln_no[0] += 1

            pe.wait_ge(s_const, 9)
            pe.wait_ge(s_vec, 16 * 15)
            for n in range(3):
                o = begin(bk_d)
                if n == 0:
                    mm(o[0:HW, :], fw1[:], mlp[0:EMB, 3, :], True, True, bk_d)
                else:
                    pe.wait_ge(s_sin, n)
                    mm(o[0:HW, :], fw2[:, n - 1, :], mlp[0:HW, 0, :], True, True, bk_d)
            pe.wait_ge(s_sin, 3)
            pe.wait_ge(s_cf, 16)
            for c in range(4):
                half, order = c // 2, c % 2
                if order == 0:
                    unit()
                for dirn in range(2):
                    for t in range(ST):
                        o = begin(bk_d)
                        at = 2 * D * dirn + D * order + 512 * half
                        mm(o, mlp[0:HW, 0, P * t:P * t + P], fw3[:, at:at + 512], True, True, bk_d)
                pe.wait_ge(s_eo, 2 * c + 2)
                if order == 1:
                    used()
                for r in range(8):
                    o = begin(bk_a)
                    part = h_even if r < 4 else h_odd
                    for k in range(ST):
                        last = r != 4 and k == ST - 1
                        mm(o, dft_f[:, r // 4, k, P * (r % 4):P * (r % 4) + P], part[:, k, :],
                           k == 0, last, bk_a if last else None)
                    if r == 4:
                        for k in range(ST):
                            mm(o, last_row[:, k, :], h_bwd[:, k, :], False, k == ST - 1,
                               bk_a if k == ST - 1 else None)
            o = begin(bk_d)
            pe.wait_ge(s_abs, 4)
            for c in range(4):
                half, order = c // 2, c % 2
                for n in range(4):
                    col = 8 * order + 4 * half + n
                    mm(o[:, col:col + 1], abs_sum[:, c, P * n:P * n + P], ones[:, 0:1], True, True,
                       bk_d if c == 3 and n == 3 else None)

            def modulation(first, last):
                for u in range(first, last + (last == 24)):
                    if u < 24:
                        w = unit()
                        o = begin(bk_a)
                        for r in range(2):
                            for g in range(4):
                                k = 4 * r + g
                                mm(o[32 * g:32 * g + 32, 0:COLS], csil[:, k, :], w[:, COLS * k:COLS * k + COLS],
                                   r == 0, r == 1, bk_a if k == 7 else None)
                        note["mod", u] = bk_a.filled.n
                        used()
                    if u > 0:
                        pe.wait_ge(s_ea, note["mod", u - 1])
                        for j in range(2):
                            col = 2 * (u - 1) + j
                            mm(mod_bank[:, col:col + 1], mod_row[:, (u - 1) % 2, P * j:P * j + P], ones[:, 0:1],
                               True, True, bk_m if col == 47 else None)
                        if u < 24:
                            owed.append(s_mrow)

            pe.wait_ge(s_x, 16)
            for g in range(2):
                o = begin(bk_d)
                for k in range(KD):
                    mm(o[0:HEADS, :], wgate[:, k, 4 * g:4 * g + 4], x[:, k, :], k == 0, k == KD - 1,
                       bk_d if k == KD - 1 else None)
            note["qk"] = bk_d.filled.n
            project(4, x, bk_d)
            project_tok(2, x, ST, bk_a)
            project(2, x, bk_a)
            note["u"] = bk_a.filled.n
            project(2, x, bk_a)
            for g in range(4):
                o = begin(bk_a)
                pe.wait_ge(s_pool, g + 1)
                mm(o, poolw[:, g, :], mixed[:, g, :], True, True, bk_a)
            o = begin(bk_a)
            pe.wait_ge(s_row, 1)
            for t in range(ST):
                mm(o[:, HEADS * t:HEADS * t + HEADS], rows[0][:, P * t:P * t + P], ident[0:HEADS, 0:HEADS],
                   True, True, bk_a if t == ST - 1 else None, tr=True)
            pe.wait_ge(s_row, 2)
            pe.wait_ge(s_em, 1)
            for h in range(HEADS):
                pick = ident[0:HEADS, h:h + 1].broadcast_to([HEADS, P])
                o = begin(bk_a)
                mm(o, pick, rows[2], True, True, bk_a)
                pe.wait_ge(s_qk, KD)
                for j in range(ST):
                    o = begin(bk_d)
                    mm(o[:, P * j:S], qk[:, 4 + h, P * j:P * j + P], qk[:, h, P * j:S], True, True, bk_d)
                den = begin(bk_a)
                note["den", h] = bk_a.filled.n
                e_bc = begin(bk_d)
                mm(e_bc, pick, rows[3], True, True, bk_d)
                read(bk_d, 1)
                for j in range(ST):
                    mm(den[:, P * j:S], ones[:], decay[:, j, P * j:S], j == 0, j == ST - 1,
                       bk_a if j == ST - 1 else None)
                num = begin(bk_d)
                for j in range(ST):
                    mm(num[:, P * j:S], v_tok[:, j, P * h:P * h + P], decay[:, j, P * j:S], j == 0,
                       j == ST - 1, bk_d if j == ST - 1 else None)
                read(bk_d)
                o = begin(bk_d)
                mm(o, ones[:], hn[:, 0, :], True, True, bk_d)
                o = begin(bk_d)
                pe.wait_ge(s_hn, h + 1)
                mm(o, ones[:], hn[:, 1, :], True, True, bk_d)
            pe.wait_ge(s_ho, HEADS)
            project(4, mixed, bk_d)

            def keys_values():
                pe.wait_ge(s_mem, 16)
                project(4, mem_t, bk_a, MEM)
                project_tok(4, mem_t, 2, bk_a)

            layer_norm(region(1), region(2), summed, keys_values)
            pe.wait_ge(s_lno, KD)
            project(4, x, bk_a)
            read(bk_a)
            note["scores"] = bk_d.filled.n
            for h in range(HEADS):
                for t in range(ST):
                    o = begin(bk_d)
                    for i in range(2):
                        mm(o[:, 0:MEM], q_x[:, 2 * h + i, P * t:P * t + P], k_x[:, 2 * h + i, :],
                           i == 0, i == 1, bk_d if i == 1 else None)
                pe.wait_ge(s_xp, ST * (h + 1))
                for m in range(2):
                    o = begin(bk_a)
                    for t in range(ST):
                        mm(o[:, P * t:P * t + P], p_exp[:, t, P * m:P * m + P], ident[:], True, True,
                           bk_a if t == ST - 1 else None, tr=True)
                owed.append(s_pread)
                read(bk_a)
                for i in range(2):
                    o = begin(bk_a)
                    for m in range(2):
                        mm(o, v_x[:, m, P * (2 * h + i):P * (2 * h + i) + P], p_t[:, m, :], m == 0, m == 1,
                           bk_a if m == 1 else None)
            read(bk_a)
            project(4, o_x, bk_d)
            layer_norm(region(2), region(3), summed)
            pe.wait_ge(s_lno, 2 * KD)
            pe.wait_ge(s_csil, 1)
            note["router"] = bk_a.filled.n
            o = begin(bk_a)
            for t in range(ST):
                for k in range(KD):
                    mm(o[:, NE * t:NE * t + NE], x[:, k, P * t:P * t + P], router[:, 0, k, :], k == 0,
                       k == KD - 1, bk_a if t == ST - 1 and k == KD - 1 else None)
            to_tokens(x)
            bk_m = Banks(psum, [7], s_mm, None)
            mod_bank = bk_m.bank()
            bk_a.banks = [0, 1, 2, 3]
            read(bk_d)
            modulation(0, 12)
            o = begin(bk_a)
            pe.wait_ge(s_gt, 1)
            for t in range(ST):
                mm(o[0:NGRP, P * t:P * t + P], in_group4[:, 4 * t:4 * t + 4], ident[:], True, True,
                   bk_a if t == ST - 1 else None, tr=True)
            modulation(12, 16)
            o = begin(bk_a)
            pe.wait_ge(s_start, 1)
            mm(o[0:NGRP, 0:1], tri4[:], gcol[:, 0:1], True, True, bk_a)
            note["start"] = bk_a.filled.n
            modulation(16, 20)
            o = begin(bk_a)
            pe.wait_ge(s_sm, 2)
            for t in range(ST):
                mm(o[:, t:t + 1], g_rows[2][:, P * t:P * t + P], ones[0:NGRP, 0:1], True, True)
            mm(o[0:1, 8:16], ones[0:NGRP, 0:1], gcol[:, 8:16], True, True, bk_a)
            note["places"] = bk_a.filled.n
            modulation(20, 24)
            pe.wait_ge(s_pl, ST)
            o = begin(bk_a)
            for b in range(BLOCKS):
                for t in range(ST):
                    mm(o[:, EPG * b:EPG * b + EPG], place[:, t, P * b:P * b + P], gate_loc[:, t, :], t == 0,
                       t == ST - 1, bk_a if t == ST - 1 and b == BLOCKS - 1 else None)
            for b in range(BLOCKS):
                o = begin(bk_a)
                for t in range(ST):
                    mm(o[:, P * t:P * t + P], place[:, t, P * b:P * b + P], ident[:], True, True,
                       bk_a if t == ST - 1 else None, tr=True)
            read(bk_a)
            bk_t = Banks(psum, [0, 1], s_mt, s_et)
            bk_y = Banks(psum, [2, 3], s_my, s_ey)

            def gather_block(b):
                for n in range(2):
                    o = begin(bk_t)
                    for j in range(4):
                        for t in range(ST):
                            mm(o[:, P * j:P * j + P], x_tok[:, t, 512 * n + P * j:512 * n + P * j + P],
                               place[:, t, bass.ds(P * b, P)], t == 0, t == ST - 1,
                               bk_t if j == 3 and t == ST - 1 else None)

            gather_block(0)
            pe.wait_ge(s_mread, 1)
            assert not owed
            note["moe1_a"], note["moe1_d"] = bk_a.filled.n, bk_d.filled.n
            with pe.Fori(0, BLOCKS) as i:
                entry = enter(i, BLOCKS, RING, 0, 12)
                bk_t.filled.enter(i, 6)
                bk_y.filled.enter(i, 2)
                o_y = [bk_y.bank(n) for n in range(2)]

                def up(e):
                    o = begin(bk_d)
                    for k in range(KD):
                        if k % 4 == 0:
                            w = unit()
                        mm(o, x_blk[:, k, :], w[:, 512 * (k % 4):512 * (k % 4) + 512], k == 0, k == KD - 1,
                           bk_d if k == KD - 1 else None)
                        if k % 4 == 3:
                            used()

                def turned(e):
                    o = begin(bk_t)
                    pe.wait_ge(s_hid, EPG * i + e + 1)
                    for j in range(2):
                        mm(o[:, P * j:P * j + P], hid[:, e % 2, P * j:P * j + P], ident[:], True, True,
                           bk_t if j == 1 else None, tr=True)

                def down(e):
                    w = unit()
                    pe.wait_ge(s_et, bk_t.filled.at())
                    for j in range(2):
                        for n in range(2):
                            last = e == EPG - 1 and j == 1
                            mm(o_y[n], hid_t[:, 2 * (e % 2) + j, :], w[:, D * j + 512 * n:D * j + 512 * n + 512],
                               e == 0 and j == 0, last, bk_y if last else None)
                    used()

                pe.wait_ge(s_et, bk_t.filled.at())
                up(0)
                up(1)
                turned(0)
                down(0)
                up(2)
                turned(1)
                down(1)
                up(3)
                turned(2)
                down(2)
                turned(3)
                down(3)
                gather_block(i + 1)
                pe.wait_ge(s_ey, bk_y.filled.at())
                for n in range(KD):
                    o = begin(bk_d)
                    mm(o, y_blk[:, P * n:P * n + P], place_t[:, i, :], True, True, bk_d)
                assert not owed
                bk_t.filled.leave(BLOCKS)
                bk_y.filled.leave(BLOCKS)
                leave(entry)
            pe.wait_ge(s_et, bk_t.filled.n)
            layer_norm(region(3), region(1), summed)
            layer_norm(x, region(2), lambda k: pe.wait_ge(s_px, k + 1))
            pe.wait_ge(s_lno, 4 * KD)
            note["u_hy"] = bk_a.filled.n
            project(12, h2, bk_a)

            for order in range(2):
                pe.wait_ge(s_uc, 3 * KD)
                if order:
                    pe.wait_ge(s_z1, KD)
                to_tokens(u_hy[0])
                read(bk_a)
                for half in range(2):
                    cos_f, sin_f = [unit().rearrange("p (k n) -> p k n", k=ST) for _ in range(2)]
                    note["k", order, half] = [(turn[0] % RING, 16 * (turn[0] // RING + 1)),
                                              ((turn[0] + 1) % RING, 16 * ((turn[0] + 1) // RING + 1))]
                    for r in range(4):
                        for f in (cos_f, sin_f):
                            o = begin(bk_d)
                            for k in range(ST):
                                mm(o, f[:, k, P * r:P * r + P], z_tok[:, k, 512 * half:512 * half + 512],
                                   k == 0, k == ST - 1, bk_d if k == ST - 1 else None)
                    used()
                    used()
                    unit()
                    unit()
                    pe.wait_ge(s_k, 4 * (2 * order + half + 1))
                    used()
                    used()
                    inv = [unit().rearrange("p (k n) -> p k n", k=4) for _ in range(2)]
                    for n in range(4):
                        o = begin(bk_d)
                        for r in range(8):
                            mm(o, spec[:, r, P * n:P * n + P], inv[r // 4][:, r % 4, :], r == 0, r == 7,
                               bk_d if r == 7 else None)
                    used()
                    used()
            pe.wait_ge(s_z1, 2 * KD)
            note["hyout"] = bk_a.filled.n
            keep[0] = 2
            project(4, u_hy[0], bk_a)
            layer_norm(region(2), region(3), lambda k: pe.wait_ge(s_res, k + 1))
            layer_norm(x, region(3), lambda k: pe.wait_ge(s_lno, 4 * KD + k + 1))
            pe.wait_ge(s_lno, 6 * KD)
            o = begin(bk_d)
            for t in range(ST):
                for k in range(KD):
                    mm(o[:, NE * t:NE * t + NE], h2[:, k, P * t:P * t + P], router[:, 1, k, :], k == 0,
                       k == KD - 1, bk_d if t == ST - 1 and k == KD - 1 else None)
            to_tokens(h2)
            o = begin(bk_a)
            pe.wait_ge(s_aff, 1)
            for t in range(ST):
                mm(o[0:NE, P * t:P * t + P], aff[:, t, 0:NE], ident[:], True, True,
                   bk_a if t == ST - 1 else None, tr=True)
            note["aff_t"] = bk_a.filled.n
            o = begin(bk_d)
            pe.wait_ge(s_top, 1)
            for t in range(ST):
                mm(o[:, NE * t:NE * t + NE], mask_t[:, P * t:P * t + P], ident[0:NE, 0:NE], True, True,
                   bk_d if t == ST - 1 else None, tr=True)

            def gather():
                for n in range(2):
                    o = begin(bk_a)
                    for t in range(ST):
                        mm(o, onehot[:, t, :], h_tok[:, t, 512 * n:512 * n + 512], t == 0, t == ST - 1,
                           bk_a if t == ST - 1 else None)
                for n in range(2):
                    read(bk_a, 1)
                    o = begin(bk_a)
                    for j in range(4):
                        mm(o[:, P * j:P * j + P], x_sel[:, 0, 512 * n + P * j:512 * n + P * j + P], ident[:],
                           True, True, bk_a if j == 3 else None, tr=True)

            pe.wait_ge(s_oh, 1)
            gather()
            assert len(owed) == 2
            keep[0] = 0
            note["moe2_a"], note["moe2_d"] = bk_a.filled.n, bk_d.filled.n
            with pe.Fori(0, NE // 2) as i:
                entry = enter(i, NE // 2, 48, 12, 16)
                read(bk_a)
                for b in (bk_a, bk_d):
                    if b is bk_d:
                        read(bk_d)
                    o = [b.bank(n) for n in range(4)]
                    for k in range(KD):
                        w = [unit(), unit()]
                        for n in range(4):
                            for e in range(2):
                                mm(o[n][CAP * e:CAP * e + CAP, :], x_sel_t[:, k, CAP * e:CAP * e + CAP],
                                   w[e][:, 512 * n:512 * n + 512], k == 0, k == KD - 1,
                                   b if k == KD - 1 and e == 1 else None)
                        used()
                        used()
                pe.wait_ge(s_oh, i + 2)
                gather()
                for n in range(4):
                    o = begin(bk_d)
                    for j in range(4):
                        f = 4 * n + j
                        mm(o[:, P * j:P * j + P], hid2[:, 0, P * f:P * f + P], ident[:], True, True,
                           bk_d if j == 3 else None, tr=True)
                pe.wait_ge(s_ohg, i + 1)
                for n in range(2):
                    o = begin(bk_a)
                    for j in range(2):
                        mm(o[:, P * j:P * j + P], onehot_g[:, 2 * n + j, :], ident[:], True, True,
                           bk_a if j == 1 else None, tr=True)
                read(bk_d)
                begin(bk_a)
                pe.wait_ge(s_ea, bk_a.filled.at(-2))
                o = [bk_a.bank(n) for n in range(2)]
                for k in range(KD):
                    w = [unit(), unit()]
                    for a in range(2):
                        for n in range(2):
                            for e in range(2):
                                mm(o[n][CAP * e:CAP * e + CAP, :], hid2_t[:, 2 * k + a, CAP * e:CAP * e + CAP],
                                   w[e][:, D * a + 512 * n:D * a + 512 * n + 512], k == 0 and a == 0,
                                   k == KD - 1 and a == 1, bk_a if k == KD - 1 and a == 1 and e == 1 else None)
                    used()
                    used()
                read(bk_a)
                for n in range(KD):
                    o = begin(bk_d)
                    mm(o, y_sel[:, 0, P * n:P * n + P], scat, True, True, bk_d)
                assert len(owed) == 2
                leave(entry)
            layer_norm(region(2), region(3), lambda k: pe.wait_ge(s_res, KD + k + 1))

        @block.scalar
        def _(act):
            bk = Banks(psum, [0, 1, 2, 3], s_ma, s_ea)
            step = Count(s_astep)
            inv_var = [0]
            ln_no = [0]

            def take():
                act.wait_ge(s_ma, bk.filled.at(1))
                o = bk.bank()
                bk.filled.n += 1
                return o

            def empty(o, dst, func=ACT.Identity, **more):
                bk.emptied.inc(act.activation(dst, o, func, **more))

            def let_go(o):
                bk.emptied.inc(act.activation(tiny[0:1, 0, 7:8], o[0:1, 0:1], ACT.Copy))

            def layer_norm(cen, sq, gain, shift, dst):
                for k in range(KD):
                    act.wait_ge(s_lnc, KD * ln_no[0] + k + 1)
                    act.activation(sq[:, k, :], cen[:, k, :], ACT.Square).then_inc(s_lnq, 1)
                yield
                rstd(ln_r[:, 1, :], ln_r[:, 0, :])
                for k in range(KD):
                    act.wait_ge(s_lnm, KD * ln_no[0] + k + 1)
                    act.activation(dst[:, k, :], cen[:, k, :], ACT.Identity, bias=shift(k), scale=gain(k))\
                       .then_inc(s_lno, 1)
                ln_no[0] += 1

            def rstd(dst, src):
                inv_var[0] += 1
                act.wait_ge(s_rv, inv_var[0])
                act.activation(dst, src, ACT.Sqrt).then_inc(s_rstd, 1)

            def whole(steps):
                for _ in steps:
                    pass

            act.wait_ge(s_vec, 16 * 15)
            act.wait_ge(s_const, 9)
            c_at = VAT["c"]
            act.activation(csil[:, :, 0], vec[:, c_at:c_at + KD], ACT.Silu).then_inc(s_csil, 1)
            for n in range(3):
                act.wait_ge(s_mlp, n + 1)
                act.activation(mlp[0:HW, 0, :], mlp[0:HW, 1, :], ACT.Sin).then_inc(s_sin, 1)
            for c in range(4):
                if c:
                    act.wait_ge(s_kst, 16 * c)
                for r in range(8):
                    empty(take(), k_out[:, r, :])
                act.wait_ge(s_ea, bk.emptied.at())
                act.dma_start(ins["spectra"][c], k_out).then_inc(s_kst, 16)
            act.wait_ge(s_gb, 1)
            step.inc(act.activation(rows[2], rows[2], ACT.Exp, scale=-1.0))
            act.wait_ge(s_astep, step.at())
            act.activation(rows[2], rows[2], ACT.Ln, bias=1.0).then_inc(s_gl, 1)
            act.wait_ge(s_row, 3)
            act.activation(rows[3], rows[3], ACT.Exp, scale=-1.0).then_inc(s_em, 1)
            for n in range(KD):
                act.wait_ge(s_ed, note["qk"] + n + 1)
                act.activation(qk[:, n, :], conv[:, n, :], ACT.Silu).then_inc(s_qk, 1)
            act.wait_ge(s_kst, 64)
            for u in range(2):
                for t in range(ST):
                    o = take()
                    empty(o[:, 0:COLS], v_tok[:, t, COLS * u:COLS * u + COLS])
            for h in range(HEADS):
                empty(take(), o_gate[:, h, :], ACT.Sigmoid)
            for g in range(4):
                if g:
                    act.wait_ge(s_pool, g)
                empty(take(), u_pad[:, 16:528])
            for g in range(4):
                empty(take(), mixed[:, 4 + g, :], scale=vcol("pool_scale", g))
            o = take()
            empty(o[:, 0:ST * HEADS], acol[:])
            act.wait_ge(s_ea, bk.emptied.at())
            for h in range(HEADS):
                o = take()
                if h:
                    act.wait_ge(s_hn, h)
                for j in range(ST):
                    act.activation(decay[:, j, P * j:S], o[:, P * j:S], ACT.Exp, bias=acol[:, j, h:h + 1])\
                       .then_inc(s_exp, 1)
                let_go(o)
                if h:
                    act.wait_ge(s_ho, h)
                empty(take(), hn[:, 2, :], ACT.Abs)
                rstd(hn[:, 3, :], hn[:, 3, :])
            ln = layer_norm(region(1), region(2), lambda k: vcol("ln_mix_g", k), lambda k: vcol("ln_mix_b", k), x)
            next(ln)
            act.wait_ge(s_ho, HEADS)
            for n in range(KD):
                o = take()
                empty(o[:, 0:MEM], k_x[:, n, :])
            for u in range(4):
                for m in range(2):
                    o = take()
                    empty(o[:, 0:COLS], v_x[:, m, COLS * u:COLS * u + COLS])
            whole(ln)
            for n in range(KD):
                empty(take(), q_x[:, n, :])
            for h in range(HEADS):
                for t in range(ST):
                    act.wait_ge(s_ed, note["scores"] + ST * h + t + 1)
                    act.activation(p_exp[:, t, :], p_exp[:, t, :], ACT.Exp, scale=XDH ** -0.5,
                                   accum_out=tiny[:, t, 1:2]).then_inc(s_xe, 1)
                for m in range(2):
                    empty(take(), p_t[:, m, :])
                for n in range(2):
                    empty(take(), o_x[:, 2 * h + n, :])
            whole(layer_norm(region(2), region(3), lambda k: vcol("ln_x_g", k), lambda k: vcol("ln_x_b", k), x))
            o = take()
            empty(o[:, 0:ST * NE], route[:, 0, :], ACT.Sigmoid)

            def rows_of_tokens(dst):
                for t in range(ST):
                    for half in range(2):
                        empty(take(), dst[:, t, 512 * half:512 * half + 512])

            def modulation(first, last):
                for u in range(first, last):
                    if u >= 2:
                        act.wait_ge(s_mrow, u - 1)
                    o = take()
                    empty(o[:, 0:COLS], mod_row[:, u % 2, :])

            rows_of_tokens(x_tok)
            modulation(0, 12)
            o = take()
            empty(o[0:NGRP, :], g_rows[0])
            modulation(12, 16)
            o = take()
            empty(o[0:NGRP, 0:1], gcol[:, 1:2])
            modulation(16, 20)
            o = take()
            act.activation(slot1[:], o[:, 0:ST], ACT.Identity).then_inc(s_slot, 1)
            empty(o[0:1, 8:16], tiny[0:1, 2, :])
            modulation(20, 24)
            o = take()
            empty(o[:, 0:EPG * BLOCKS], gate_blk[:, 0:BLOCKS, :].rearrange("p b j -> p (b j)"))
            for b in range(BLOCKS):
                empty(take(), place_t[:, b, :])
            bk_t = Banks(psum, [0, 1], s_mt, s_et)
            bk_y = Banks(psum, [2, 3], s_my, s_ey)

            def take_from(b):
                act.wait_ge(b.filled.sem, b.filled.at(1))
                o = b.bank()
                b.filled.n += 1
                return o

            def copy_from(b, dst, n=S):
                o = take_from(b)
                b.emptied.inc(act.activation(dst, o[:, 0:n], ACT.Identity))

            def gathered_block():
                for n in range(2):
                    copy_from(bk_t, x_blk[:, 4 * n:4 * n + 4, :].rearrange("p k n -> p (k n)"))

            act.wait_ge(s_pl, ST)
            gathered_block()
            with act.Fori(0, BLOCKS) as i:
                for c_ in (bk_t.filled, bk_t.emptied):
                    c_.enter(i, 6)
                for c_ in (bk_y.filled, bk_y.emptied):
                    c_.enter(i, 2)

                def gate(e):
                    act.wait_ge(s_md, 12 * i + note["moe1_d"] + e + 1)
                    o = psum[:, 4 + (note["moe1_d"] + e) % 4, :]
                    act.activation(silu1[:, e % 2, :], o[:, 0:FE], ACT.Silu).then_inc(s_si1, 1)

                def turned(e):
                    copy_from(bk_t, hid_t[:, 2 * (e % 2):2 * (e % 2) + 2, :].rearrange("p k n -> p (k n)"), 2 * P)

                gate(0)
                gate(1)
                turned(0)
                gate(2)
                turned(1)
                gate(3)
                turned(2)
                turned(3)
                for n in range(2):
                    copy_from(bk_y, y_blk[:, 512 * n:512 * n + 512])
                gathered_block()
                for c_ in (bk_t.filled, bk_t.emptied, bk_y.filled, bk_y.emptied):
                    c_.leave(BLOCKS)
            whole(layer_norm(region(3), region(1), lambda k: vcol("ln_moe_g", k), lambda k: vcol("ln_moe_b", k), x))
            whole(layer_norm(region(1), region(2), lambda k: modp[:, 8 + k:9 + k], lambda k: modc[:, k:k + 1], h2))
            act.wait_ge(s_hz, 1)
            for n in range(3 * KD):
                o = take()
                if n >= 2:
                    act.wait_ge(s_uc, n - 1)
                empty(o, hpad[:, n % 2, 1:S + 1], bias=vcol("hy_b_in", n))

            for order in range(2):
                rows_of_tokens(z_tok)
            for n in range(KD):
                empty(take(), region(2)[:, n, :], bias=modg[:, n:n + 1], scale=modp[:, 16 + n:17 + n])
            whole(layer_norm(region(2), region(3), lambda k: vcol("ln_g2", k), lambda k: vcol("ln_b2", k), x))
            whole(layer_norm(region(1), region(3), lambda k: modp[:, 32 + k:33 + k],
                             lambda k: modc[:, 24 + k:25 + k], h2))
            act.wait_ge(s_r0, 1)
            act.activation(route[:, 0, :], route[:, 0, :], ACT.Exp).then_inc(s_r1, 1)
            rows_of_tokens(h_tok)
            o = take()
            empty(o[0:NE, :], aff_t)

            def gathered():
                for n in range(2):
                    empty(take(), x_sel[:, 0, 512 * n:512 * n + 512])
                for n in range(2):
                    o = take()
                    empty(o.rearrange("p (k n) -> p k n", k=4), x_sel_t[:, 4 * n:4 * n + 4, :])

            gathered()
            with act.Fori(0, NE // 2) as i:
                bk.filled.enter(i, 12)
                bk.emptied.enter(i, 12)
                for n in range(4):
                    empty(take(), silu2[:, 0, 512 * n:512 * n + 512], ACT.Silu)
                gathered()
                for n in range(2):
                    o = take()
                    empty(o[:, 0:256], scat[:, 256 * n:256 * n + 256])
                for n in range(2):
                    empty(take(), y_sel[:, 0, 512 * n:512 * n + 512])
                bk.filled.leave(NE // 2)
                bk.emptied.leave(NE // 2)
            whole(layer_norm(region(2), region(3), lambda k: vcol("ln_g2", 8 + k), lambda k: vcol("ln_b2", 8 + k), x))

        @block.vector
        def _(dve):
            bk = Banks(psum, [4, 5, 6, 7], s_md, s_ed)
            step = Count(s_step)
            inv_var = [0]
            ln_no = [0]

            def take():
                dve.wait_ge(s_md, bk.filled.at(1))
                o = bk.bank()
                bk.filled.n += 1
                return o

            def done(ins_):
                bk.emptied.inc(ins_)

            def let_go(o):
                done(dve.tensor_copy(tiny[0:1, 1, 7:8], o[0:1, 0:1]))

            def after_bank():
                dve.wait_ge(s_ed, bk.emptied.at())

            def do(ins_):
                step.inc(ins_)

            def after():
                dve.wait_ge(s_step, step.at())

            def tt(dst, a, b, op):
                return dve.tensor_tensor(dst, a, b, op)

            def ts(dst, a, s1, op0, s2=None, op1=None):
                if op1 is None:
                    return dve.tensor_scalar(dst, a, s1, None, op0)
                return dve.tensor_scalar(dst, a, s1, s2, op0, op1)

            def stt(dst, a, scal, b, op0, op1):
                return dve.scalar_tensor_tensor(out=dst, in0=a, scalar=scal, in1=b, op0=op0, op1=op1)

            def inverse_var(o, dst, scale, eps):
                done(ts(dst, o, scale, ALU.mult, eps, ALU.add))
                after_bank()
                dve.reciprocal(dst, dst).then_inc(s_rv, 1)
                inv_var[0] += 1
                dve.wait_ge(s_rstd, inv_var[0])

            def layer_norm(src, cen, eps=LN_EPS):
                o = take()
                for k in range(KD):
                    tt(cen[:, k, :], src[:, k, :], o, ALU.subtract).then_inc(s_lnc, 1)
                let_go(o)
                inverse_var(take(), ln_r[:, 0, :], 1.0, eps)
                for k in range(KD):
                    tt(cen[:, k, :], cen[:, k, :], ln_r[:, 1, :], ALU.mult).then_inc(s_lnm, 1)
                ln_no[0] += 1

            dve.wait_ge(s_vec, 16 * 15)
            dve.wait_ge(s_const, 9)
            a, r = mlp[0:HW, 1, :], mlp[0:HW, 2, :]
            for n in range(3):
                o = take()
                b_col = fvec[:, 0:1] if n == 0 else fvec[:, n + 1:n + 2]
                done(ts(a, o[0:HW, :], b_col, ALU.add, fvec[:, 1:2], ALU.mult))
                after_bank()
                do(ts(r, a, 1.0 / TWO_PI, ALU.mult, ROUND, ALU.add))
                after()
                do(ts(r, r, ROUND, ALU.subtract))
                after()
                do(stt(a, r, -PI_HI, a, ALU.mult, ALU.add))
                after()
                do(stt(a, r, -PI_LO, a, ALU.mult, ALU.add))
                after()
                ts(a, a, -PI_IN, ALU.max, PI_IN, ALU.min).then_inc(s_mlp, 1)
            for c in range(4):
                half = c // 2
                dve.wait_ge(s_arrived[half], 16)
                win = ring[:, half, :].rearrange("p (k n) -> p k n", k=ST)
                if c:
                    dve.wait_ge(s_ma, 8 * c)
                for taps in (h_fwd, h_bwd):
                    for t in range(ST):
                        done(tt(taps[:, t, :], take(), win[:, t, :], ALU.mult))
                after_bank()
                do(dve.memset(h_bwd[0:1, 0, :], 0.0))
                after()
                tt(h_even, h_fwd, h_bwd, ALU.add).then_inc(s_eo, 1)
                tt(h_odd, h_fwd, h_bwd, ALU.subtract).then_inc(s_eo, 1)
                do(dve.tensor_reduce(abs_sum[:, c, :], h_fwd.rearrange("p k n -> p n k"), AX, ALU.add,
                                     apply_absolute_value=True))
                do(dve.tensor_reduce(abs_tmp, h_bwd.rearrange("p k n -> p n k"), AX, ALU.add,
                                     apply_absolute_value=True))
                after()
                tt(abs_sum[:, c, :], abs_sum[:, c, :], abs_tmp, ALU.add).then_inc(s_abs, 1)
            done(dve.reciprocal(filt_rn[:], take()[:, 0:16]))
            done(ts(rows[0], take()[0:HEADS, :], gbias[:, 0:1], ALU.add))
            done(ts(rows[1], take()[0:HEADS, :], gbias[:, 1:2], ALU.add))
            after_bank()
            stt(rows[2], rows[1], -1.0, rows[1], ALU.mult, ALU.max).then_inc(s_gb, 1)
            dve.wait_ge(s_gl, 1)
            do(stt(rows[1], rows[1], 0.0, rows[2], ALU.min, ALU.subtract))
            after()
            do(dve.tensor_tensor_scan(rows[3], rows[1], rows[1], 0.0, ALU.add, ALU.bypass))
            after()
            tt(rows[0], rows[0], rows[3], ALU.subtract).then_inc(s_row, 1)
            dve.wait_ge(s_row, 1)
            do(dve.tensor_tensor_scan(rows[1], rows[0], rows[0], 0.0, ALU.max, ALU.max))
            after()
            ts(rows[2], rows[1], -1.0, ALU.mult).then_inc(s_row, 1)
            tt(rows[3], rows[3], rows[1], ALU.add).then_inc(s_row, 1)
            for n in range(KD):
                z = take()
                do(ts(conv[:, n, :], z, vcol("conv", 24 + n), ALU.mult))
                for back in range(1, 4):
                    after()
                    ins_ = stt(conv[:, n, back:S], z[:, 0:S - back], vcol("conv", 8 * (3 - back) + n),
                               conv[:, n, back:S], ALU.mult, ALU.add)
                    if back == 3:
                        done(ins_)
                    else:
                        do(ins_)
            do(dve.memset(u_pad[:, 0:16], 0.0))
            for g in range(4):
                dve.wait_ge(s_ea, note["u"] + g + 1)
                after()
                cur, lo = u_pad, 0
                for d in range(g + 1):
                    nxt = (pool_a, pool_b)[d % 2]
                    lo += 1 << d
                    do(tt(nxt[:, lo:528], cur[:, lo:528], cur[:, lo - (1 << d):528 - (1 << d)], ALU.add))
                    after()
                    cur = nxt
                do(stt(mixed[:, g, :], cur[:, 16:528], 1.0 / POOLW[g], u_pad[:, 16:528], ALU.mult, ALU.subtract))
                do(tt(route[:, 0, 0:16], cur[:, 16:32], pool16[:, g, :], ALU.mult))
                after()
                tt(mixed[:, g, 0:16], route[:, 0, 0:16], u_pad[:, 16:32], ALU.subtract).then_inc(s_pool, 1)
            for h in range(HEADS):
                for j in range(ST):
                    o = take()
                    dve.wait_ge(s_tri, ST * h + j + 1)
                    done(stt(decay[:, j, P * j:S], o[:, P * j:S], DH ** -0.5, decay[:, j, P * j:S],
                             ALU.mult, ALU.mult))
                dve.wait_ge(s_ea, note["den", h] + 1)
                done(tt(hn[:, 2, :], take(), hn[:, 2, :], ALU.max))
                after_bank()
                do(dve.reciprocal(hn[:, 2, :], hn[:, 2, :]))
                after()
                done(tt(hn[:, 0, :], take(), hn[:, 2, :], ALU.mult))
                after_bank()
                done(stt(hn[:, 0, :], take(), -1.0 / DH, hn[:, 0, :], ALU.mult, ALU.add))
                after_bank()
                tt(hn[:, 1, :], hn[:, 0, :], hn[:, 0, :], ALU.mult).then_inc(s_hn, 1)
                inverse_var(take(), hn[:, 3, :], 1.0 / DH, LN_EPS)
                do(tt(hn[:, 0, :], hn[:, 0, :], hn[:, 3, :], ALU.mult))
                after()
                stt(mixed[:, h, :], hn[:, 0, :], vcol("head_g", h), o_gate[:, h, :], ALU.mult, ALU.mult)\
                    .then_inc(s_ho, 1)
            for n in range(KD):
                done(stt(region(1)[:, n, :], x[:, n, :], ALPHA, take(), ALU.mult, ALU.add))
            after_bank()
            layer_norm(region(1), region(1))
            for h in range(HEADS):
                if h:
                    dve.wait_ge(s_pread, h)
                for t in range(ST):
                    o = take()
                    do(dve.tensor_reduce(tiny[:, t, 0:1], o[:, 0:MEM], AX, ALU.max))
                    after()
                    done(ts(p_exp[:, t, :], o[:, 0:MEM], tiny[:, t, 0:1], ALU.subtract))
                for t in range(ST):
                    dve.wait_ge(s_xe, ST * h + t + 1)
                    do(dve.reciprocal(tiny[:, t, 2:3], tiny[:, t, 1:2]))
                    after()
                    ts(p_exp[:, t, :], p_exp[:, t, :], tiny[:, t, 2:3], ALU.mult).then_inc(s_xp, 1)
            dve.wait_ge(s_lno, KD)
            for n in range(KD):
                done(stt(region(2)[:, n, :], x[:, n, :], ALPHA, take(), ALU.mult, ALU.add))
            after_bank()
            layer_norm(region(2), region(2))
            dve.wait_ge(s_ea, note["router"] + 1)
            score = route[:, 0, :]
            sel = route[:, 1, :]
            g2 = route[:, 2, :]
            pairs = ptmp[:, 0, 0:96].rearrange("p (g q) -> p g q", q=6)
            cmp_ = ptmp[:, 1, 0:256].rearrange("p (e f) -> p e f", e=NE)
            cmp2 = ptmp[:, 0, 256:512].rearrange("p (e f) -> p e f", e=NE)
            for t in range(ST):
                do(tt(sel[:, NE * t:NE * t + NE], score[:, NE * t:NE * t + NE], rbias[:], ALU.add))
            after()
            sel4 = sel.rearrange("p (g m) -> p g m", m=4)
            q = 0
            for i_ in range(4):
                for j_ in range(i_ + 1, 4):
                    do(tt(pairs[:, :, q], sel4[:, :, i_], sel4[:, :, j_], ALU.add))
                    q += 1
            after()
            do(dve.tensor_reduce(g2[:, 0:16], pairs, AX, ALU.max))
            after()

            def ranks(dst, val, n):
                c1, c2 = cmp_[:, 0:n, 0:n], cmp2[:, 0:n, 0:n]
                of = val.rearrange("p (o f) -> p o f", o=1).broadcast_to([P, n, n])
                to = val.rearrange("p (e o) -> p e o", o=1).broadcast_to([P, n, n])
                do(tt(c1, of, to, ALU.is_equal))
                do(tt(c2, of, to, ALU.is_gt))
                after()
                do(tt(c1, c1, lower[:, 0:n, 0:n], ALU.mult))
                after()
                do(tt(c1, c1, c2, ALU.add))
                after()
                do(dve.tensor_reduce(dst, c1, AX, ALU.add))
                after()

            for t in range(ST):
                ranks(g2[:, 16 + 4 * t:20 + 4 * t], g2[:, 4 * t:4 * t + 4], 4)
            ts(in_group4, in_group4, 0.0, ALU.is_equal).then_inc(s_gt, 1)
            dve.wait_ge(s_gt, 1)
            do(ts(g2[:, 32:48], in_group4, 1.0, ALU.subtract, -NEG, ALU.mult))
            in_group = g2[:, 16:32].rearrange("p (g o) -> p g o", o=1).broadcast_to([P, 16, 4])
            out_group = g2[:, 32:48].rearrange("p (g o) -> p g o", o=1).broadcast_to([P, 16, 4])
            do(tt(sel4, sel4, in_group, ALU.mult))
            after()
            do(tt(sel4, sel4, out_group, ALU.add))
            after()
            rank = route[:, 3, :]
            for t in range(ST):
                ranks(rank[:, NE * t:NE * t + NE], sel[:, NE * t:NE * t + NE], NE)
            do(stt(rank, rank, 2.0, score, ALU.is_lt, ALU.mult))
            after()
            rank3 = rank.rearrange("p (t e) -> p t e", e=NE)
            do(dve.tensor_reduce(route[:, 4, 0:ST], rank3, AX, ALU.add))
            after()
            do(dve.reciprocal(route[:, 4, 8:8 + ST], route[:, 4, 0:ST]))
            after()
            for t in range(ST):
                do(ts(gates[:, t, :], rank3[:, t, :], route[:, 4, 8 + t:9 + t], ALU.mult))
            after()
            for t in range(ST):
                do(dve.tensor_reduce(gate_loc[:, t, :], gates[:, t, :].rearrange("p (g j) -> p j g", j=EPG), AX,
                                     ALU.add))
            dve.wait_ge(s_ea, note["mod", 11] + 1)
            do(dve.tensor_tensor_scan(g_rows[1], g_rows[0], g_rows[0], 0.0, ALU.add, ALU.bypass))
            after()
            do(ts(gcol[:, 2:3], g_rows[1][:, S - 1:S], 1.0 / P, ALU.mult))
            after()
            do(ts(gcol[:, 4:8], iota[0:NGRP, 0:4], gcol[:, 2:3], ALU.is_lt))
            after()
            dve.tensor_reduce(gcol[:, 0:1], gcol[:, 4:8], AX, ALU.add).then_inc(s_start, 1)
            dve.wait_ge(s_start, 1)
            dve.wait_ge(s_ea, note["start"])
            do(ts(gcol[:, 2:3], gcol[:, 1:2], float(P), ALU.mult, 1.0, ALU.subtract))
            do(tt(gcol[:, 3:4], gcol[:, 1:2], gcol[:, 0:1], ALU.add))
            after()
            stt(g_rows[2], g_rows[1], gcol[:, 2:3], g_rows[0], ALU.add, ALU.mult).then_inc(s_sm, 1)
            ts(gcol[:, 8:16], iota[0:NGRP, 0:8], gcol[:, 3:4], ALU.is_ge).then_inc(s_sm, 1)
            dve.wait_ge(s_ea, note["places"])
            ts(block_group[:], tiny[0:1, 2, :], float(NGRP - 1), ALU.min).then_inc(s_blk, 1)
            dve.wait_ge(s_iota, 1)
            for t in range(ST):
                ts(place[:, t, :], iota_d, slot1[:, t:t + 1], ALU.is_equal).then_inc(s_pl, 1)
            m_at = VAT["mod_b"]
            dve.wait_ge(s_mm, 1)
            tt(modc[:], psum[:, 7, 0:48], vec[:, m_at:m_at + 48], ALU.add).then_inc(s_mread, 1)
            dve.wait_ge(s_mread, 1)
            do(ts(modp[:], modc[:], 1.0, ALU.add))
            after()
            b_at = VAT["hy_b_out"]
            do(tt(modg[:], modp[:, 16:24], vec[:, b_at:b_at + KD], ALU.mult))
            dve.wait_ge(s_lno, 2 * KD)
            do(ts(y1, x, ALPHA, ALU.mult))
            after()
            with dve.Fori(0, BLOCKS) as i:
                bk.filled.enter(i, 12)
                bk.emptied.enter(i, 12)
                for e in range(EPG):
                    o = take()
                    dve.wait_ge(s_si1, EPG * i + e + 1)
                    ins_ = stt(hid[:, e % 2, :], o[:, FE:2 * FE], gate_blk[:, i, e:e + 1], silu1[:, e % 2, :],
                               ALU.mult, ALU.mult)
                    ins_.then_inc(s_hid, 1)
                    dve.wait_ge(s_hid, EPG * i + e + 1)
                    let_go(o)
                for n in range(KD):
                    done(tt(y1[:, n, :], take(), y1[:, n, :], ALU.add))
                bk.filled.leave(BLOCKS)
                bk.emptied.leave(BLOCKS)
            after_bank()
            layer_norm(region(3), region(3))
            dve.wait_ge(s_pos, 16)
            for k in range(KD):
                dve.wait_ge(s_lno, 2 * KD + k + 1)
                tt(x[:, k, :], x[:, k, :], pos[:, k, :], ALU.add).then_inc(s_px, 1)
            dve.wait_ge(s_px, KD)
            dve.memset(hpad, 0.0).then_inc(s_hz, 1)
            layer_norm(x, region(1), MOD_EPS)
            for n in range(3 * KD):
                dst = u_hy[n // KD][:, n % KD, :]
                dve.wait_ge(s_ea, note["u_hy"] + n + 1)
                do(ts(dst, hpad[:, n % 2, 1:S + 1], vcol("hy_conv_w", 24 + n), ALU.mult,
                      vcol("hy_conv_b", n), ALU.add))
                after()
                do(stt(dst, hpad[:, n % 2, 0:S], vcol("hy_conv_w", n), dst, ALU.mult, ALU.add))
                after()
                stt(dst, hpad[:, n % 2, 2:S + 2], vcol("hy_conv_w", 48 + n), dst, ALU.mult, ALU.add)\
                    .then_inc(s_uc, 1)
            dve.wait_ge(s_uc, 3 * KD)
            for order in range(2):
                for half in range(2):
                    ks = []
                    for slot_, value in note["k", order, half]:
                        dve.wait_ge(s_arrived[slot_], value)
                        ks.append(ring[:, slot_, :].rearrange("p (k n) -> p k n", k=4))
                    kc, ksn = ks
                    for r_ in range(4):
                        zc, zs = take(), take()
                        t1, t2 = ptmp[:, 0, :], ptmp[:, 1, :]
                        do(tt(spec[:, r_, :], zc, kc[:, r_, :], ALU.mult))
                        done(tt(spec[:, 4 + r_, :], zc, ksn[:, r_, :], ALU.mult))
                        do(tt(t1, zs, ksn[:, r_, :], ALU.mult))
                        done(tt(t2, zs, kc[:, r_, :], ALU.mult))
                        after()
                        after_bank()
                        if r_ == 0:
                            do(dve.tensor_copy(spec[0:1, 4, :], t1[0:1, :]))
                            after()
                            do(dve.memset(t1[0:1, :], 0.0))
                            do(dve.memset(t2[0:1, :], 0.0))
                            after()
                        do(tt(spec[:, r_, :], spec[:, r_, :], t1, ALU.subtract))
                        tt(spec[:, 4 + r_, :], spec[:, 4 + r_, :], t2, ALU.add).then_inc(s_k, 1)
                        dve.wait_ge(s_k, 4 * (2 * order + half) + r_ + 1)
                    after()
                    for n in range(4):
                        m = 4 * half + n
                        z = u_hy[0][:, m, :]
                        t1, t2 = ptmp[:, 0, :], ptmp[:, 1, :]
                        do(ts(t1, z, vcol("hy_f_bias", 8 * order + m), ALU.mult))
                        after()
                        done(stt(t2, take(), filt_rn[:, 8 * order + m:8 * order + m + 1], t1, ALU.mult, ALU.add))
                        after_bank()
                        tt(z, t2, u_hy[1 + order][:, m, :], ALU.mult).then_inc(s_z1, 1)
                        dve.wait_ge(s_z1, KD * order + 4 * half + n + 1)
            for n in range(KD):
                dve.wait_ge(s_ea, note["hyout"] + n + 1)
                stt(region(2)[:, n, :], x[:, n, :], ALPHA, region(2)[:, n, :], ALU.mult, ALU.add)\
                    .then_inc(s_res, 1)
            dve.wait_ge(s_res, KD)
            layer_norm(region(2), region(2))
            dve.wait_ge(s_lno, 5 * KD)
            layer_norm(x, region(1), MOD_EPS)
            logit = route[:, 0, :]
            l3 = logit.rearrange("p (t e) -> p t e", e=NE)
            o = take()[:, 0:ST * NE]
            do(dve.tensor_reduce(route[:, 1, 0:ST], o.rearrange("p (t e) -> p t e", e=NE), AX, ALU.max))
            after()
            for t in range(ST):
                ins_ = ts(l3[:, t, :], o[:, NE * t:NE * t + NE], route[:, 1, t:t + 1], ALU.subtract)
                if t == ST - 1:
                    done(ins_)
                else:
                    do(ins_)
            after_bank()
            after()
            do(dve.memset(tiny[:, 3, 3:4], 0.0))
            after()
            dve.memset(tiny[:, 3, 4:5], 0.0).then_inc(s_r0, 1)
            dve.wait_ge(s_r1, 1)
            do(dve.tensor_reduce(route[:, 2, 0:ST], l3, AX, ALU.add))
            after()
            do(dve.reciprocal(route[:, 2, 8:8 + ST], route[:, 2, 0:ST]))
            after()
            for t in range(ST):
                ins_ = ts(aff[:, t, 0:NE], l3[:, t, :], route[:, 2, 8 + t:9 + t], ALU.mult)
                if t == ST - 1:
                    ins_.then_inc(s_aff, 1)
                else:
                    do(ins_)
            dve.wait_ge(s_lno, 6 * KD)
            do(dve.memset(y2, 0.0))
            dve.wait_ge(s_ea, note["aff_t"])
            do(dve.tensor_copy(work_t, aff_t))
            after()
            for _ in range(CAP // 8):
                do(dve.max(top8[:], work_t))
                after()
                do(dve.match_replace(work_t, top8[:], work_t, -1.0))
                after()
            do(ts(mask_t, work_t, 0.0, ALU.is_lt))
            after()
            do(dve.tensor_tensor_scan(work_t, mask_t, mask_t, 0.0, ALU.add, ALU.bypass))
            after()
            do(tt(work_t, work_t, mask_t, ALU.mult))
            after()
            ts(mask_t, work_t, 1.0, ALU.subtract).then_inc(s_top, 1)
            o = take()
            done(dve.tensor_copy(slot[:, :, 0:NE], o[:, 0:ST * NE].rearrange("p (t e) -> p t e", e=NE)))
            after_bank()

            def one_hot(first, gated):
                for t in range(ST):
                    for e in range(2):
                        place = slot[:, t, bass.ds(first + e, 1)]
                        at = slice(CAP * e, CAP * e + CAP)
                        if gated:
                            ins_ = ts(onehot_g[:, t, at], iota[:], place, ALU.is_equal,
                                      aff[:, t, bass.ds(first + e, 1)], ALU.mult)
                        else:
                            ins_ = ts(onehot[:, t, at], iota[:], place, ALU.is_equal)
                        if t == ST - 1 and e == 1:
                            ins_.then_inc(s_ohg if gated else s_oh, 1)

            one_hot(0, False)
            with dve.Fori(0, NE // 2) as i:
                bk.filled.enter(i, 16)
                bk.emptied.enter(i, 16)
                dve.wait_ge(s_ma, 12 * i + note["moe2_a"] + 1)
                one_hot(2 * i + 2, False)
                one_hot(2 * i, True)
                for n in range(4):
                    o = take()
                    dve.wait_ge(s_ea, 12 * i + note["moe2_a"] + n + 1)
                    done(tt(hid2[:, 0, 512 * n:512 * n + 512], o, silu2[:, 0, 512 * n:512 * n + 512], ALU.mult))
                for n in range(4):
                    o = take()
                    done(dve.tensor_copy(hid2_t[:, 4 * n:4 * n + 4, :], o.rearrange("p (k n) -> p k n", k=4)))
                for n in range(KD):
                    done(tt(y2[:, n, :], take(), y2[:, n, :], ALU.add))
                bk.filled.leave(NE // 2)
                bk.emptied.leave(NE // 2)
            after_bank()
            for n in range(KD):
                do(ts(y2[:, n, :], y2[:, n, :], modp[:, 40 + n:41 + n], ALU.mult))
                after()
                stt(region(2)[:, n, :], x[:, n, :], ALPHA, y2[:, n, :], ALU.mult, ALU.add).then_inc(s_res, 1)
            dve.wait_ge(s_res, 2 * KD)
            layer_norm(region(2), region(2))


def _constants():
    import numpy as np

    t = np.arange(S)
    f = np.arange(S)
    n = 2 * S
    ang = 2.0 * np.pi * ((t[:, None] * f[None, :]) % n) / n
    sign = 1.0 - 2.0 * (t % 2)
    fwd = np.concatenate([np.cos(ang), np.sin(ang)], 1)
    fwd[:, S] = sign
    weight = np.where(f == 0, 1.0, 2.0) / n
    inv = np.concatenate([(np.cos(ang) * weight).T, (np.sin(ang) * 2.0 / n).T], 0)
    inv[S] = sign / n
    dft = [fwd[:, 512 * a:512 * a + 512].reshape(ST, P, 512).transpose(1, 0, 2).reshape(P, UNIT) for a in range(2)]
    dft += [inv[512 * a:512 * a + 512].reshape(4, P, S).transpose(1, 0, 2).reshape(P, UNIT) for a in range(2)]
    last = np.zeros((S, P))
    last[:, 0] = 2.0 * sign
    f32 = np.float32
    t01 = t.astype(f32) / f32(S - 1)
    bands = (EMB - 1) // 2
    freq = np.linspace(1e-4, bands - 1, bands, dtype=f32)
    angle = freq[None, :] * (f32(2.0 * np.pi) * t.astype(f32) / f32(S))[:, None]
    z = np.concatenate([t01[:, None], np.cos(angle), -np.sin(angle)], -1)
    hi, lo = np.log(1e-2) / 0.3, np.log(1e-2) / 1.5
    delta = np.linspace(lo, hi, D, dtype=f32)
    window = np.exp(-t01[:, None] * np.abs(delta)[None, :])
    window = window.reshape(ST, P, 2, 512).transpose(2, 1, 0, 3).reshape(2, P, UNIT)
    quarter = D // 4
    omega = f32(1.0) / (f32(10000.0) ** (np.arange(quarter, dtype=f32) / f32(quarter)))

    def emb(p):
        a = p.astype(f32)[:, None] * omega[None, :]
        return np.concatenate([np.sin(a), np.cos(a)], -1)

    pos = np.concatenate([emb(t // 64), emb(t % 64)], -1)
    pool16 = np.stack([1.0 / np.minimum(np.arange(1, 17), w) for w in POOLW])
    lower = (np.arange(NE)[None, :] < np.arange(NE)[:, None])
    return {
        "dft": np.stack(dft), "last_row": last.reshape(ST, P, P).transpose(1, 0, 2), "zfeat": z.T,
        "window": window, "pos": pos.T.reshape(KD, P, S).transpose(1, 0, 2),
        "tri4": np.triu(np.ones((NGRP, NGRP)), 1),
        "pool16": np.broadcast_to(pool16, (P, 4, 16)), "lower": lower[None],
    }


def _layout(a):
    import numpy as np

    def slabs(w):
        n = w.shape[1] // COLS
        return w.reshape(KD, P, n, COLS).transpose(2, 1, 0, 3).reshape(n, P, UNIT)

    def cols(v):
        v = v.reshape(-1, P)
        return v.T

    w_in = a["w_in"][0]
    m = 4 * 512
    up = np.concatenate([a["w_gate"][0], a["w_up"][0]], 2)
    up = up.reshape(NE, 2, 4, P, 2 * FE).transpose(0, 1, 3, 2, 4).reshape(NE, 2, P, UNIT)
    down = a["w_down"][0].reshape(NE, 2, P, D).transpose(0, 2, 1, 3).reshape(NE, 1, P, UNIT)
    moe1 = np.concatenate([up, down], 1).reshape(NGRP, 3 * EPG, P, UNIT)
    parts = {
        "mod": slabs(a["mod_w_2"][0]), "in": slabs(np.concatenate([w_in[:, :m], w_in[:, m + 8:]], 1)),
        "mix": slabs(a["w_mix_out"][0]), "xkv": slabs(a["w_xkv"][0]), "xq": slabs(a["w_xq"][0]),
        "xo": slabs(a["w_xo"][0]), "hyin": slabs(a["hy_w_in_2"][0]),
        "hyout": slabs(a["hy_w_out_2"][0]),
    }
    vecs = {
        "conv": a["conv_qk"][0], "head_g": a["head_norm_g"][0], "pool_scale": a["pool_scale"][0],
        "ln_mix_g": a["ln_mix_g"][0], "ln_mix_b": a["ln_mix_b"][0], "ln_x_g": a["ln_x_g"][0],
        "ln_x_b": a["ln_x_b"][0], "ln_moe_g": a["ln_moe_g"][0], "ln_moe_b": a["ln_moe_b"][0],
        "mod_b": a["mod_b_2"][0], "ln_g2": a["ln_g_2"][0], "ln_b2": a["ln_b_2"][0], "hy_b_in": a["hy_b_in_2"][0],
        "hy_conv_w": a["hy_conv_w_2"][0], "hy_conv_b": a["hy_conv_b_2"][0], "hy_f_bias": a["hy_f_bias_2"][0],
        "hy_b_out": a["hy_b_out_2"][0], "c": a["c_2"][0],
    }
    router = np.stack([a["router_w"], a["moe_router_2"][0]])
    return {
        "moe1": moe1,
        "stream": np.concatenate([parts[name] for name, _ in STREAM]),
        "vecs": np.concatenate([cols(vecs[name]) for name, _ in VECS], 1),
        "fvecs": np.stack([a["hy_f_b1_2"][0], a["hy_f_freq_2"][0], a["hy_f_b2_2"][0, 0], a["hy_f_b2_2"][0, 1]], 1),
        "fw1": a["hy_f_w1_2"][0], "fw2": a["hy_f_w2_2"][0].transpose(1, 0, 2), "fw3": a["hy_f_w3_2"][0],
        "gbias": np.stack([a["b_i"][0], a["b_f"][0]], 1),
        "wgate": w_in[:, m:m + 8].reshape(KD, P, 8).transpose(1, 0, 2),
        "poolw": a["pool_w"][0].transpose(1, 0, 2),
        "router": router.reshape(2, KD, P, NE).transpose(2, 0, 1, 3), "rbias": a["router_bias"][None],
        "x": a["x"][0].T.reshape(KD, P, S).transpose(1, 0, 2),
        "mem": a["mem"][0].T.reshape(KD, P, MEM).transpose(1, 0, 2),
        "w1": a["moe_w1_2"][0].reshape(NE, KD, P, FF), "w3": a["moe_w3_2"][0].reshape(NE, KD, P, FF),
        "w2": a["moe_w2_2"][0].reshape(NE, KD, 2 * P, D),
    }


def kernel(**inputs):
    import numpy as np
    import concourse.bacc as bacc
    from concourse.bass_utils import run_bass_kernel_spmd

    a = {name: np.asarray(v) for name, v in inputs.items()}
    arrays = {**_layout(a), **_constants()}
    arrays = {f"in_{name}": np.ascontiguousarray(v, np.float32) for name, v in arrays.items()}
    nc = bacc.Bacc("TRN2", target_bir_lowering=False, num_devices=1)
    ins = {name[3:]: nc.dram_tensor(name, v.shape, F32, kind="ExternalInput").ap() for name, v in arrays.items()}
    ins["spectra"] = nc.dram_tensor("in_spectra", (4, P, 8, 512), F32, kind="Internal").ap()
    out = nc.dram_tensor("out", (P, KD, S), F32, kind="ExternalOutput").ap()
    build(nc, ins, out)
    r = run_bass_kernel_spmd(nc, [arrays], core_ids=[0])
    got = r.results[0]["out"]
    return got.transpose(2, 1, 0).reshape(1, S, D)
```

```python
from contextlib import ExitStack

import concourse.bass as bass
from concourse import mybir

P = 128
D = 1024
KD = D // P
S = 512
ST = S // P
MEM = 256
HEADS = 4
DH = 128
XDH = 256
NE = 16
NGRP = 4
FE = 256
FF = 2048
EPG = NE // NGRP
BLOCKS = 7
ORDER1 = [0, 1, 3, 4, 2, 6, 7, 5, 9, 10, 8, 11]
CAP = 64
POOLW = (2, 4, 8, 16)
HW = 64
EMB = 33
UNIT = 2048
COLS = UNIT // KD
RING = 6
RING2 = 12
ALPHA = 2.0 ** 0.25
LN_EPS = 1e-5
MOD_EPS = 1e-6
NEG = -1.0e30

F32 = mybir.dt.float32
F32R = mybir.dt.float32r
ALU = mybir.AluOpType
ACT = mybir.ActivationFunctionType
AX = mybir.AxisListType.X

STREAM = [("mod", 24), ("in", 10), ("mix", 4), ("xkv", 8), ("xq", 4), ("xo", 4), ("hyin", 12), ("hyout", 4)]
BASE = {}
_n = 0
for _name, _units in STREAM:
    BASE[_name] = _n
    _n += _units
UNITS = _n

PER_BLOCK = 3 * EPG
SPLIT_BLOCK = 2 * EPG
HIGH = 4
_first = {"in": BASE["in"], "moe1": BASE["hyin"], "hyin": BASE["hyin"] + PER_BLOCK * BLOCKS}
_first["hyout"] = _first["hyin"] + 12 + 24
SPLIT = ([u for u in range(_first["in"], _first["moe1"])]
         + [_first["moe1"] + PER_BLOCK * b + u for b in range(BLOCKS) for u in range(PER_BLOCK) if ORDER1[u] % 3 < 2]
         + [_first["hyin"] + u for u in range(12)]
         + [_first["hyin"] + 12 + 6 * b + u for b in range(4) for u in range(2)]
         + [_first["hyout"] + u for u in range(4)])

VECS = [("conv", 32), ("head_g", 4), ("pool_scale", 4), ("ln_mix_g", 8), ("ln_mix_b", 8), ("ln_x_g", 8),
        ("ln_x_b", 8), ("ln_moe_g", 8), ("ln_moe_b", 8), ("mod_b", 48), ("ln_g2", 16), ("ln_b2", 16),
        ("hy_b_in", 24), ("hy_conv_w", 72), ("hy_conv_b", 24), ("hy_f_bias", 16), ("hy_b_out", 8), ("c", 8)]
VAT = {}
_n = 0
for _name, _units in VECS:
    VAT[_name] = _n
    _n += _units
NVEC = _n

TWO_PI = 6.283185307179586
PI_HI = 6.28125
PI_LO = TWO_PI - PI_HI
ROUND = 12582912.0
PI_IN = 3.1415925


class Count:

    def __init__(self, sem):
        self.sem, self.n, self.i, self.per, self.first = sem, 0, None, 0, 0

    def at(self, more=0):
        v = self.n + more
        return v if self.i is None else v + self.i * self.per

    def inc(self, ins, by=1):
        ins.then_inc(self.sem, by)
        self.n += by

    def enter(self, i, per):
        self.i, self.per, self.first = i, per, self.n

    def leave(self, rounds):
        assert self.n - self.first == self.per, (self.n - self.first, self.per)
        self.n, self.i = self.first + self.per * rounds, None


class Banks:

    def __init__(self, psum, banks, filled, emptied):
        self.psum, self.banks = psum, banks
        self.filled, self.emptied = Count(filled), Count(emptied)

    def bank(self, more=0):
        return self.psum[:, self.banks[(self.filled.n + more) % len(self.banks)], :]


def build(nc, ins, out):
    with ExitStack() as ctx:
        def sb(name, shape):
            return ctx.enter_context(nc.sbuf_tensor(name, shape, F32))

        def sem(name):
            return ctx.enter_context(nc.semaphore(name))

        def under(name, shape):
            with nc.sbuf_tensor(name, shape, F32) as tensor:
                return tensor

        def part(name, shape):
            return ctx.enter_context(nc.sbuf_tensor(name, shape, F32R))

        ring = under("ring", [P, RING2, UNIT])
        w_low = [part(f"weights_low{r}", [P, UNIT]) for r in range(RING)]
        w_high = [part(f"weights_high{r}", [P, UNIT]) for r in range(HIGH)]
        f_high = part("features_high_part", [P, KD, S])
        arena = under("arena", [P, 6, KD * S])
        arena_low = [part(f"arena_low{r}", [P, KD * S]) for r in range(6)]
        psum = ctx.enter_context(nc.psum_tensor("psum", [P, 8, 512], F32))

        ones = sb("ones", [P, P])
        mean_w = sb("mean_w", [P, P])
        ident = sb("ident", [P, P])
        iota = sb("iota", [P, CAP])
        vec = sb("vec", [P, NVEC])
        fvec = sb("fvec", [HW, 4])
        fw1 = sb("fw1", [EMB, HW])
        fw2 = sb("fw2", [HW, 2, HW])
        gbias = sb("gbias", [HEADS, 2])
        wgate = sb("wgate", [P, KD, 8])
        pool16 = sb("pool16", [P, 4, 16])
        router = sb("router", [P, 2, KD, NE])
        rbias = sb("rbias", [P, NE])
        lower = sb("lower", [P, NE, NE])
        csil = sb("csil", [P, KD, 32])
        tri4 = sb("tri4", [NGRP, NGRP])
        gcol = sb("gcol", [NGRP, 8 + BLOCKS + 1])
        block_group = ctx.enter_context(nc.sbuf_tensor("block_group", [1, 8], mybir.dt.int32))
        slot1 = sb("slot1", [P, ST])
        gate_loc = sb("gate_loc", [P, ST, EPG])
        gate_blk = sb("gate_blk", [P, 8, EPG])
        modc = sb("modc", [P, 48])
        modp = sb("modp", [P, 48])
        modg = sb("modg", [P, 8])
        filt_rn = sb("filt_rn", [P, 16])
        acol = sb("acol", [P, ST, HEADS])
        tiny = sb("tiny", [P, 4, 8])
        route = sb("route", [P, 6, ST * NE])
        gates = sb("gates", [P, ST, NE])
        slot = sb("slot", [P, ST, NE + 2])
        aff = sb("aff", [P, ST, NE + 2])
        zero = sb("zero", [P, 1])

        def vcol(name, j):
            return vec[:, VAT[name] + j:VAT[name] + j + 1]

        def region(r, at=0, tiles=KD, width=S):
            return arena[:, r, at:at + tiles * width].rearrange("p (k n) -> p k n", k=tiles)

        def low_region(r, at=0, tiles=KD, width=S):
            return arena_low[r][:, at:at + tiles * width].rearrange("p (k n) -> p k n", k=tiles)

        dft_f = region(0).rearrange("p (a k) n -> p a k n", a=2)
        h_fwd, h_bwd = region(1, 0, ST), region(1, 2048, ST)
        h_even, h_odd = region(2, 0, ST), region(2, 2048, ST)
        k_out = region(3)
        abs_sum = region(4, 0, ST)
        mlp = region(4, 2048, 4)
        abs_tmp = region(4, 3072, 1)[:, 0, :]
        fw3 = arena[0:HW, 5, :]
        dft_parts = [[w_high[a][:].rearrange("p (k n) -> p k n", k=ST), low_region(0, 2048 * a, ST)] for a in range(2)]
        even_parts = [w_high[2][:].rearrange("p (k n) -> p k n", k=ST), low_region(2, 0, ST)]
        odd_parts = [w_high[3][:].rearrange("p (k n) -> p k n", k=ST), low_region(2, 2048, ST)]
        windows = ring[:, RING2 - 2:RING2, :]
        mod_row = region(4, 3584, 2, COLS)
        x = region(0)
        qk = region(1)
        conv = qk
        x_low, mixed_low = low_region(2), low_region(5)
        v_tok, o_gate = region(3, 0, ST), region(3, 2048, ST)
        u_pad = arena[:, 4, 0:528]
        pool_a = arena[:, 4, 528:1056]
        pool_b = arena[:, 4, 1056:1584]
        rows = [arena[0:HEADS, 4, 1584 + 512 * n:2096 + 512 * n] for n in range(4)]
        mixed = region(5)
        decay = region(2, 0, ST)
        hn = region(2, 2048, 4)
        mem_t, k_x = region(3, 0, KD, MEM), region(3, 2048, KD, MEM)
        v_x = region(4, 0, 2, D)
        p_exp = region(4, 2048, 4, MEM)
        p_t = region(4, 3072, 2)
        q_x, o_x = region(5), region(1)
        mem_high, mem_low = low_region(4, 2048, KD, MEM), low_region(3, 0, KD, MEM)
        x1_low, o_x_low = low_region(2), low_region(1)
        x_tok, x_tok_low = region(1, 0, 2 * ST, S), low_region(1, 0, 2 * ST, S)
        place = low_region(2, 0, ST, D)
        place_t = low_region(5, 0, BLOCKS, S)
        logits_t = [arena[0:NE, 5, 1536:2048], arena[0:NE, 3, 0:512]]
        g_rows = [arena[0:NGRP, 5, 512 * n:512 * n + 512] for n in range(3)]
        y1 = region(3)
        iota_d = arena[:, 4, 0:D]
        x_blk = [low_region(4, 0, KD, P), low_region(4, D, KD, P)]
        silu1 = region(4, 2048, 2, FE)
        hid = region(4, 2560, 2, FE)
        hid_t = region(4, 3072, 4, P)
        y_blk = [arena_low[4][:, 2048:3072], arena_low[4][:, 3072:4096]]
        pos = region(5)
        h2 = region(4)
        u_hy = [region(1), region(2), region(3)]
        h2_low, z_low = low_region(4), low_region(1)
        z_tok, z_tok_low = region(4), low_region(4)
        spec = region(5)
        h_tok = region(5, 0, ST, D)
        y2 = region(1)
        x_sel = region(2, 0, 1, D)
        x_sel_t = region(2, 1024, KD, P)
        y_sel = region(2, 2048, 1, D)
        onehot = region(2, 3072, ST, P)
        onehot_g = region(2, 3584, ST, P)
        hid2, silu2 = region(3, 0, 1, FF), region(3, 2048, 1, FF)
        hid2_t = region(4, 0, FF // P, P)
        scat = arena[:, 4, 2048:2560]
        aff_t = arena[0:NE, 4, 2560:3072]
        work_t = arena[0:NE, 4, 3072:3584]
        mask_t = arena[0:NE, 4, 3584:4096]
        hpad = arena[:, 5, 0:2 * (S + 2)].rearrange("p (b n) -> p b n", b=2)
        scratch = sb("scratch", [P, 2, S])
        last_row = scratch[:, 0, :].rearrange("p (k n) -> p k n", k=ST)
        poolw = scratch[:, 1, :].rearrange("p (k n) -> p k n", k=4)
        ptmp = scratch
        ln_stat = scratch[:, :, 0:P]
        top8 = sb("top8", [NE, 8])
        in_group4 = route[:, 2, 16:32]

        s_arrived = [sem(f"arrived{r}") for r in range(RING)]
        s_arrived2 = [sem(f"expert_arrived{r}") for r in range(RING2)]
        s_used = sem("units_used")
        s_ma, s_ea = sem("act_filled"), sem("act_emptied")
        s_md, s_ed = sem("dve_filled"), sem("dve_emptied")
        s_whi, s_wlo = sem("weights_high"), sem("weights_low")
        s_bhi = sem("bank_high")
        s_fhi, s_flo = sem("features_high"), sem("features_low")
        s_const = sem("pool_consts")
        s_net = sem("network_in")
        s_vec = sem("vectors_in")
        s_cf = sem("dft_in")
        s_win = sem("windows_in")
        s_step = sem("dve_step")
        s_astep = sem("act_step")
        s_mlp = sem("mlp_arg")
        s_sin = sem("mlp_sine")
        s_hw = sem("taps_windowed")
        s_eo = sem("taps_even_odd")
        s_kst = sem("filter_stored")
        s_kout = sem("filter_copied")
        s_abs = sem("taps_abs_sum")
        s_csil = sem("c_silu")
        s_x = sem("x_in")
        s_gb = sem("gate_rows")
        s_gl = sem("gate_ln")
        s_conv = sem("conv_done")
        s_qk = sem("qk_ready")
        s_upad = sem("pool_input")
        s_pool = sem("pool_done")
        s_row = sem("rows_ready")
        s_exp = sem("decay_exp")
        s_tri = sem("decay_masked")
        s_rv = sem("inverse_var")
        s_rstd = sem("rstd")
        s_hn = sem("head_square")
        s_ho = sem("head_out")
        s_den = sem("den_abs")
        s_res = sem("residual_sum")
        s_lnc = sem("ln_centred")
        s_lnq = sem("ln_square")
        s_lnm = sem("ln_scaled")
        s_lno = sem("ln_out")
        s_mem = sem("mem_in")
        s_xs = sem("scores_shifted")
        s_xe = sem("scores_exp")
        s_xp = sem("probs_ready")
        s_pread = sem("probs_read")
        s_em = sem("den_floor")
        s_ohg = sem("gated_onehots")
        s_aff = sem("affinities")
        s_r0 = sem("logits_shifted")
        s_r1 = sem("logits_exp")
        s_gt = sem("group_masks")
        s_blk = sem("block_groups")
        s_start = sem("group_blocks")
        s_sm = sem("place_rows")
        s_pl = sem("places")
        s_iota = sem("iota_ready")
        s_slot = sem("place_columns")
        s_gates = sem("gates_ready")
        s_si1 = sem("silu1")
        s_hid = sem("hidden1")
        s_mt, s_et = sem("blk_filled"), sem("blk_emptied")
        s_my, s_ey = sem("out_filled"), sem("out_emptied")
        s_pos = sem("pos_in")
        s_px = sem("pos_added")
        s_hz = sem("hy_pad_zero")
        s_uc = sem("hy_conv")
        s_zt = sem("z_tok_ready")
        s_k = sem("spectrum_product")
        s_z1 = sem("z_next")
        s_ys = sem("hy_out_scaled")
        s_top = sem("top_ready")
        s_oh = sem("onehots")
        s_si2 = sem("silu2")
        s_hid2 = sem("hidden2")
        s_y0 = sem("y2_zero")
        s_g2 = sem("moe2_groups_a")
        s_out = sem("out_stored")

        def spectra_of(c):
            return (8 + 12) * c - 1

        note = {}

        block = ctx.enter_context(nc.Block())

        @block.sync
        def _(sp):
            used = Count(s_used)
            turn = [0]
            arrived = s_arrived

            def load(src, dst_shape=None):
                slots = len(arrived)
                slot_ = turn[0] % slots
                if used.i is not None or turn[0] >= slots:
                    sp.wait_ge(s_used, used.at(1 - slots))
                dst = ring[:, slot_, :]
                if dst_shape is not None:
                    dst = dst_shape(dst)
                sp.dma_start(dst, src).then_inc(arrived[slot_], 16)
                used.n += 1
                turn[0] += 1

            network = [(fw1[:], ins["fw1"]), (mlp[0:EMB, 3, :], ins["zfeat"]), (fvec[:], ins["fvecs"]),
                       (fw2[:], ins["fw2"])]
            for dst, src in network:
                sp.dma_start(dst, src).then_inc(s_net, 16)
            small = [(fw3, ins["fw3"]), (vec[:], ins["vecs"]), (gbias[:], ins["gbias"]), (wgate[:], ins["wgate"]),
                     (poolw, ins["poolw"]), (pool16[:], ins["pool16"]), (last_row, ins["last_row"]),
                     (router[:], ins["router"]), (rbias[:], ins["rbias"].broadcast_to([P, NE])),
                     (tri4[:], ins["tri4"]), (lower[:], ins["lower"].broadcast_to([P, NE, NE]))]
            sp.dma_start(dft_f, ins["dft"][0:2].rearrange("a p (k n) -> p a k n", k=ST)).then_inc(s_cf, 16)
            for dst, src in small:
                sp.dma_start(dst, src).then_inc(s_vec, 16)
            for half in range(2):
                sp.dma_start(windows[:, half, :], ins["window"][half]).then_inc(s_win, 16)
            for u in range(24):
                load(ins["stream"][BASE["mod"] + u])
            for u in range(14):
                if u == RING:
                    sp.wait_ge(s_ma, spectra_of(4))
                    sp.dma_start(x, ins["x"]).then_inc(s_x, 16)
                load(ins["stream"][BASE["in"] + u])
            sp.wait_ge(s_ho, HEADS)
            sp.dma_start(mem_t, ins["mem"]).then_inc(s_mem, 16)
            for u in range(16):
                load(ins["stream"][BASE["xkv"] + u])
            sp.wait_ge(s_blk, 1)
            with sp.Fori(0, BLOCKS) as i:
                used.enter(i, 12)
                group = sp.value_load(block_group[0:1, bass.ds(i, 1)], min_val=0, max_val=NGRP - 1)
                for j in ORDER1:
                    load(ins["moe1"][group, j])
                used.leave(BLOCKS)
            turn[0] += 12 * (BLOCKS - 1)
            for u in range(12):
                if u == RING:
                    sp.wait_ge(s_lnc, 2 * KD + 1)
                    sp.dma_start(pos, ins["pos"]).then_inc(s_pos, 16)
                load(ins["stream"][BASE["hyin"] + u])
            for order in range(2):
                for half in range(2):
                    load(ins["dft"][0])
                    load(ins["dft"][1])
                    if order == 0 and half == 0:
                        sp.wait_ge(s_kst, 16 * 4)
                    c = 2 * half + order
                    load(ins["spectra"][c, :, 0:4, :], lambda d: d.rearrange("p (k n) -> p k n", k=4))
                    load(ins["spectra"][c, :, 4:8, :], lambda d: d.rearrange("p (k n) -> p k n", k=4))
                    load(ins["dft"][2])
                    load(ins["dft"][3])
            for u in range(4):
                load(ins["stream"][BASE["hyout"] + u])
            sp.wait_ge(s_used, used.at())
            arrived, turn[0] = s_arrived2, 0
            with sp.Fori(0, NE // 2) as i:
                used.enter(i, 48)
                for name in ("w1", "w3"):
                    for k in range(KD):
                        for e in range(2):
                            load(ins[name][2 * i + e, k])
                for k in range(KD):
                    for e in range(2):
                        load(ins["w2"][2 * i + e, k].rearrange("(a p) n -> p a n", a=2),
                             lambda d: d.rearrange("p (a n) -> p a n", a=2))
                used.leave(NE // 2)
            for k in range(KD):
                sp.wait_ge(s_lno, 6 * KD + k + 1)
                sp.dma_start(out[:, k, :], x[:, k, :]).then_inc(s_out, 16)
            sp.wait_ge(s_out, 16 * KD)

        @block.gpsimd
        def _(pool):
            pool.memset(ones[:], 1.0).then_inc(s_const, 1)
            pool.memset(mean_w[:], 1.0 / D).then_inc(s_const, 1)
            pool.memset(ident[:], 0.0).then_inc(s_const, 1)
            pool.memset(csil[:], 0.0).then_inc(s_const, 1)
            pool.memset(slot[:], -1.0).then_inc(s_const, 1)
            pool.memset(aff[:], 0.0).then_inc(s_const, 1)
            pool.memset(zero[:], 0.0).then_inc(s_const, 1)
            pool.wait_ge(s_const, 7)
            pool.affine_select(out=ident[:], in_=ident[:], compare_op=ALU.not_equal, fill=1.0, base=0,
                               pattern=[[-1, P]], channel_multiplier=1).then_inc(s_const, 1)
            pool.iota(iota[:], pattern=[[1, CAP]], base=0, channel_multiplier=0,
                      allow_small_or_imprecise_dtypes=True).then_inc(s_const, 1)
            for h in range(HEADS):
                for j in range(ST):
                    pool.wait_ge(s_exp, ST * h + j + 1)
                    blk = decay[:, j, P * j:P * j + P]
                    pool.affine_select(out=blk, in_=blk, compare_op=ALU.is_ge, fill=0.0, base=0,
                                       pattern=[[1, P]], channel_multiplier=-1).then_inc(s_tri, 1)
            pool.wait_ge(s_lnc, KD + 1)
            pool.iota(iota_d, pattern=[[1, D]], base=0, channel_multiplier=0,
                      allow_small_or_imprecise_dtypes=True).then_inc(s_iota, 1)

        @block.tensor
        def _(pe):
            bk_a = Banks(psum, [0, 1, 2, 3], s_ma, s_ea)
            bk_d = Banks(psum, [4, 5, 6, 7], s_md, s_ed)
            unit_no = Count(s_used)
            turn = [0]
            owed = []
            arrived = s_arrived

            def begin(b):
                if b.filled.i is not None or b.filled.n >= len(b.banks):
                    pe.wait_ge(b.emptied.sem, b.filled.at(1 - len(b.banks)))
                return b.bank()

            def mm(o, lhs, rhs, start, stop, ends=None, tr=False):
                if tr:
                    ins_ = pe.transpose(o, lhs, rhs)
                else:
                    ins_ = pe.matmul(o, lhs, rhs, start=start, stop=stop)
                if ends is not None:
                    ends.filled.inc(ins_)
                elif owed:
                    ins_.then_inc(owed.pop(0), 1)
                return ins_

            def read(b, ago=0):
                pe.wait_ge(b.emptied.sem, b.filled.at(-ago))

            def unit():
                slots = len(arrived)
                slot_ = turn[0] % slots
                turns = turn[0] // slots + 1
                v = 16 * turns if unit_no.i is None else unit_no.i * (16 * unit_no.per // slots) + 16 * turns
                pe.wait_ge(arrived[slot_], v)
                turn[0] += 1
                unit_no.n += 1
                return ring[:, slot_, :]

            def used():
                owed.append(s_used)

            def enter(i, rounds, per_units, per_a, per_d):
                unit_no.enter(i, per_units)
                bk_a.filled.enter(i, per_a)
                bk_d.filled.enter(i, per_d)
                return turn[0], rounds

            def leave(entry):
                t0, rounds = entry
                for c_ in (unit_no, bk_a.filled, bk_d.filled):
                    c_.leave(rounds)
                turn[0] = t0 + unit_no.per * rounds

            low_parts = Count(s_wlo)
            tiles_split = [0]

            def split_unit():
                n, slot_ = low_parts.n, turn[0] % RING
                pe.wait_ge(s_wlo, low_parts.at(1))
                low_parts.n += 1
                turn[0] += 1
                unit_no.n += 1
                return w_high[n % HIGH][:], w_low[slot_][:]

            def product(o, lhs, rhs, start, stop, ends):
                mm(o, lhs[0], rhs[0], start, False)
                mm(o, lhs[0], rhs[1], False, False)
                mm(o, lhs[1], rhs[0], False, stop, ends if stop else None)

            def project(units, high, low, b, n=S, fresh=0):
                for u in range(units):
                    w = split_unit()
                    for j in range(COLS // P):
                        o = begin(b)
                        for k in range(KD):
                            if k < fresh and u == 0 and j == 0:
                                tiles_split[0] += 1
                                pe.wait_ge(s_flo, tiles_split[0])
                            at = slice(COLS * k + P * j, COLS * k + P * j + P)
                            product(o[:, 0:n], [w_[:, at] for w_ in w], [high[:, k, :], low[:, k, :]],
                                    k == 0, k == KD - 1, b)
                    used()

            def project_tok(units, high, low, tiles, b):
                for _u in range(units):
                    w = split_unit()
                    for t in range(tiles):
                        o = begin(b)
                        for k in range(KD):
                            at = slice(P * t, P * t + P)
                            product(o[:, 0:COLS], [high[:, k, at], low[:, k, at]],
                                    [w_[:, COLS * k:COLS * k + COLS] for w_ in w], k == 0, k == KD - 1, b)
                    used()

            def to_tokens(src):
                for t in range(ST):
                    for half in range(2):
                        o = begin(bk_a)
                        for n in range(4):
                            mm(o[:, P * n:P * n + P], src[:, 4 * half + n, P * t:P * t + P], ident[:], True, True,
                               bk_a if n == 3 else None, tr=True)

            ln_no = [0]

            def summed(k):
                pe.wait_ge(s_ed, bk_d.filled.n - KD + k + 1)

            def token_means(src, ready):
                o = begin(bk_d)
                for k in range(KD):
                    ready(k)
                    for t in range(ST):
                        mm(o[32 * t:32 * t + 32, 0:P], mean_w[:, 0:32], src[:, k, P * t:P * t + P], k == 0,
                           k == KD - 1, bk_d if k == KD - 1 and t == ST - 1 else None)

            def along_rows(stat):
                o = begin(bk_d)
                for t in range(ST):
                    pick = ident[:, 32 * t:32 * t + 1].broadcast_to([P, P])
                    mm(o[:, P * t:P * t + P], pick, stat, True, True, bk_d if t == ST - 1 else None)

            def layer_norm(src, sq, ready, tail=lambda: None):
                token_means(src, ready)
                read(bk_d)
                along_rows(ln_stat[:, 0, :])
                tail()
                token_means(sq, lambda k: pe.wait_ge(s_lnq, KD * ln_no[0] + k + 1))
                ln_no[0] += 1
                pe.wait_ge(s_rstd, HEADS + ln_no[0])
                along_rows(ln_stat[:, 1, :])

            pe.wait_ge(s_const, 9)
            pe.wait_ge(s_net, 16 * 4)
            for n in range(3):
                o = begin(bk_d)
                if n == 0:
                    mm(o[0:HW, :], fw1[:], mlp[0:EMB, 3, :], True, True, bk_d)
                else:
                    pe.wait_ge(s_sin, n)
                    mm(o[0:HW, :], fw2[:, n - 1, :], mlp[0:HW, 0, :], True, True, bk_d)
            pe.wait_ge(s_sin, 3)
            pe.wait_ge(s_vec, 16 * 11)
            def modulation_row(u):
                w = unit()
                o = begin(bk_a)
                for r in range(2):
                    for g in range(4):
                        k = 4 * r + g
                        mm(o[32 * g:32 * g + 32, 0:COLS], csil[:, k, :], w[:, COLS * k:COLS * k + COLS],
                           r == 0, r == 1, bk_a if k == 7 else None)
                note["mod", u] = bk_a.filled.n
                used()

            def modulation_columns(u):
                o = begin(bk_a)
                pe.wait_ge(s_ea, note["mod", u])
                for j in range(2):
                    mm(o[:, j:j + 1], mod_row[:, u % 2, P * j:P * j + P], ones[:, 0:1], True, True,
                       bk_a if j == 1 else None)

            pe.wait_ge(s_csil, 1)
            tiles_split[0] += 2

            def taps(c):
                half, order = c // 2, c % 2
                for dirn in range(2):
                    for t in range(ST):
                        o = begin(bk_d)
                        at = 2 * D * dirn + D * order + 512 * half
                        mm(o, mlp[0:HW, 0, P * t:P * t + P], fw3[:, at:at + 512], True, True, bk_d)

            def modulation(first):
                for u in range(first, first + 6):
                    modulation_row(u)
                    if u:
                        modulation_columns(u - 1)

            def half_spectrum(odd):
                tiles_split[0] += 1
                pe.wait_ge(s_flo, tiles_split[0])
                for r in range(4):
                    o = begin(bk_a)
                    extra = odd and r == 0
                    for k in range(ST):
                        product(o, [f[:, k, P * r:P * r + P] for f in dft_parts[1 if odd else 0]],
                                [h[:, k, :] for h in (odd_parts if odd else even_parts)], k == 0,
                                not extra and k == ST - 1, bk_a)
                    if extra:
                        for k in range(ST):
                            mm(o, last_row[:, k, :], h_bwd[:, k, :], False, k == ST - 1,
                               bk_a if k == ST - 1 else None)

            taps(0)
            modulation(0)
            for c in range(4):
                half_spectrum(True)
                if c < 3:
                    taps(c + 1)
                half_spectrum(False)
                if c < 3:
                    modulation(6 * c + 6)
            o = begin(bk_d)
            pe.wait_ge(s_abs, 4)
            for c in range(4):
                half, order = c // 2, c % 2
                for n in range(4):
                    col = 8 * order + 4 * half + n
                    mm(o[:, col:col + 1], abs_sum[:, c, P * n:P * n + P], ones[:, 0:1], True, True,
                       bk_d if c == 3 and n == 3 else None)

            modulation_columns(23)

            pe.wait_ge(s_x, 16)
            o = begin(bk_d)
            for k in range(KD):
                for g in range(2):
                    mm(o[32 * g:32 * g + HEADS, :], wgate[:, k, 4 * g:4 * g + 4], x[:, k, :], k == 0, k == KD - 1,
                       bk_d if k == KD - 1 and g == 1 else None)
            note["qk"] = bk_d.filled.n
            project(4, f_high, x_low, bk_d, fresh=KD)
            project_tok(2, f_high, x_low, ST, bk_a)
            project(2, f_high, x_low, bk_a)
            note["u"] = bk_a.filled.n
            project(2, f_high, x_low, bk_a)
            for g in range(4):
                o = begin(bk_a)
                pe.wait_ge(s_pool, g + 1)
                mm(o, poolw[:, g, :], mixed[:, g, :], True, True, bk_a)
            o = begin(bk_a)
            pe.wait_ge(s_row, 1)
            for t in range(ST):
                mm(o[:, HEADS * t:HEADS * t + HEADS], rows[0][:, P * t:P * t + P], ident[0:HEADS, 0:HEADS],
                   True, True, bk_a if t == ST - 1 else None, tr=True)
            pe.wait_ge(s_row, 2)
            pe.wait_ge(s_em, 1)
            for h in range(HEADS):
                pick = ident[0:HEADS, h:h + 1].broadcast_to([HEADS, P])
                o = begin(bk_a)
                mm(o, pick, rows[2], True, True, bk_a)
                pe.wait_ge(s_qk, KD)
                for j in range(ST):
                    o = begin(bk_d)
                    mm(o[:, P * j:S], qk[:, 4 + h, P * j:P * j + P], qk[:, h, P * j:S], True, True, bk_d)
                den = begin(bk_a)
                note["den", h] = bk_a.filled.n
                e_bc = begin(bk_d)
                mm(e_bc, pick, rows[3], True, True, bk_d)
                read(bk_d, 1)
                for j in range(ST):
                    mm(den[:, P * j:S], ones[:], decay[:, j, P * j:S], j == 0, j == ST - 1,
                       bk_a if j == ST - 1 else None)
                num = begin(bk_d)
                for j in range(ST):
                    mm(num[:, P * j:S], v_tok[:, j, P * h:P * h + P], decay[:, j, P * j:S], j == 0,
                       j == ST - 1, bk_d if j == ST - 1 else None)
                read(bk_d)
                o = begin(bk_d)
                mm(o, ones[:], hn[:, 0, :], True, True, bk_d)
                o = begin(bk_d)
                pe.wait_ge(s_hn, h + 1)
                mm(o, ones[:], hn[:, 1, :], True, True, bk_d)
            tiles_split[0] += 4
            project(4, f_high, mixed_low, bk_d, fresh=4)

            def keys_values():
                project(4, mem_high, mem_low, bk_a, MEM, fresh=2)
                project_tok(4, mem_high, mem_low, 2, bk_a)

            layer_norm(region(1), region(2), summed, keys_values)
            project(4, f_high, x1_low, bk_a, fresh=KD)
            read(bk_a)
            note["scores"] = bk_d.filled.n
            for h in range(HEADS):
                for t in range(ST):
                    o = begin(bk_d)
                    for i in range(2):
                        mm(o[:, 0:MEM], q_x[:, 2 * h + i, P * t:P * t + P], k_x[:, 2 * h + i, :],
                           i == 0, i == 1, bk_d if i == 1 else None)
                pe.wait_ge(s_xp, ST * (h + 1))
                for m in range(2):
                    o = begin(bk_a)
                    for t in range(ST):
                        mm(o[:, P * t:P * t + P], p_exp[:, t, P * m:P * m + P], ident[:], True, True,
                           bk_a if t == ST - 1 else None, tr=True)
                owed.append(s_pread)
                read(bk_a)
                note["o_x", h] = bk_a.filled.n
                for i in range(2):
                    o = begin(bk_a)
                    for m in range(2):
                        mm(o, v_x[:, m, P * (2 * h + i):P * (2 * h + i) + P], p_t[:, m, :], m == 0, m == 1,
                           bk_a if m == 1 else None)
            project(4, f_high, o_x_low, bk_d, fresh=KD)
            layer_norm(region(2), region(3), summed)
            def router_logits(m, src, ready):
                o = begin(bk_a)
                for k in range(KD):
                    ready(k)
                    mm(o[0:NE, :], router[:, m, k, :], src[:, k, :], k == 0, k == KD - 1,
                       bk_a if k == KD - 1 else None)
                read(bk_a)

            def logits_to_tokens(m, b):
                o = begin(b)
                for t in range(ST):
                    mm(o[:, NE * t:NE * t + NE], logits_t[m][:, P * t:P * t + P], ident[0:NE, 0:NE], True, True,
                       b if t == ST - 1 else None, tr=True)

            router_logits(0, x, lambda k: pe.wait_ge(s_lno, KD + k + 1))
            logits_to_tokens(0, bk_a)
            note["router"] = bk_a.filled.n
            note["x_tok"] = bk_a.filled.n
            to_tokens(x)
            o = begin(bk_a)
            pe.wait_ge(s_gt, 1)
            for t in range(ST):
                mm(o[0:NGRP, P * t:P * t + P], in_group4[:, 4 * t:4 * t + 4], ident[:], True, True,
                   bk_a if t == ST - 1 else None, tr=True)
            note["group_rows"] = bk_a.filled.n
            o = begin(bk_a)
            pe.wait_ge(s_start, 1)
            mm(o[0:NGRP, 0:1], tri4[:], gcol[:, 0:1], True, True, bk_a)
            note["start"] = bk_a.filled.n
            o = begin(bk_a)
            pe.wait_ge(s_sm, 2)
            for t in range(ST):
                mm(o[:, t:t + 1], g_rows[2][:, P * t:P * t + P], ones[0:NGRP, 0:1], True, True)
            mm(o[0:1, 8:16], ones[0:NGRP, 0:1], gcol[:, 8:16], True, True, bk_a)
            note["places"] = bk_a.filled.n
            pe.wait_ge(s_pl, ST)
            for b in range(BLOCKS):
                o = begin(bk_a)
                for t in range(ST):
                    mm(o[:, P * t:P * t + P], place[:, t, P * b:P * b + P].bitcast(F32), ident[:], True, True,
                       bk_a if t == ST - 1 else None, tr=True)
            o = begin(bk_a)
            pe.wait_ge(s_gates, ST)
            for b in range(BLOCKS):
                for t in range(ST):
                    mm(o[:, EPG * b:EPG * b + EPG], place[:, t, P * b:P * b + P].bitcast(F32), gate_loc[:, t, :], t == 0,
                       t == ST - 1, bk_a if t == ST - 1 and b == BLOCKS - 1 else None)
            read(bk_a)
            bk_t = Banks(psum, [0, 1], s_mt, s_et)
            bk_y = Banks(psum, [2, 3], s_my, s_ey)

            def gather_half(b, n):
                o = begin(bk_t)
                for j in range(4):
                    for t in range(ST):
                        for high in (True, False):
                            tile = (f_high if high else x_tok_low)[:, 2 * t + n, P * j:P * j + P]
                            mm(o[:, P * j:P * j + P], tile, place[:, t, bass.ds(P * b, P)], t == 0 and high,
                               t == ST - 1 and not high, bk_t if j == 3 and t == ST - 1 and not high else None)

            tiles_split[0] += 2 * ST
            pe.wait_ge(s_flo, tiles_split[0])
            for n in range(2):
                gather_half(0, n)
            assert not owed
            note["moe1_a"], note["moe1_d"] = bk_a.filled.n, bk_d.filled.n
            with pe.Fori(0, BLOCKS) as i:
                entry = enter(i, BLOCKS, PER_BLOCK, 0, 12)
                low_parts.enter(i, SPLIT_BLOCK)
                bk_t.filled.enter(i, 6)
                bk_y.filled.enter(i, 2)
                o_y = [bk_y.bank(n) for n in range(2)]
                at = []

                def up(e, between=lambda: None):
                    o = begin(bk_d)
                    for k in range(KD):
                        if k % 4 == 0:
                            w = split_unit()
                        cols = slice(512 * (k % 4), 512 * (k % 4) + 512)
                        product(o, [x_[:, k, :] for x_ in x_blk], [w_[:, cols] for w_ in w], k == 0, k == KD - 1, bk_d)
                        if k % 4 == 3:
                            used()
                            if k == 3:
                                between()

                def turned(e):
                    o = begin(bk_t)
                    pe.wait_ge(s_hid, EPG * i + e + 1)
                    for j in range(2):
                        mm(o[:, P * j:P * j + P], hid[:, e % 2, P * j:P * j + P], ident[:], True, True,
                           bk_t if j == 1 else None, tr=True)
                    return bk_t.filled.at()

                def down(e, turned_at):
                    w = unit()
                    pe.wait_ge(s_et, turned_at)
                    for j in range(2):
                        for n in range(2):
                            last = e == EPG - 1 and j == 1
                            mm(o_y[n], hid_t[:, 2 * (e % 2) + j, :], w[:, D * j + 512 * n:D * j + 512 * n + 512],
                               e == 0 and j == 0, last, bk_y if last else None)
                    used()

                pe.wait_ge(s_et, bk_t.filled.at())
                up(0)
                for e in range(1, EPG):
                    up(e, lambda: at.append(turned(e - 1)))
                    down(e - 1, at[-1])
                at.append(turned(EPG - 1))
                gather_half(i + 1, 0)
                down(EPG - 1, at[-1])
                gather_half(i + 1, 1)
                pe.wait_ge(s_ey, bk_y.filled.at())
                for n in range(KD):
                    o = begin(bk_d)
                    for part in range(2):
                        mm(o, y_blk[part][:, P * n:P * n + P], place_t[:, i, :], part == 0, part == 1,
                           bk_d if part == 1 else None)
                assert not owed
                low_parts.leave(BLOCKS)
                bk_t.filled.leave(BLOCKS)
                bk_y.filled.leave(BLOCKS)
                leave(entry)
            pe.wait_ge(s_et, bk_t.filled.n)
            layer_norm(region(3), region(1), summed)
            layer_norm(x, region(2), lambda k: pe.wait_ge(s_px, k + 1))
            note["u_hy"] = bk_a.filled.n
            project(12, f_high, h2_low, bk_a, fresh=KD)

            for order in range(2):
                pe.wait_ge(s_uc, 3 * KD)
                if order:
                    pe.wait_ge(s_z1, KD)
                note["z_tok", order] = bk_a.filled.n
                to_tokens(u_hy[0])
                tiles_split[0] += 2 * ST
                pe.wait_ge(s_flo, tiles_split[0])
                for half in range(2):
                    tables = [[f.rearrange("p (k n) -> p k n", k=ST) for f in split_unit()] for _ in range(2)]
                    note["k", order, half] = [(turn[0] % RING, 16 * (turn[0] // RING + 1)),
                                              ((turn[0] + 1) % RING, 16 * ((turn[0] + 1) // RING + 1))]
                    for r in range(4):
                        for table in tables:
                            o = begin(bk_d)
                            for k in range(ST):
                                product(o, [f[:, k, P * r:P * r + P] for f in table],
                                        [z[:, 4 * half + k, :] for z in (f_high, z_tok_low)],
                                        k == 0, k == ST - 1, bk_d)
                    used()
                    used()
                    unit()
                    unit()
                    pe.wait_ge(s_k, 4 * (2 * order + half + 1))
                    used()
                    used()
                    inv = [unit().rearrange("p (k n) -> p k n", k=4) for _ in range(2)]
                    for n in range(4):
                        o = begin(bk_d)
                        for r in range(8):
                            mm(o, spec[:, r, P * n:P * n + P], inv[r // 4][:, r % 4, :], r == 0, r == 7,
                               bk_d if r == 7 else None)
                    used()
                    used()
            note["hyout"] = bk_a.filled.n
            project(4, f_high, z_low, bk_a, fresh=KD)
            layer_norm(region(2), region(3), lambda k: pe.wait_ge(s_res, k + 1))
            layer_norm(x, region(3), lambda k: pe.wait_ge(s_lno, 4 * KD + k + 1))
            router_logits(1, h2, lambda k: pe.wait_ge(s_lno, 5 * KD + k + 1))
            logits_to_tokens(1, bk_d)
            to_tokens(h2)
            o = begin(bk_a)
            pe.wait_ge(s_aff, 1)
            for t in range(ST):
                mm(o[0:NE, P * t:P * t + P], aff[:, t, 0:NE], ident[:], True, True,
                   bk_a if t == ST - 1 else None, tr=True)
            note["aff_t"] = bk_a.filled.n
            o = begin(bk_d)
            pe.wait_ge(s_top, 1)
            for t in range(ST):
                mm(o[:, NE * t:NE * t + NE], mask_t[:, P * t:P * t + P], ident[0:NE, 0:NE], True, True,
                   bk_d if t == ST - 1 else None, tr=True)

            def gather():
                for n in range(2):
                    o = begin(bk_a)
                    for t in range(ST):
                        mm(o, onehot[:, t, :], h_tok[:, t, 512 * n:512 * n + 512], t == 0, t == ST - 1,
                           bk_a if t == ST - 1 else None)
                for n in range(2):
                    read(bk_a, 1)
                    o = begin(bk_a)
                    for j in range(4):
                        mm(o[:, P * j:P * j + P], x_sel[:, 0, 512 * n + P * j:512 * n + P * j + P], ident[:],
                           True, True, bk_a if j == 3 else None, tr=True)

            pe.wait_ge(s_oh, 1)
            gather()
            assert not owed
            arrived, turn[0] = s_arrived2, 0
            note["moe2_a"], note["moe2_d"] = bk_a.filled.n, bk_d.filled.n
            with pe.Fori(0, NE // 2) as i:
                entry = enter(i, NE // 2, 48, 12, 16)
                read(bk_a)
                for b in (bk_a, bk_d):
                    if b is bk_d:
                        read(bk_d)
                    o = [b.bank(n) for n in range(4)]
                    for k in range(KD):
                        w = [unit(), unit()]
                        for n in range(4):
                            for e in range(2):
                                mm(o[n][CAP * e:CAP * e + CAP, :], x_sel_t[:, k, CAP * e:CAP * e + CAP],
                                   w[e][:, 512 * n:512 * n + 512], k == 0, k == KD - 1,
                                   b if k == KD - 1 and e == 1 else None)
                        used()
                        used()
                pe.wait_ge(s_oh, i + 2)
                gather()
                for n in range(4):
                    o = begin(bk_d)
                    for j in range(4):
                        f = 4 * n + j
                        mm(o[:, P * j:P * j + P], hid2[:, 0, P * f:P * f + P], ident[:], True, True,
                           bk_d if j == 3 else None, tr=True)
                pe.wait_ge(s_ohg, i + 1)
                for n in range(2):
                    o = begin(bk_a)
                    for j in range(2):
                        mm(o[:, P * j:P * j + P], onehot_g[:, 2 * n + j, :], ident[:], True, True,
                           bk_a if j == 1 else None, tr=True)
                read(bk_d)
                begin(bk_a)
                pe.wait_ge(s_ea, bk_a.filled.at(-2))
                o = [bk_a.bank(n) for n in range(2)]
                for k in range(KD):
                    w = [unit(), unit()]
                    for a in range(2):
                        for n in range(2):
                            for e in range(2):
                                mm(o[n][CAP * e:CAP * e + CAP, :], hid2_t[:, 2 * k + a, CAP * e:CAP * e + CAP],
                                   w[e][:, D * a + 512 * n:D * a + 512 * n + 512], k == 0 and a == 0,
                                   k == KD - 1 and a == 1, bk_a if k == KD - 1 and a == 1 and e == 1 else None)
                    used()
                    used()
                read(bk_a)
                for n in range(KD):
                    o = begin(bk_d)
                    if owed:
                        mm(o[:, 0:1], y_sel[:, 0, P * n:P * n + P], scat[:, 0:1], True, True)
                    mm(o, y_sel[:, 0, P * n:P * n + P], scat, True, True, bk_d)
                assert not owed
                leave(entry)
            layer_norm(region(2), region(3), lambda k: pe.wait_ge(s_res, KD + k + 1))

        @block.scalar
        def _(act):
            bk = Banks(psum, [0, 1, 2, 3], s_ma, s_ea)
            step = Count(s_astep)
            inv_var = [0]
            ln_no = [0]

            def take():
                act.wait_ge(s_ma, bk.filled.at(1))
                o = bk.bank()
                bk.filled.n += 1
                return o

            def empty(o, dst, func=ACT.Identity, **more):
                bk.emptied.inc(act.activation(dst, o, func, **more))

            def let_go(o):
                bk.emptied.inc(act.activation(tiny[0:1, 0, 7:8], o[0:1, 0:1], ACT.Copy))

            high_parts = Count(s_whi)

            def split(units=1):
                for _ in range(units):
                    n = high_parts.n
                    u = SPLIT[n]
                    last = (SPLIT[n - HIGH] if high_parts.i is None or n < HIGH else
                            SPLIT[n - HIGH + SPLIT_BLOCK] - PER_BLOCK)
                    arrivals, last_used = 16 * (u // RING + 1), last + 1
                    if high_parts.i is not None:
                        arrivals = arrivals + high_parts.i * (16 * PER_BLOCK // RING)
                        last_used = last_used + high_parts.i * PER_BLOCK
                    act.wait_ge(s_arrived[u % RING], arrivals)
                    if n >= HIGH:
                        act.wait_ge(s_used, last_used)
                    high_parts.inc(act.activation(w_high[n % HIGH][:], ring[:, u % RING, :], ACT.Copy))

            def high(dst, src, func=ACT.Copy, **more):
                act.activation(dst, src, func, **more).then_inc(s_fhi, 1)

            def layer_norm(cen, sq, gain, shift, dst, parted=False):
                for k in range(KD):
                    act.wait_ge(s_lnc, KD * ln_no[0] + k + 1)
                    act.activation(sq[:, k, :], cen[:, k, :], ACT.Square).then_inc(s_lnq, 1)
                act.activation(tiny[0:1, 0, 6:7], zero[0:1, :], ACT.Sqrt)
                yield
                rstd(ln_stat[:, 1, :], ln_stat[:, 1, :])
                for k in range(KD):
                    act.wait_ge(s_lnm, KD * ln_no[0] + k + 1)
                    act.activation(dst[:, k, :], cen[:, k, :], ACT.Identity, bias=shift(k), scale=gain(k))\
                       .then_inc(s_lno, 1)
                    if parted:
                        high(f_high[:, k, :], cen[:, k, :], ACT.Identity, bias=shift(k), scale=gain(k))
                ln_no[0] += 1

            def rstd(dst, src):
                inv_var[0] += 1
                act.wait_ge(s_rv, inv_var[0])
                act.activation(dst, src, ACT.Sqrt).then_inc(s_rstd, 1)

            def whole(steps):
                for _ in steps:
                    pass

            act.wait_ge(s_const, 9)
            for n in range(3):
                act.wait_ge(s_mlp, n + 1)
                act.activation(mlp[0:HW, 0, :], mlp[0:HW, 1, :], ACT.Sin).then_inc(s_sin, 1)
            act.wait_ge(s_vec, 16 * 11)
            c_at = VAT["c"]
            act.activation(csil[:, :, 0], vec[:, c_at:c_at + KD], ACT.Silu).then_inc(s_csil, 1)
            act.wait_ge(s_cf, 16)
            for a in range(2):
                high(dft_parts[a][0], dft_f[:, a])

            def modulation(first):
                for u in range(first, first + 6):
                    empty(take()[:, 0:COLS], mod_row[:, u % 2, :])
                    if u:
                        empty(take()[:, 0:2], modc[:, 2 * u - 2:2 * u])

            def high_taps(c, odd):
                act.wait_ge(s_eo, 2 * c + (1 if odd else 2))
                high((odd_parts if odd else even_parts)[0], h_odd if odd else h_even)

            modulation(0)
            high_taps(0, True)
            high_taps(0, False)
            for c in range(4):
                if c:
                    act.wait_ge(s_kst, 16 * c)
                for r in range(4, 8):
                    empty(take(), k_out[:, r, :])
                if c < 3:
                    high_taps(c + 1, True)
                for r in range(4):
                    empty(take(), k_out[:, r, :])
                act.wait_ge(s_ea, bk.emptied.at())
                act.dma_start(ins["spectra"][c], k_out).then_inc(s_kst, 16)
                if c < 3:
                    modulation(6 * c + 6)
                    high_taps(c + 1, False)
            empty(take()[:, 0:2], modc[:, 46:48])
            note["mod_end"] = bk.emptied.n
            split()
            split()
            act.wait_ge(s_x, 16)
            for k in range(KD):
                high(f_high[:, k, :], x[:, k, :])
            act.wait_ge(s_gb, 1)
            step.inc(act.activation(rows[2], rows[2], ACT.Exp, scale=-1.0))
            act.wait_ge(s_astep, step.at())
            act.activation(rows[2], rows[2], ACT.Ln, bias=1.0).then_inc(s_gl, 1)
            act.wait_ge(s_row, 3)
            act.activation(rows[3], rows[3], ACT.Exp, scale=-1.0).then_inc(s_em, 1)
            for n in range(KD):
                act.wait_ge(s_ed, note["qk"] + n + 1)
                act.activation(qk[:, n, :], conv[:, n, :], ACT.Silu).then_inc(s_qk, 1)
                if n % 2 == 1:
                    split()
            act.wait_ge(s_kst, 64)
            for u in range(2):
                for t in range(ST):
                    o = take()
                    empty(o[:, 0:COLS], v_tok[:, t, COLS * u:COLS * u + COLS])
                split()
            for h in range(HEADS):
                empty(take(), o_gate[:, h, :], ACT.Sigmoid)
                if h % 2 == 1:
                    split()
            for g in range(4):
                if g:
                    act.wait_ge(s_pool, g)
                empty(take(), u_pad[:, 16:528])
                if g == 1:
                    split()
            for g in range(4):
                o = take()
                high(f_high[:, 4 + g, :], o, ACT.Identity, scale=vcol("pool_scale", g))
                empty(o, mixed[:, 4 + g, :], scale=vcol("pool_scale", g))
            o = take()
            empty(o[:, 0:ST * HEADS], acol[:])
            split()
            act.wait_ge(s_ea, bk.emptied.at())
            for h in range(HEADS):
                o = take()
                if h:
                    act.wait_ge(s_hn, h)
                for j in range(ST):
                    act.activation(decay[:, j, P * j:S], o[:, P * j:S], ACT.Exp, bias=acol[:, j, h:h + 1])\
                       .then_inc(s_exp, 1)
                let_go(o)
                if h:
                    act.wait_ge(s_ho, h)
                    high(f_high[:, h - 1, :], mixed[:, h - 1, :])
                empty(take(), hn[:, 2, :], ACT.Abs)
                rstd(hn[:, 3, :], hn[:, 3, :])
            act.wait_ge(s_ho, HEADS)
            high(f_high[:, HEADS - 1, :], mixed[:, HEADS - 1, :])
            split(2)
            act.wait_ge(s_mem, 16)
            for half in range(2):
                high(mem_high[:, 4 * half:4 * half + 4, :], mem_t[:, 4 * half:4 * half + 4, :])
            split(2)
            ln = layer_norm(region(1), region(2), lambda k: vcol("ln_mix_g", k), lambda k: vcol("ln_mix_b", k), x,
                            parted=True)
            next(ln)
            for n in range(KD):
                o = take()
                empty(o[:, 0:MEM], k_x[:, n, :])
                if n % 2 == 1:
                    split()
            for u in range(4):
                for m in range(2):
                    o = take()
                    empty(o[:, 0:COLS], v_x[:, m, COLS * u:COLS * u + COLS])
                split()
            whole(ln)
            for n in range(KD):
                empty(take(), q_x[:, n, :])
                if n % 2 == 1:
                    split()
            for h in range(HEADS):
                for t in range(ST):
                    act.wait_ge(s_ed, note["scores"] + ST * h + t + 1)
                    act.activation(p_exp[:, t, :], p_exp[:, t, :], ACT.Exp, scale=XDH ** -0.5,
                                   accum_out=tiny[:, t, 1:2]).then_inc(s_xe, 1)
                for m in range(2):
                    empty(take(), p_t[:, m, :])
                for n in range(2):
                    o = take()
                    high(f_high[:, 2 * h + n, :], o)
                    empty(o, o_x[:, 2 * h + n, :])
            split(2)
            whole(layer_norm(region(2), region(3), lambda k: vcol("ln_x_g", k), lambda k: vcol("ln_x_b", k), x))
            empty(take()[0:NE, :], logits_t[0])
            empty(take()[:, 0:ST * NE], route[:, 0, :], ACT.Sigmoid)

            def rows_of_tokens(dst):
                for t in range(ST):
                    for half in range(2):
                        empty(take(), dst[:, t, 512 * half:512 * half + 512])

            for n in range(2 * ST):
                o = take()
                high(f_high[:, n, :], o)
                empty(o, x_tok[:, n, :])
            o = take()
            empty(o[0:NGRP, :], g_rows[0])
            o = take()
            empty(o[0:NGRP, 0:1], gcol[:, 1:2])
            o = take()
            act.activation(slot1[:], o[:, 0:ST], ACT.Identity).then_inc(s_slot, 1)
            empty(o[0:1, 8:16], tiny[0:1, 2, :])
            for b in range(BLOCKS):
                empty(take(), place_t[:, b, :])
            o = take()
            empty(o[:, 0:EPG * BLOCKS], gate_blk[:, 0:BLOCKS, :].rearrange("p b j -> p (b j)"))
            bk_t = Banks(psum, [0, 1], s_mt, s_et)
            bk_y = Banks(psum, [2, 3], s_my, s_ey)

            def take_from(b):
                act.wait_ge(b.filled.sem, b.filled.at(1))
                o = b.bank()
                b.filled.n += 1
                return o

            bank_high = Count(s_bhi)

            def high_from(b, dst, n=S):
                bank_high.inc(act.activation(dst, take_from(b)[:, 0:n], ACT.Copy))

            def gathered_half(n):
                high_from(bk_t, x_blk[0][:, 4 * n:4 * n + 4, :].rearrange("p k n -> p (k n)"))

            split(3)
            act.wait_ge(s_pl, ST)
            for n in range(2):
                gathered_half(n)
            with act.Fori(0, BLOCKS) as i:
                high_parts.enter(i, SPLIT_BLOCK)
                bank_high.enter(i, 4)
                bk_t.filled.enter(i, 6)
                bk_y.filled.enter(i, 2)

                def gate(e):
                    act.wait_ge(s_md, 12 * i + note["moe1_d"] + e + 1)
                    o = psum[:, 4 + (note["moe1_d"] + e) % 4, :]
                    act.activation(silu1[:, e % 2, :], o[:, 0:FE], ACT.Silu).then_inc(s_si1, 1)

                def turned(e):
                    bk_t.emptied.inc(act.activation(hid_t[:, 2 * (e % 2):2 * (e % 2) + 2, :].rearrange("p k n -> p (k n)"),
                                                    take_from(bk_t)[:, 0:2 * P], ACT.Identity))

                split()
                gate(0)
                split()
                turned(0)
                split()
                gate(1)
                split(2)
                turned(1)
                gate(2)
                turned(2)
                split()
                gate(3)
                split()
                turned(3)
                gathered_half(0)
                split()
                act.wait_ge(s_my, bk_y.filled.at(2))
                for n in range(2):
                    high_from(bk_y, y_blk[0][:, 512 * n:512 * n + 512])
                gathered_half(1)
                for c_ in (high_parts, bank_high, bk_t.filled, bk_y.filled):
                    c_.leave(BLOCKS)
            whole(layer_norm(region(3), region(1), lambda k: vcol("ln_moe_g", k), lambda k: vcol("ln_moe_b", k), x))
            whole(layer_norm(region(1), region(2), lambda k: modp[:, 8 + k:9 + k], lambda k: modc[:, k:k + 1], h2,
                             parted=True))
            act.wait_ge(s_hz, 1)
            for n in range(3 * KD):
                o = take()
                if n >= 2:
                    act.wait_ge(s_uc, n - 1)
                empty(o, hpad[:, n % 2, 1:S + 1], bias=vcol("hy_b_in", n))
                if n % 2 == 1 and n < 2 * 9:
                    split()

            for order in range(2):
                split(2)
                for t in range(ST):
                    for half in range(2):
                        o = take()
                        high(f_high[:, 4 * half + t, :], o)
                        empty(o, z_tok[:, 4 * half + t, :])
                split(2)
            for m in range(KD):
                if m == KD // 2:
                    split()
                    split()
                act.wait_ge(s_z1, KD + m + 1)
                high(f_high[:, m, :], u_hy[0][:, m, :])
            for n in range(KD):
                empty(take(), region(2)[:, n, :], bias=modg[:, n:n + 1], scale=modp[:, 16 + n:17 + n])
                if n % 2 == 1 and n < 4:
                    split()
            whole(layer_norm(region(2), region(3), lambda k: vcol("ln_g2", k), lambda k: vcol("ln_b2", k), x))
            whole(layer_norm(region(1), region(3), lambda k: modp[:, 32 + k:33 + k],
                             lambda k: modc[:, 24 + k:25 + k], h2))
            empty(take()[0:NE, :], logits_t[1])
            act.wait_ge(s_r0, 1)
            act.activation(route[:, 0, :], route[:, 0, :], ACT.Exp).then_inc(s_r1, 1)
            rows_of_tokens(h_tok)
            o = take()
            empty(o[0:NE, :], aff_t)

            def gathered():
                for n in range(2):
                    empty(take(), x_sel[:, 0, 512 * n:512 * n + 512])
                for n in range(2):
                    o = take()
                    empty(o.rearrange("p (k n) -> p k n", k=4), x_sel_t[:, 4 * n:4 * n + 4, :])

            gathered()
            with act.Fori(0, NE // 2) as i:
                bk.filled.enter(i, 12)
                bk.emptied.enter(i, 12)
                for n in range(4):
                    empty(take(), silu2[:, 0, 512 * n:512 * n + 512], ACT.Silu)
                gathered()
                for n in range(2):
                    o = take()
                    empty(o[:, 0:256], scat[:, 256 * n:256 * n + 256])
                for n in range(2):
                    empty(take(), y_sel[:, 0, 512 * n:512 * n + 512])
                bk.filled.leave(NE // 2)
                bk.emptied.leave(NE // 2)
            whole(layer_norm(region(2), region(3), lambda k: vcol("ln_g2", 8 + k), lambda k: vcol("ln_b2", 8 + k), x))

        @block.vector
        def _(dve):
            bk = Banks(psum, [4, 5, 6, 7], s_md, s_ed)
            step = Count(s_step)
            inv_var = [0]
            ln_no = [0]

            def take():
                dve.wait_ge(s_md, bk.filled.at(1))
                o = bk.bank()
                bk.filled.n += 1
                return o

            def done(ins_):
                bk.emptied.inc(ins_)

            def let_go(o):
                done(dve.tensor_copy(tiny[0:1, 1, 7:8], o[0:1, 0:1]))

            def after_bank():
                dve.wait_ge(s_ed, bk.emptied.at())

            def do(ins_):
                step.inc(ins_)

            def after():
                dve.wait_ge(s_step, step.at())

            def tt(dst, a, b, op):
                return dve.tensor_tensor(dst, a, b, op)

            def ts(dst, a, s1, op0, s2=None, op1=None):
                if op1 is None:
                    return dve.tensor_scalar(dst, a, s1, None, op0)
                return dve.tensor_scalar(dst, a, s1, s2, op0, op1)

            def stt(dst, a, scal, b, op0, op1):
                return dve.scalar_tensor_tensor(out=dst, in0=a, scalar=scal, in1=b, op0=op0, op1=op1)

            def inverse_var(o, dst, scale, eps):
                done(ts(dst, o, scale, ALU.mult, eps, ALU.add))
                after_bank()
                dve.reciprocal(dst, dst).then_inc(s_rv, 1)
                inv_var[0] += 1
                dve.wait_ge(s_rstd, inv_var[0])

            low_parts = Count(s_wlo)
            tiles_split = [0]
            banks_split = Count(s_bhi)

            def split(units=1):
                for _ in range(units):
                    n = low_parts.n
                    slot_ = SPLIT[n] % RING
                    dve.wait_ge(s_whi, low_parts.at(1))
                    low_parts.inc(tt(w_low[slot_][:], ring[:, slot_, :], w_high[n % HIGH][:].bitcast(F32),
                                     ALU.subtract))

            def low_of_bank(b, dst, high, n=S):
                dve.wait_ge(s_bhi, banks_split.at(1))
                banks_split.n += 1
                o = b.bank()
                b.filled.n += 1
                b.emptied.inc(tt(dst, o[:, 0:n], high.bitcast(F32), ALU.subtract))

            def low(dst, src, high):
                tiles_split[0] += 1
                dve.wait_ge(s_fhi, tiles_split[0])
                tt(dst, src, high.bitcast(F32), ALU.subtract).then_inc(s_flo, 1)

            def layer_norm(src, cen, eps=LN_EPS, between=lambda: None):
                done(dve.tensor_copy(ln_stat[:, 0, :], take()[:, 0:P]))
                o = take()
                for k in range(KD):
                    tt(cen[:, k, :], src[:, k, :], o, ALU.subtract).then_inc(s_lnc, 1)
                let_go(o)
                between()
                inv_var[0] += 1
                done(ts(ln_stat[:, 1, :], take()[:, 0:P], eps, ALU.add))
                after_bank()
                dve.reciprocal(ln_stat[:, 1, :], ln_stat[:, 1, :]).then_inc(s_rv, 1)
                o = take()
                for k in range(KD):
                    tt(cen[:, k, :], cen[:, k, :], o, ALU.mult).then_inc(s_lnm, 1)
                let_go(o)
                ln_no[0] += 1

            dve.wait_ge(s_net, 16 * 4)
            dve.wait_ge(s_const, 9)
            a, r = mlp[0:HW, 1, :], mlp[0:HW, 2, :]
            for n in range(3):
                o = take()
                b_col = fvec[:, 0:1] if n == 0 else fvec[:, n + 1:n + 2]
                done(ts(a, o[0:HW, :], b_col, ALU.add, fvec[:, 1:2], ALU.mult))
                after_bank()
                do(ts(r, a, 1.0 / TWO_PI, ALU.mult, ROUND, ALU.add))
                after()
                do(ts(r, r, ROUND, ALU.subtract))
                after()
                do(stt(a, r, -PI_HI, a, ALU.mult, ALU.add))
                after()
                do(stt(a, r, -PI_LO, a, ALU.mult, ALU.add))
                after()
                ts(a, a, -PI_IN, ALU.max, PI_IN, ALU.min).then_inc(s_mlp, 1)
            dve.wait_ge(s_vec, 16 * 11)
            for n in range(2):
                low(dft_parts[n][1], dft_f[:, n], dft_parts[n][0])
            for c in range(4):
                half = c // 2
                if c == 0:
                    dve.wait_ge(s_win, 2 * 16)
                win = windows[:, half, :].rearrange("p (k n) -> p k n", k=ST)
                for taps in (h_fwd, h_bwd):
                    for t in range(ST):
                        done(tt(taps[:, t, :], take(), win[:, t, :], ALU.mult))
                after_bank()
                do(dve.memset(h_bwd[0:1, 0, :], 0.0))
                after()
                tt(h_odd, h_fwd, h_bwd, ALU.subtract).then_inc(s_eo, 1)
                dve.wait_ge(s_eo, 2 * c + 1)
                low(odd_parts[1], h_odd, odd_parts[0])
                if c:
                    dve.wait_ge(s_ma, spectra_of(c))
                tt(h_even, h_fwd, h_bwd, ALU.add).then_inc(s_eo, 1)
                do(dve.tensor_reduce(abs_sum[:, c, :], h_fwd.rearrange("p k n -> p n k"), AX, ALU.add,
                                     apply_absolute_value=True))
                do(dve.tensor_reduce(abs_tmp, h_bwd.rearrange("p k n -> p n k"), AX, ALU.add,
                                     apply_absolute_value=True))
                after()
                tt(abs_sum[:, c, :], abs_sum[:, c, :], abs_tmp, ALU.add).then_inc(s_abs, 1)
                dve.wait_ge(s_eo, 2 * c + 2)
                low(even_parts[1], h_even, even_parts[0])
            done(dve.reciprocal(filt_rn[:], take()[:, 0:16]))
            split(2)
            for k in range(KD):
                low(x_low[:, k, :], x[:, k, :], f_high[:, k, :])
            o = take()
            do(ts(rows[0], o[0:HEADS, :], gbias[:, 0:1], ALU.add))
            done(ts(rows[1], o[32:32 + HEADS, :], gbias[:, 1:2], ALU.add))
            after_bank()
            stt(rows[2], rows[1], -1.0, rows[1], ALU.mult, ALU.max).then_inc(s_gb, 1)
            dve.wait_ge(s_gl, 1)
            do(stt(rows[1], rows[1], 0.0, rows[2], ALU.min, ALU.subtract))
            after()
            do(dve.tensor_tensor_scan(rows[3], rows[1], rows[1], 0.0, ALU.add, ALU.bypass))
            after()
            tt(rows[0], rows[0], rows[3], ALU.subtract).then_inc(s_row, 1)
            dve.wait_ge(s_row, 1)
            do(dve.tensor_tensor_scan(rows[1], rows[0], rows[0], 0.0, ALU.max, ALU.max))
            after()
            ts(rows[2], rows[1], -1.0, ALU.mult).then_inc(s_row, 1)
            tt(rows[3], rows[3], rows[1], ALU.add).then_inc(s_row, 1)
            for n in range(KD):
                z = take()
                do(ts(conv[:, n, :], z, vcol("conv", 24 + n), ALU.mult))
                for back in range(1, 4):
                    after()
                    ins_ = stt(conv[:, n, back:S], z[:, 0:S - back], vcol("conv", 8 * (3 - back) + n),
                               conv[:, n, back:S], ALU.mult, ALU.add)
                    if back == 3:
                        done(ins_)
                    else:
                        do(ins_)
                if n % 2 == 1:
                    split()
            split(4)
            do(dve.memset(u_pad[:, 0:16], 0.0))
            for g in range(4):
                dve.wait_ge(s_ea, note["u"] + g + 1)
                after()
                cur, lo = u_pad, 0
                for d in range(g + 1):
                    nxt = (pool_a, pool_b)[d % 2]
                    lo += 1 << d
                    do(tt(nxt[:, lo:528], cur[:, lo:528], cur[:, lo - (1 << d):528 - (1 << d)], ALU.add))
                    after()
                    cur = nxt
                do(stt(mixed[:, g, :], cur[:, 16:528], 1.0 / POOLW[g], u_pad[:, 16:528], ALU.mult, ALU.subtract))
                do(tt(route[:, 0, 0:16], cur[:, 16:32], pool16[:, g, :], ALU.mult))
                after()
                tt(mixed[:, g, 0:16], route[:, 0, 0:16], u_pad[:, 16:32], ALU.subtract).then_inc(s_pool, 1)
                if g == 1:
                    split()
            for g in range(4):
                dve.wait_ge(s_ea, note["u"] + 4 + g + 1)
                low(mixed_low[:, 4 + g, :], mixed[:, 4 + g, :], f_high[:, 4 + g, :])
            split()
            for h in range(HEADS):
                for j in range(ST):
                    o = take()
                    dve.wait_ge(s_tri, ST * h + j + 1)
                    done(stt(decay[:, j, P * j:S], o[:, P * j:S], DH ** -0.5, decay[:, j, P * j:S],
                             ALU.mult, ALU.mult))
                if h:
                    low(mixed_low[:, h - 1, :], mixed[:, h - 1, :], f_high[:, h - 1, :])
                dve.wait_ge(s_ea, note["den", h] + 1)
                done(tt(hn[:, 2, :], take(), hn[:, 2, :], ALU.max))
                after_bank()
                do(dve.reciprocal(hn[:, 2, :], hn[:, 2, :]))
                after()
                done(tt(hn[:, 0, :], take(), hn[:, 2, :], ALU.mult))
                after_bank()
                done(stt(hn[:, 0, :], take(), -1.0 / DH, hn[:, 0, :], ALU.mult, ALU.add))
                after_bank()
                tt(hn[:, 1, :], hn[:, 0, :], hn[:, 0, :], ALU.mult).then_inc(s_hn, 1)
                inverse_var(take(), hn[:, 3, :], 1.0 / DH, LN_EPS)
                do(tt(hn[:, 0, :], hn[:, 0, :], hn[:, 3, :], ALU.mult))
                after()
                stt(mixed[:, h, :], hn[:, 0, :], vcol("head_g", h), o_gate[:, h, :], ALU.mult, ALU.mult)\
                    .then_inc(s_ho, 1)
            low(mixed_low[:, HEADS - 1, :], mixed[:, HEADS - 1, :], f_high[:, HEADS - 1, :])
            for n in range(KD):
                if n == 2:
                    split()
                if n == 4:
                    split()
                    for half in range(2):
                        at = slice(4 * half, 4 * half + 4)
                        low(mem_low[:, at, :], mem_t[:, at, :], mem_high[:, at, :])
                if n == 6:
                    split()
                done(stt(region(1)[:, n, :], x[:, n, :], ALPHA, take(), ALU.mult, ALU.add))
            after_bank()
            split()
            layer_norm(region(1), region(1), between=lambda: split(8))
            for k in range(KD):
                dve.wait_ge(s_lno, k + 1)
                low(x1_low[:, k, :], x[:, k, :], f_high[:, k, :])
            split(4)
            def low_o_x(h):
                for n in range(2 * h, 2 * h + 2):
                    dve.wait_ge(s_ea, note["o_x", h] + n % 2 + 1)
                    low(o_x_low[:, n, :], o_x[:, n, :], f_high[:, n, :])

            for h in range(HEADS):
                if h:
                    dve.wait_ge(s_pread, h)
                for t in range(ST):
                    o = take()
                    do(dve.tensor_reduce(tiny[:, t, 0:1], o[:, 0:MEM], AX, ALU.max))
                    after()
                    done(ts(p_exp[:, t, :], o[:, 0:MEM], tiny[:, t, 0:1], ALU.subtract))
                for t in range(ST):
                    dve.wait_ge(s_xe, ST * h + t + 1)
                    do(dve.reciprocal(tiny[:, t, 2:3], tiny[:, t, 1:2]))
                    after()
                    ts(p_exp[:, t, :], p_exp[:, t, :], tiny[:, t, 2:3], ALU.mult).then_inc(s_xp, 1)
                if h:
                    low_o_x(h - 1)
            low_o_x(HEADS - 1)
            for n in range(KD):
                if n in (2, 4):
                    split()
                done(stt(region(2)[:, n, :], x[:, n, :], ALPHA, take(), ALU.mult, ALU.add))
            after_bank()
            layer_norm(region(2), region(2))
            dve.wait_ge(s_ea, note["router"])
            score = route[:, 0, :]
            sel = route[:, 1, :]
            g2 = route[:, 2, :]
            pairs = ptmp[:, 0, 0:96].rearrange("p (g q) -> p g q", q=6)
            cmp_ = ptmp[:, 1, 0:256].rearrange("p (e f) -> p e f", e=NE)
            cmp2 = ptmp[:, 0, 256:512].rearrange("p (e f) -> p e f", e=NE)
            for t in range(ST):
                do(tt(sel[:, NE * t:NE * t + NE], score[:, NE * t:NE * t + NE], rbias[:], ALU.add))
            after()
            sel4 = sel.rearrange("p (g m) -> p g m", m=4)
            q = 0
            for i_ in range(4):
                for j_ in range(i_ + 1, 4):
                    do(tt(pairs[:, :, q], sel4[:, :, i_], sel4[:, :, j_], ALU.add))
                    q += 1
            after()
            do(dve.tensor_reduce(g2[:, 0:16], pairs, AX, ALU.max))
            after()

            def ranks(dst, val, n):
                c1, c2 = cmp_[:, 0:n, 0:n], cmp2[:, 0:n, 0:n]
                of = val.rearrange("p (o f) -> p o f", o=1).broadcast_to([P, n, n])
                to = val.rearrange("p (e o) -> p e o", o=1).broadcast_to([P, n, n])
                do(tt(c1, of, to, ALU.is_equal))
                do(tt(c2, of, to, ALU.is_gt))
                after()
                do(tt(c1, c1, lower[:, 0:n, 0:n], ALU.mult))
                after()
                do(tt(c1, c1, c2, ALU.add))
                after()
                do(dve.tensor_reduce(dst, c1, AX, ALU.add))
                after()

            for t in range(ST):
                ranks(g2[:, 16 + 4 * t:20 + 4 * t], g2[:, 4 * t:4 * t + 4], 4)
            ts(in_group4, in_group4, 0.0, ALU.is_equal).then_inc(s_gt, 1)
            dve.wait_ge(s_gt, 1)
            do(ts(g2[:, 32:48], in_group4, 1.0, ALU.subtract, -NEG, ALU.mult))
            in_group = g2[:, 16:32].rearrange("p (g o) -> p g o", o=1).broadcast_to([P, 16, 4])
            out_group = g2[:, 32:48].rearrange("p (g o) -> p g o", o=1).broadcast_to([P, 16, 4])
            do(tt(sel4, sel4, in_group, ALU.mult))
            after()
            do(tt(sel4, sel4, out_group, ALU.add))
            after()
            rank = route[:, 3, :]

            def expert_ranks(t):
                ranks(rank[:, NE * t:NE * t + NE], sel[:, NE * t:NE * t + NE], NE)

            expert_ranks(0)
            dve.wait_ge(s_ea, note["group_rows"])
            do(dve.tensor_tensor_scan(g_rows[1], g_rows[0], g_rows[0], 0.0, ALU.add, ALU.bypass))
            after()
            do(ts(gcol[:, 2:3], g_rows[1][:, S - 1:S], 1.0 / P, ALU.mult))
            after()
            do(ts(gcol[:, 4:8], iota[0:NGRP, 0:4], gcol[:, 2:3], ALU.is_lt))
            after()
            dve.tensor_reduce(gcol[:, 0:1], gcol[:, 4:8], AX, ALU.add).then_inc(s_start, 1)
            dve.wait_ge(s_start, 1)
            expert_ranks(1)
            dve.wait_ge(s_ea, note["start"])
            do(ts(gcol[:, 2:3], gcol[:, 1:2], float(P), ALU.mult, 1.0, ALU.subtract))
            do(tt(gcol[:, 3:4], gcol[:, 1:2], gcol[:, 0:1], ALU.add))
            after()
            stt(g_rows[2], g_rows[1], gcol[:, 2:3], g_rows[0], ALU.add, ALU.mult).then_inc(s_sm, 1)
            ts(gcol[:, 8:16], iota[0:NGRP, 0:8], gcol[:, 3:4], ALU.is_ge).then_inc(s_sm, 1)
            expert_ranks(2)
            dve.wait_ge(s_ea, note["places"])
            ts(block_group[:], tiny[0:1, 2, :], float(NGRP - 1), ALU.min).then_inc(s_blk, 1)
            dve.wait_ge(s_iota, 1)
            for t in range(ST):
                ts(place[:, t, :], iota_d, slot1[:, t:t + 1], ALU.is_equal).then_inc(s_pl, 1)
            expert_ranks(3)
            do(stt(rank, rank, 2.0, score, ALU.is_lt, ALU.mult))
            after()
            rank3 = rank.rearrange("p (t e) -> p t e", e=NE)
            do(dve.tensor_reduce(route[:, 4, 0:ST], rank3, AX, ALU.add))
            after()
            do(dve.reciprocal(route[:, 4, 8:8 + ST], route[:, 4, 0:ST]))
            after()
            for t in range(ST):
                do(ts(gates[:, t, :], rank3[:, t, :], route[:, 4, 8 + t:9 + t], ALU.mult))
            after()
            for t in range(ST):
                dve.tensor_reduce(gate_loc[:, t, :], gates[:, t, :].rearrange("p (g j) -> p j g", j=EPG), AX,
                                  ALU.add).then_inc(s_gates, 1)
            for n in range(2 * ST):
                dve.wait_ge(s_ea, note["x_tok"] + n + 1)
                low(x_tok_low[:, n, :], x_tok[:, n, :], f_high[:, n, :])
            m_at = VAT["mod_b"]
            dve.wait_ge(s_ea, note["mod_end"])
            do(tt(modc[:], modc[:], vec[:, m_at:m_at + 48], ALU.add))
            after()
            do(ts(modp[:], modc[:], 1.0, ALU.add))
            after()
            b_at = VAT["hy_b_out"]
            do(tt(modg[:], modp[:, 16:24], vec[:, b_at:b_at + KD], ALU.mult))
            dve.wait_ge(s_lno, 2 * KD)
            do(ts(y1, x, ALPHA, ALU.mult))
            after()
            bk_t = Banks(psum, [0, 1], s_mt, s_et)
            bk_y = Banks(psum, [2, 3], s_my, s_ey)

            def gathered_half(n):
                x_high, x_low_ = [x_[:, 4 * n:4 * n + 4, :].rearrange("p k n -> p (k n)") for x_ in x_blk]
                low_of_bank(bk_t, x_low_, x_high)

            split(3)
            for n in range(2):
                gathered_half(n)
            with dve.Fori(0, BLOCKS) as i:
                bk.filled.enter(i, 12)
                bk.emptied.enter(i, 12)
                low_parts.enter(i, SPLIT_BLOCK)
                banks_split.enter(i, 4)
                bk_t.filled.enter(i, 6)
                bk_y.filled.enter(i, 2)

                def hidden(e):
                    o = take()
                    dve.wait_ge(s_si1, EPG * i + e + 1)
                    ins_ = stt(hid[:, e % 2, :], o[:, FE:2 * FE], gate_blk[:, i, e:e + 1], silu1[:, e % 2, :],
                               ALU.mult, ALU.mult)
                    ins_.then_inc(s_hid, 1)
                    dve.wait_ge(s_hid, EPG * i + e + 1)
                    let_go(o)

                split()
                hidden(0)
                split(2)
                hidden(1)
                split(2)
                hidden(2)
                split()
                hidden(3)
                split()
                bk_t.filled.n += EPG
                gathered_half(0)
                split()
                for n in range(2):
                    at = slice(512 * n, 512 * n + 512)
                    low_of_bank(bk_y, y_blk[1][:, at], y_blk[0][:, at])
                gathered_half(1)
                for n in range(KD):
                    done(tt(y1[:, n, :], take(), y1[:, n, :], ALU.add))
                for c_ in (bk.filled, bk.emptied, low_parts, banks_split, bk_t.filled, bk_y.filled):
                    c_.leave(BLOCKS)
            after_bank()
            layer_norm(region(3), region(3))
            dve.wait_ge(s_pos, 16)
            for k in range(KD):
                dve.wait_ge(s_lno, 2 * KD + k + 1)
                tt(x[:, k, :], x[:, k, :], pos[:, k, :], ALU.add).then_inc(s_px, 1)
            dve.wait_ge(s_px, KD)
            dve.memset(hpad, 0.0).then_inc(s_hz, 1)
            layer_norm(x, region(1), MOD_EPS)
            for k in range(KD):
                dve.wait_ge(s_lno, 3 * KD + k + 1)
                low(h2_low[:, k, :], h2[:, k, :], f_high[:, k, :])
            for n in range(3 * KD):
                dst = u_hy[n // KD][:, n % KD, :]
                dve.wait_ge(s_ea, note["u_hy"] + n + 1)
                do(ts(dst, hpad[:, n % 2, 1:S + 1], vcol("hy_conv_w", 24 + n), ALU.mult,
                      vcol("hy_conv_b", n), ALU.add))
                after()
                do(stt(dst, hpad[:, n % 2, 0:S], vcol("hy_conv_w", n), dst, ALU.mult, ALU.add))
                after()
                stt(dst, hpad[:, n % 2, 2:S + 2], vcol("hy_conv_w", 48 + n), dst, ALU.mult, ALU.add)\
                    .then_inc(s_uc, 1)
                if n % 2 == 1 and n < 2 * 9:
                    split()
            dve.wait_ge(s_uc, 3 * KD)
            split(2)
            for order in range(2):
                for n in range(2 * ST):
                    dve.wait_ge(s_ea, note["z_tok", order] + n + 1)
                    tile = 4 * (n % 2) + n // 2
                    low(z_tok_low[:, tile, :], z_tok[:, tile, :], f_high[:, tile, :])
                for half in range(2):
                    ks = []
                    for slot_, value in note["k", order, half]:
                        dve.wait_ge(s_arrived[slot_], value)
                        ks.append(ring[:, slot_, :].rearrange("p (k n) -> p k n", k=4))
                    kc, ksn = ks
                    for r_ in range(4):
                        zc, zs = take(), take()
                        t1, t2 = ptmp[:, 0, :], ptmp[:, 1, :]
                        do(tt(spec[:, r_, :], zc, kc[:, r_, :], ALU.mult))
                        done(tt(spec[:, 4 + r_, :], zc, ksn[:, r_, :], ALU.mult))
                        do(tt(t1, zs, ksn[:, r_, :], ALU.mult))
                        done(tt(t2, zs, kc[:, r_, :], ALU.mult))
                        after()
                        after_bank()
                        if r_ == 0:
                            do(dve.tensor_copy(spec[0:1, 4, :], t1[0:1, :]))
                            after()
                            do(dve.memset(t1[0:1, :], 0.0))
                            do(dve.memset(t2[0:1, :], 0.0))
                            after()
                        do(tt(spec[:, r_, :], spec[:, r_, :], t1, ALU.subtract))
                        tt(spec[:, 4 + r_, :], spec[:, 4 + r_, :], t2, ALU.add).then_inc(s_k, 1)
                        dve.wait_ge(s_k, 4 * (2 * order + half) + r_ + 1)
                    after()
                    for n in range(4):
                        if n == 2:
                            split(2)
                        m = 4 * half + n
                        z = u_hy[0][:, m, :]
                        t1, t2 = ptmp[:, 0, :], ptmp[:, 1, :]
                        do(ts(t1, z, vcol("hy_f_bias", 8 * order + m), ALU.mult))
                        after()
                        done(stt(t2, take(), filt_rn[:, 8 * order + m:8 * order + m + 1], t1, ALU.mult, ALU.add))
                        after_bank()
                        tt(z, t2, u_hy[1 + order][:, m, :], ALU.mult).then_inc(s_z1, 1)
                        dve.wait_ge(s_z1, KD * order + 4 * half + n + 1)
                        if order == 1:
                            low(z_low[:, m, :], z, f_high[:, m, :])
            for n in range(KD):
                dve.wait_ge(s_ea, note["hyout"] + n + 1)
                if n in (2, 4):
                    split()
                stt(region(2)[:, n, :], x[:, n, :], ALPHA, region(2)[:, n, :], ALU.mult, ALU.add)\
                    .then_inc(s_res, 1)
            dve.wait_ge(s_res, KD)
            layer_norm(region(2), region(2))
            dve.wait_ge(s_lno, 5 * KD)
            layer_norm(x, region(1), MOD_EPS)
            logit = route[:, 0, :]
            l3 = logit.rearrange("p (t e) -> p t e", e=NE)
            o = take()[:, 0:ST * NE]
            do(dve.tensor_reduce(route[:, 1, 0:ST], o.rearrange("p (t e) -> p t e", e=NE), AX, ALU.max))
            after()
            for t in range(ST):
                ins_ = ts(l3[:, t, :], o[:, NE * t:NE * t + NE], route[:, 1, t:t + 1], ALU.subtract)
                if t == ST - 1:
                    done(ins_)
                else:
                    do(ins_)
            after_bank()
            after()
            do(dve.memset(tiny[:, 3, 3:4], 0.0))
            after()
            dve.memset(tiny[:, 3, 4:5], 0.0).then_inc(s_r0, 1)
            dve.wait_ge(s_r1, 1)
            do(dve.tensor_reduce(route[:, 2, 0:ST], l3, AX, ALU.add))
            after()
            do(dve.reciprocal(route[:, 2, 8:8 + ST], route[:, 2, 0:ST]))
            after()
            for t in range(ST):
                ins_ = ts(aff[:, t, 0:NE], l3[:, t, :], route[:, 2, 8 + t:9 + t], ALU.mult)
                if t == ST - 1:
                    ins_.then_inc(s_aff, 1)
                else:
                    do(ins_)
            dve.wait_ge(s_lno, 6 * KD)
            do(dve.memset(y2, 0.0))
            dve.wait_ge(s_ea, note["aff_t"])
            do(dve.tensor_copy(work_t, aff_t))
            after()
            for _ in range(CAP // 8):
                do(dve.max(top8[:], work_t))
                after()
                do(dve.match_replace(work_t, top8[:], work_t, -1.0))
                after()
            do(ts(mask_t, work_t, 0.0, ALU.is_lt))
            after()
            do(dve.tensor_tensor_scan(work_t, mask_t, mask_t, 0.0, ALU.add, ALU.bypass))
            after()
            do(tt(work_t, work_t, mask_t, ALU.mult))
            after()
            ts(mask_t, work_t, 1.0, ALU.subtract).then_inc(s_top, 1)
            o = take()
            done(dve.tensor_copy(slot[:, :, 0:NE], o[:, 0:ST * NE].rearrange("p (t e) -> p t e", e=NE)))
            after_bank()

            def one_hot(first, gated):
                for t in range(ST):
                    for e in range(2):
                        place = slot[:, t, bass.ds(first + e, 1)]
                        at = slice(CAP * e, CAP * e + CAP)
                        if gated:
                            ins_ = ts(onehot_g[:, t, at], iota[:], place, ALU.is_equal,
                                      aff[:, t, bass.ds(first + e, 1)], ALU.mult)
                        else:
                            ins_ = ts(onehot[:, t, at], iota[:], place, ALU.is_equal)
                        if t == ST - 1 and e == 1:
                            ins_.then_inc(s_ohg if gated else s_oh, 1)

            one_hot(0, False)
            do(ts(x, x, ALPHA, ALU.mult))
            after()
            with dve.Fori(0, NE // 2) as i:
                bk.filled.enter(i, 16)
                bk.emptied.enter(i, 16)
                dve.wait_ge(s_ma, 12 * i + note["moe2_a"] + 1)
                one_hot(2 * i + 2, False)
                one_hot(2 * i, True)
                for n in range(4):
                    o = take()
                    dve.wait_ge(s_ea, 12 * i + note["moe2_a"] + n + 1)
                    done(tt(hid2[:, 0, 512 * n:512 * n + 512], o, silu2[:, 0, 512 * n:512 * n + 512], ALU.mult))
                for n in range(4):
                    o = take()
                    done(dve.tensor_copy(hid2_t[:, 4 * n:4 * n + 4, :], o.rearrange("p (k n) -> p k n", k=4)))
                for n in range(KD):
                    done(tt(y2[:, n, :], take(), y2[:, n, :], ALU.add))
                bk.filled.leave(NE // 2)
                bk.emptied.leave(NE // 2)
            after_bank()
            for n in range(KD):
                stt(region(2)[:, n, :], y2[:, n, :], modp[:, 40 + n:41 + n], x[:, n, :], ALU.mult, ALU.add)\
                    .then_inc(s_res, 1)
            dve.wait_ge(s_res, 2 * KD)
            layer_norm(region(2), region(2))


def _constants():
    import numpy as np

    t = np.arange(S)
    f = np.arange(S)
    n = 2 * S
    ang = 2.0 * np.pi * ((t[:, None] * f[None, :]) % n) / n
    sign = 1.0 - 2.0 * (t % 2)
    fwd = np.concatenate([np.cos(ang), np.sin(ang)], 1)
    fwd[:, S] = sign
    weight = np.where(f == 0, 1.0, 2.0) / n
    inv = np.concatenate([(np.cos(ang) * weight).T, (np.sin(ang) * 2.0 / n).T], 0)
    inv[S] = sign / n
    dft = [fwd[:, 512 * a:512 * a + 512].reshape(ST, P, 512).transpose(1, 0, 2).reshape(P, UNIT) for a in range(2)]
    dft += [inv[512 * a:512 * a + 512].reshape(4, P, S).transpose(1, 0, 2).reshape(P, UNIT) for a in range(2)]
    last = np.zeros((S, P))
    last[:, 0] = 2.0 * sign
    f32 = np.float32
    t01 = t.astype(f32) / f32(S - 1)
    bands = (EMB - 1) // 2
    freq = np.linspace(1e-4, bands - 1, bands, dtype=f32)
    angle = freq[None, :] * (f32(2.0 * np.pi) * t.astype(f32) / f32(S))[:, None]
    z = np.concatenate([t01[:, None], np.cos(angle), -np.sin(angle)], -1)
    hi, lo = np.log(1e-2) / 0.3, np.log(1e-2) / 1.5
    delta = np.linspace(lo, hi, D, dtype=f32)
    window = np.exp(-t01[:, None] * np.abs(delta)[None, :])
    window = window.reshape(ST, P, 2, 512).transpose(2, 1, 0, 3).reshape(2, P, UNIT)
    quarter = D // 4
    omega = f32(1.0) / (f32(10000.0) ** (np.arange(quarter, dtype=f32) / f32(quarter)))

    def emb(p):
        a = p.astype(f32)[:, None] * omega[None, :]
        return np.concatenate([np.sin(a), np.cos(a)], -1)

    pos = np.concatenate([emb(t // 64), emb(t % 64)], -1)
    pool16 = np.stack([1.0 / np.minimum(np.arange(1, 17), w) for w in POOLW])
    lower = (np.arange(NE)[None, :] < np.arange(NE)[:, None])
    return {
        "dft": np.stack(dft), "last_row": last.reshape(ST, P, P).transpose(1, 0, 2), "zfeat": z.T,
        "window": window, "pos": pos.T.reshape(KD, P, S).transpose(1, 0, 2),
        "tri4": np.triu(np.ones((NGRP, NGRP)), 1),
        "pool16": np.broadcast_to(pool16, (P, 4, 16)), "lower": lower[None],
    }


def _layout(a):
    import numpy as np

    def slabs(w):
        n = w.shape[1] // COLS
        return w.reshape(KD, P, n, COLS).transpose(2, 1, 0, 3).reshape(n, P, UNIT)

    def cols(v):
        v = v.reshape(-1, P)
        return v.T

    w_in = a["w_in"][0]
    m = 4 * 512
    up = np.concatenate([a["w_gate"][0], a["w_up"][0]], 2)
    up = up.reshape(NE, 2, 4, P, 2 * FE).transpose(0, 1, 3, 2, 4).reshape(NE, 2, P, UNIT)
    down = a["w_down"][0].reshape(NE, 2, P, D).transpose(0, 2, 1, 3).reshape(NE, 1, P, UNIT)
    moe1 = np.concatenate([up, down], 1).reshape(NGRP, 3 * EPG, P, UNIT)
    parts = {
        "mod": slabs(a["mod_w_2"][0]), "in": slabs(np.concatenate([w_in[:, :m], w_in[:, m + 8:]], 1)),
        "mix": slabs(a["w_mix_out"][0]), "xkv": slabs(a["w_xkv"][0]), "xq": slabs(a["w_xq"][0]),
        "xo": slabs(a["w_xo"][0]), "hyin": slabs(a["hy_w_in_2"][0]),
        "hyout": slabs(a["hy_w_out_2"][0]),
    }
    vecs = {
        "conv": a["conv_qk"][0], "head_g": a["head_norm_g"][0], "pool_scale": a["pool_scale"][0],
        "ln_mix_g": a["ln_mix_g"][0], "ln_mix_b": a["ln_mix_b"][0], "ln_x_g": a["ln_x_g"][0],
        "ln_x_b": a["ln_x_b"][0], "ln_moe_g": a["ln_moe_g"][0], "ln_moe_b": a["ln_moe_b"][0],
        "mod_b": a["mod_b_2"][0], "ln_g2": a["ln_g_2"][0], "ln_b2": a["ln_b_2"][0], "hy_b_in": a["hy_b_in_2"][0],
        "hy_conv_w": a["hy_conv_w_2"][0], "hy_conv_b": a["hy_conv_b_2"][0], "hy_f_bias": a["hy_f_bias_2"][0],
        "hy_b_out": a["hy_b_out_2"][0], "c": a["c_2"][0],
    }
    router = np.stack([a["router_w"], a["moe_router_2"][0]])
    return {
        "moe1": moe1,
        "stream": np.concatenate([parts[name] for name, _ in STREAM]),
        "vecs": np.concatenate([cols(vecs[name]) for name, _ in VECS], 1),
        "fvecs": np.stack([a["hy_f_b1_2"][0], a["hy_f_freq_2"][0], a["hy_f_b2_2"][0, 0], a["hy_f_b2_2"][0, 1]], 1),
        "fw1": a["hy_f_w1_2"][0], "fw2": a["hy_f_w2_2"][0].transpose(1, 0, 2), "fw3": a["hy_f_w3_2"][0],
        "gbias": np.stack([a["b_i"][0], a["b_f"][0]], 1),
        "wgate": w_in[:, m:m + 8].reshape(KD, P, 8).transpose(1, 0, 2),
        "poolw": a["pool_w"][0].transpose(1, 0, 2),
        "router": router.reshape(2, KD, P, NE).transpose(2, 0, 1, 3), "rbias": a["router_bias"][None],
        "x": a["x"][0].T.reshape(KD, P, S).transpose(1, 0, 2),
        "mem": a["mem"][0].T.reshape(KD, P, MEM).transpose(1, 0, 2),
        "w1": a["moe_w1_2"][0].reshape(NE, KD, P, FF), "w3": a["moe_w3_2"][0].reshape(NE, KD, P, FF),
        "w2": a["moe_w2_2"][0].reshape(NE, KD, 2 * P, D),
    }


def kernel(**inputs):
    import numpy as np
    import concourse.bacc as bacc
    from concourse.bass_utils import run_bass_kernel_spmd

    a = {name: np.asarray(v) for name, v in inputs.items()}
    arrays = {**_layout(a), **_constants()}
    arrays = {f"in_{name}": np.ascontiguousarray(v, np.float32) for name, v in arrays.items()}
    nc = bacc.Bacc("TRN2", target_bir_lowering=False, num_devices=1)
    ins = {name[3:]: nc.dram_tensor(name, v.shape, F32, kind="ExternalInput").ap() for name, v in arrays.items()}
    ins["spectra"] = nc.dram_tensor("in_spectra", (4, P, 8, 512), F32, kind="Internal").ap()
    out = nc.dram_tensor("out", (P, KD, S), F32, kind="ExternalOutput").ap()
    build(nc, ins, out)
    r = run_bass_kernel_spmd(nc, [arrays], core_ids=[0])
    got = r.results[0]["out"]
    return got.transpose(2, 1, 0).reshape(1, S, D)
```
